# Optimizing a Trainium2 kernel written in Bass

```python
import jax, jax.numpy as jnp
from jax import lax
import numpy as np

D_MODEL = 1024
BATCH = 1
SEQ = 512
DEPTH = 2

N_MIXERS = 2
N_A_LAYERS = (DEPTH + 1) // 2
N_B_LAYERS = DEPTH // 2
RMS_EPS = 1e-6
LRU_WIDTH = D_MODEL
LRU_HEADS = 4
LRU_BLOCK = LRU_WIDTH // LRU_HEADS
CONV_WIDTH = 4
LRU_C = 8.0
RWKV_HEAD = 64
RWKV_HEADS = D_MODEL // RWKV_HEAD
DECAY_LORA = 64
AAA_LORA = 64
GATE_LORA = 128
RWKV_GN_EPS = 64e-5
MEM_LEN = 256
MEM_HEADS = 4
MEM_HEAD_DIM = D_MODEL // MEM_HEADS
D_FF = 4 * D_MODEL


def rms_norm(x, g):
    xf = x.astype(jnp.float32)
    y = xf * lax.rsqrt(jnp.mean(xf * xf, axis=-1, keepdims=True) + RMS_EPS)
    return (y * g.astype(jnp.float32)).astype(x.dtype)

def _lru_combine(c1, c2):
    a1, b1 = c1
    a2, b2 = c2
    return a1 * a2, a2 * b1 + b2

def rglru_mixer(x, conv_w, conv_b, w_in, b_in, gate_w, gate_b, lam, w_out, b_out):
    B, S, _ = x.shape
    proj = x @ w_in + b_in
    y_branch, u = jnp.split(proj, 2, axis=-1)
    y_branch = jax.nn.gelu(y_branch, approximate=True)
    u_pad = jnp.pad(u, ((0, 0), (CONV_WIDTH - 1, 0), (0, 0)))
    conv = conv_b + u_pad[:, 0:S] * conv_w[0]
    for tap in range(1, CONV_WIDTH):
        conv = conv + u_pad[:, tap:tap + S] * conv_w[tap]
    ub = conv.reshape(B, S, LRU_HEADS, LRU_BLOCK)
    gates = jax.nn.sigmoid(jnp.einsum('bshi,ghij->gbshj', ub, gate_w) + gate_b[:, None, None])
    r_gate = gates[0].reshape(B, S, LRU_WIDTH).astype(jnp.float32)
    i_gate = gates[1].reshape(B, S, LRU_WIDTH).astype(jnp.float32)
    log_a = -LRU_C * r_gate * jax.nn.softplus(-lam.astype(jnp.float32))
    a = jnp.exp(log_a)
    mult = jnp.sqrt(-jnp.expm1(2.0 * log_a))
    b = mult * i_gate * conv.astype(jnp.float32)
    _, h = lax.associative_scan(_lru_combine, (a, b), axis=1)
    return (h.astype(x.dtype) * y_branch) @ w_out + b_out

def rwkv7_mixer(x, mu, w_rkv, w0, w1, w2, a0, a1, a2, g1, g2, k_k, k_a, r_k, gn_g, gn_b, w_o):
    B, S, D = x.shape
    H, N = RWKV_HEADS, RWKV_HEAD
    x_prev = jnp.pad(x, ((0, 0), (1, 0), (0, 0)))[:, :S]
    xx = x_prev - x
    r = (x + xx * mu[0]) @ w_rkv[0]
    xw = x + xx * mu[1]
    k = (x + xx * mu[2]) @ w_rkv[1]
    v = (x + xx * mu[3]) @ w_rkv[2]
    xa = x + xx * mu[4]
    xg = x + xx * mu[5]
    w_log = -jax.nn.softplus(-(w0 + jnp.tanh(xw @ w1) @ w2).astype(jnp.float32)) - 0.5
    decay = jnp.exp(-jnp.exp(w_log))
    a = jax.nn.sigmoid(a0 + (xa @ a1) @ a2)
    g = jax.nn.sigmoid(xg @ g1) @ g2
    kk = (k * k_k).reshape(B, S, H, N).astype(jnp.float32)
    kk = kk / jnp.maximum(jnp.linalg.norm(kk, axis=-1, keepdims=True), 1e-12)
    k = k * (1.0 + (a - 1.0) * k_a)

    rh = r.reshape(B, S, H, N).astype(jnp.float32)
    kh = k.reshape(B, S, H, N).astype(jnp.float32)
    vh = v.reshape(B, S, H, N).astype(jnp.float32)
    wh = decay.reshape(B, S, H, N)
    ah = a.reshape(B, S, H, N).astype(jnp.float32)
    rem_a = -kk
    rem_b = kk * ah

    def step(state, inp):
        r_t, w_t, k_t, v_t, a_t, b_t = inp
        sa = jnp.einsum('bhij,bhj->bhi', state, a_t)
        state = (state * w_t[:, :, None, :] + sa[..., None] * b_t[:, :, None, :]
                 + v_t[..., None] * k_t[:, :, None, :])
        y_t = jnp.einsum('bhij,bhj->bhi', state, r_t)
        return state, y_t

    seq_inputs = tuple(jnp.moveaxis(t, 1, 0) for t in (rh, wh, kh, vh, rem_a, rem_b))
    state0 = jnp.zeros((B, H, N, N), jnp.float32)
    _, ys = lax.scan(step, state0, seq_inputs)
    y = jnp.moveaxis(ys, 0, 1)
    mean = jnp.mean(y, axis=-1, keepdims=True)
    var = jnp.mean(jnp.square(y - mean), axis=-1, keepdims=True)
    yn = ((y - mean) * lax.rsqrt(var + RWKV_GN_EPS)).reshape(B, S, D)
    yn = yn * gn_g.astype(jnp.float32) + gn_b.astype(jnp.float32)
    bonus = jnp.sum(rh * kh * r_k.astype(jnp.float32), axis=-1, keepdims=True) * vh
    out = (yn + bonus.reshape(B, S, D)).astype(x.dtype)
    return (out * g) @ w_o

def mem_cross_attention(h, mem_n, w_q, w_kv, w_o):
    B, S, D = h.shape
    M = mem_n.shape[1]
    q = (h @ w_q).reshape(B, S, MEM_HEADS, MEM_HEAD_DIM)
    kv = (mem_n @ w_kv).reshape(B, M, 2, MEM_HEADS, MEM_HEAD_DIM)
    k, v = kv[:, :, 0], kv[:, :, 1]
    s = jnp.einsum('bqhd,bkhd->bhqk', q, k).astype(jnp.float32) * (MEM_HEAD_DIM ** -0.5)
    p = jax.nn.softmax(s, axis=-1).astype(h.dtype)
    o = jnp.einsum('bhqk,bkhd->bqhd', p, v).reshape(B, S, D)
    return o @ w_o

def sqrelu_mlp(h, w_up, w_down):
    return jnp.square(jax.nn.relu(h @ w_up)) @ w_down

def first_inputs(seed: int = 0) -> dict:
    key = jax.random.key(seed)
    ks = iter(jax.random.split(key, 48))
    f32 = jnp.float32

    def nrm(shape, scale):
        return jax.random.normal(next(ks), shape, f32) * scale

    def unif(shape, lo, hi):
        return jax.random.uniform(next(ks), shape, f32, lo, hi)

    D, NA, NB = D_MODEL, N_A_LAYERS, N_B_LAYERS
    x = nrm((BATCH, SEQ, D), 1.0)
    mem = nrm((BATCH, MEM_LEN, D), 1.0)
    ln_gains = 1.0 + nrm((DEPTH, 6, D), 0.05)
    mem_norm = 1.0 + nrm((D,), 0.05)
    a_conv_w = nrm((NA, CONV_WIDTH, LRU_WIDTH), CONV_WIDTH ** -0.5)
    a_conv_b = nrm((NA, LRU_WIDTH), 0.01)
    a_w_in = nrm((NA, D, 2 * LRU_WIDTH), D ** -0.5)
    a_b_in = nrm((NA, 2 * LRU_WIDTH), 0.01)
    a_gate_w = nrm((NA, 2, LRU_HEADS, LRU_BLOCK, LRU_BLOCK), LRU_BLOCK ** -0.5)
    a_gate_b = nrm((NA, 2, LRU_HEADS, LRU_BLOCK), 0.01)
    u = unif((NA, LRU_WIDTH), 0.81, 0.998)
    sp = -0.5 * jnp.log(u)
    a_lambda = -jnp.log(jnp.expm1(sp))
    a_w_out = nrm((NA, LRU_WIDTH, D), LRU_WIDTH ** -0.5)
    a_b_out = nrm((NA, D), 0.01)
    b_mu = unif((NB, 6, D), 0.0, 1.0)
    b_w_rkv = nrm((NB, 3, D, D), D ** -0.5)
    b_w0 = unif((NB, D), -6.0, -1.0)
    b_w1 = nrm((NB, D, DECAY_LORA), D ** -0.5)
    b_w2 = nrm((NB, DECAY_LORA, D), 0.1 * DECAY_LORA ** -0.5)
    b_a0 = nrm((NB, D), 0.1)
    b_a1 = nrm((NB, D, AAA_LORA), D ** -0.5)
    b_a2 = nrm((NB, AAA_LORA, D), 0.1 * AAA_LORA ** -0.5)
    b_g1 = nrm((NB, D, GATE_LORA), D ** -0.5)
    b_g2 = nrm((NB, GATE_LORA, D), GATE_LORA ** -0.5)
    b_k_k = 0.85 + nrm((NB, D), 0.05)
    b_k_a = 1.0 + nrm((NB, D), 0.05)
    b_r_k = nrm((NB, RWKV_HEADS, RWKV_HEAD), 0.1)
    b_gn_g = 1.0 + nrm((NB, D), 0.05)
    b_gn_b = nrm((NB, D), 0.01)
    b_w_o = nrm((NB, D, D), D ** -0.5)
    c_w_q = nrm((DEPTH, D, D), D ** -0.5)
    c_w_kv = nrm((DEPTH, D, 2 * D), D ** -0.5)
    c_w_o = nrm((DEPTH, D, D), D ** -0.5)
    m_w_up = nrm((DEPTH, D, D_FF), D ** -0.5)
    m_w_down = nrm((DEPTH, D_FF, D), D_FF ** -0.5)
    return {"x": x, "mem": mem, "ln_gains": ln_gains, "mem_norm": mem_norm,
            "a_conv_w": a_conv_w, "a_conv_b": a_conv_b, "a_w_in": a_w_in, "a_b_in": a_b_in,
            "a_gate_w": a_gate_w, "a_gate_b": a_gate_b, "a_lambda": a_lambda,
            "a_w_out": a_w_out, "a_b_out": a_b_out,
            "b_mu": b_mu, "b_w_rkv": b_w_rkv, "b_w0": b_w0, "b_w1": b_w1, "b_w2": b_w2,
            "b_a0": b_a0, "b_a1": b_a1, "b_a2": b_a2, "b_g1": b_g1, "b_g2": b_g2,
            "b_k_k": b_k_k, "b_k_a": b_k_a, "b_r_k": b_r_k, "b_gn_g": b_gn_g, "b_gn_b": b_gn_b,
            "b_w_o": b_w_o,
            "c_w_q": c_w_q, "c_w_kv": c_w_kv, "c_w_o": c_w_o,
            "m_w_up": m_w_up, "m_w_down": m_w_down}

def first_block(x, mem, ln_gains, mem_norm,
              a_conv_w, a_conv_b, a_w_in, a_b_in, a_gate_w, a_gate_b, a_lambda, a_w_out, a_b_out,
              b_mu, b_w_rkv, b_w0, b_w1, b_w2, b_a0, b_a1, b_a2, b_g1, b_g2,
              b_k_k, b_k_a, b_r_k, b_gn_g, b_gn_b, b_w_o,
              c_w_q, c_w_kv, c_w_o, m_w_up, m_w_down):
    mem_n = rms_norm(mem, mem_norm)
    for i in range(DEPTH):
        g = ln_gains[i]
        j = i // N_MIXERS
        hn = rms_norm(x, g[0])
        if i % N_MIXERS == 0:
            t = rglru_mixer(hn, a_conv_w[j], a_conv_b[j], a_w_in[j], a_b_in[j], a_gate_w[j],
                            a_gate_b[j], a_lambda[j], a_w_out[j], a_b_out[j])
        else:
            t = rwkv7_mixer(hn, b_mu[j], b_w_rkv[j], b_w0[j], b_w1[j], b_w2[j], b_a0[j],
                            b_a1[j], b_a2[j], b_g1[j], b_g2[j], b_k_k[j], b_k_a[j], b_r_k[j],
                            b_gn_g[j], b_gn_b[j], b_w_o[j])
        x = x + rms_norm(t, g[1])
        c = mem_cross_attention(rms_norm(x, g[2]), mem_n, c_w_q[i], c_w_kv[i], c_w_o[i])
        x = x + rms_norm(c, g[3])
        m = sqrelu_mlp(rms_norm(x, g[4]), m_w_up[i], m_w_down[i])
        x = x + rms_norm(m, g[5])
    return x


DEPTH_2 = 1

N_MEM = 256
EPS = 1e-6

HEAD_DIM = 64
DIL_PATTERNS = ((128, 1), (512, 4), (2048, 16))
N_GROUPS = len(DIL_PATTERNS)
ATTN_SLOTS = 4
ATTN_HEADS = N_GROUPS * ATTN_SLOTS
ATTN_WIDTH = ATTN_HEADS * HEAD_DIM
ATTN_OUT = ATTN_SLOTS * HEAD_DIM
ROT_DIM = HEAD_DIM // 4
ROPE_THETA = 500000.0

CONV_WIDTH_2 = 768
CONV_K = 3

MEM_HEAD_DIM_2 = 128
MEM_WIDTH = MEM_HEADS * MEM_HEAD_DIM_2

N_BRANCH = 3
IN_SIZES = (ATTN_WIDTH, ATTN_WIDTH, ATTN_WIDTH, CONV_WIDTH_2, CONV_WIDTH_2, CONV_WIDTH_2,
            MEM_WIDTH, N_BRANCH * D_MODEL)
IN_COLS = sum(IN_SIZES)
IN_SPLITS = tuple(int(c) for c in np.cumsum(IN_SIZES)[:-1])

N_EXPERT_GROUPS = 4
EXPERTS_PER_GROUP = 8
N_EXPERTS = N_EXPERT_GROUPS * EXPERTS_PER_GROUP
TOP_K = 2
EXPERT_FF = 512
MOE_BLOCK = 256


def _rmsnorm(x, g):
    xf = x.astype(jnp.float32)
    y = xf * lax.rsqrt(jnp.mean(xf * xf, axis=-1, keepdims=True) + EPS)
    return (y * g.astype(jnp.float32)).astype(x.dtype)

def _rope_tables(positions):
    inv = ROPE_THETA ** (-jnp.arange(0, ROT_DIM, 2, dtype=jnp.float32) / ROT_DIM)
    ang = positions.astype(jnp.float32)[..., None] * inv
    return jnp.cos(ang)[:, :, None, :], jnp.sin(ang)[:, :, None, :]

def _partial_rope(t, cos, sin):
    tr = t[..., :ROT_DIM].astype(jnp.float32)
    t1, t2 = tr[..., :ROT_DIM // 2], tr[..., ROT_DIM // 2:]
    rot = jnp.concatenate([t1 * cos - t2 * sin, t2 * cos + t1 * sin], axis=-1)
    return jnp.concatenate([rot.astype(t.dtype), t[..., ROT_DIM:]], axis=-1)

def _banded_attention(q, k, v, half):
    b, g, L, h, dh = q.shape
    blk = half
    nb = -(-L // blk)
    lp = nb * blk
    qb = jnp.pad(q, ((0, 0), (0, 0), (0, lp - L), (0, 0), (0, 0))).reshape(b, g, nb, blk, h, dh)
    pad_k = ((0, 0), (0, 0), (blk, lp - L + blk), (0, 0), (0, 0))

    def windows(t):
        tb = jnp.pad(t, pad_k).reshape(b, g, nb + 2, blk, h, dh)
        return jnp.concatenate([tb[:, :, :-2], tb[:, :, 1:-1], tb[:, :, 2:]], axis=3)

    kw, vw = windows(k), windows(v)
    qpos = np.arange(nb)[:, None] * blk + np.arange(blk)[None, :]
    kpos = np.arange(nb)[:, None] * blk - blk + np.arange(3 * blk)[None, :]
    valid = ((np.abs(qpos[:, :, None] - kpos[:, None, :]) <= half)
             & (kpos[:, None, :] >= 0) & (kpos[:, None, :] < L))
    s = jnp.einsum('bgnqhd,bgnkhd->bgnhqk', qb, kw).astype(jnp.float32) * (dh ** -0.5)
    s = jnp.where(jnp.asarray(valid)[:, None], s, jnp.finfo(jnp.float32).min)
    m = jnp.max(s, axis=-1, keepdims=True)
    p = jnp.exp(s - m)
    den = jnp.sum(p, axis=-1)
    o = jnp.einsum('bgnhqk,bgnkhd->bgnqhd', p.astype(v.dtype), vw)
    o = o / jnp.transpose(den, (0, 1, 2, 4, 3))[..., None].astype(o.dtype)
    lse = jnp.transpose(m[..., 0] + jnp.log(den), (0, 1, 2, 4, 3))
    o = o.reshape(b, g, lp, h, dh)[:, :, :L]
    lse = lse.reshape(b, g, lp, h)[:, :, :L]
    return o, lse

def _dilated_attention(q, k, v, window, dilation):
    b, s, h, dh = q.shape
    L = s // dilation
    half = window // (2 * dilation)

    def to_sub(t):
        return jnp.transpose(t.reshape(b, L, dilation, h, dh), (0, 2, 1, 3, 4))

    o, lse = _banded_attention(to_sub(q), to_sub(k), to_sub(v), half)
    o = jnp.transpose(o, (0, 2, 1, 3, 4)).reshape(b, s, h, dh)
    lse = jnp.transpose(lse, (0, 2, 1, 3)).reshape(b, s, h)
    return o, lse

def _hierarchical_moe(h, w_rg, b_rg, w_re, b_re, w_gate, w_up, w_down):
    b, s, d = h.shape
    n = b * s
    hf = h.reshape(n, d)
    hr = hf.astype(jnp.float32)
    pg = jax.nn.softmax(hr @ w_rg.astype(jnp.float32) + b_rg.astype(jnp.float32), axis=-1)
    pg_top, g_idx = lax.top_k(pg, 1)
    el = (hr @ w_re.astype(jnp.float32) + b_re.astype(jnp.float32)).reshape(n, N_EXPERT_GROUPS, EXPERTS_PER_GROUP)
    sel = jnp.einsum('ng,nge->ne', jax.nn.one_hot(g_idx[:, 0], N_EXPERT_GROUPS, dtype=jnp.float32), el)
    pe_top, e_idx = lax.top_k(jax.nn.softmax(sel, axis=-1), TOP_K)
    weights = pg_top * pe_top / jnp.sum(pe_top, axis=-1, keepdims=True)
    ids = g_idx * EXPERTS_PER_GROUP + e_idx

    nk = n * TOP_K
    e = ids.reshape(nk).astype(jnp.int32)
    w = weights.reshape(nk)
    t = jnp.repeat(jnp.arange(n, dtype=jnp.int32), TOP_K)
    order = jnp.argsort(e, stable=True)
    e_s, t_s, w_s = e[order], t[order], w[order]
    counts = jnp.bincount(e, length=N_EXPERTS)
    padded = ((counts + MOE_BLOCK - 1) // MOE_BLOCK) * MOE_BLOCK
    start = jnp.cumsum(counts) - counts
    pend = jnp.cumsum(padded)
    pstart = pend - padded
    dest = pstart[e_s] + (jnp.arange(nk, dtype=jnp.int32) - start[e_s])
    n_rows = (-(-nk // MOE_BLOCK) + N_EXPERTS) * MOE_BLOCK
    n_blk = n_rows // MOE_BLOCK
    row_tok = jnp.zeros((n_rows,), jnp.int32).at[dest].set(t_s)
    row_w = jnp.zeros((n_rows,), jnp.float32).at[dest].set(w_s)
    blk_exp = jnp.minimum(jnp.searchsorted(pend, jnp.arange(n_blk) * MOE_BLOCK, side='right'),
                          N_EXPERTS - 1).astype(jnp.int32)

    def expert_block(args):
        tok, wt, ex = args
        xb = hf[tok]
        a = xb @ w_gate[ex]
        u = xb @ w_up[ex]
        y = (jax.nn.silu(a) * u) @ w_down[ex]
        return y * wt[:, None].astype(y.dtype)

    ys = lax.map(expert_block, (row_tok.reshape(n_blk, MOE_BLOCK),
                                row_w.reshape(n_blk, MOE_BLOCK), blk_exp))
    out = jnp.zeros((n, d), h.dtype).at[row_tok].add(ys.reshape(n_rows, d).astype(h.dtype))
    return out.reshape(b, s, d)

def second_inputs(seed: int = 0) -> dict:
    key = jax.random.key(seed)
    ks = jax.random.split(key, 24)
    f32 = jnp.float32

    def nrm(k, shape, scale):
        return jax.random.normal(k, shape, f32) * scale

    def gain(k, dim):
        return 1.0 + 0.05 * jax.random.normal(k, (DEPTH_2, dim), f32)

    x = jax.random.normal(ks[0], (BATCH, SEQ, D_MODEL), f32)
    mem = jax.random.normal(ks[1], (BATCH, N_MEM, D_MODEL), f32)
    positions = (jnp.arange(SEQ, dtype=jnp.int32)[None, :]
                 + jax.random.randint(ks[2], (BATCH, 1), 0, 4096, dtype=jnp.int32))
    return {
        'x': x,
        'mem': mem,
        'positions': positions,
        'g_mix': gain(ks[3], D_MODEL),
        'g_mem': gain(ks[4], D_MODEL),
        'w_in': nrm(ks[5], (DEPTH_2, D_MODEL, IN_COLS), D_MODEL ** -0.5),
        'g_qn_attn': gain(ks[6], HEAD_DIM),
        'g_kn_attn': gain(ks[7], HEAD_DIM),
        'w_conv': nrm(ks[8], (DEPTH_2, CONV_K, CONV_WIDTH_2), CONV_K ** -0.5),
        'w_mem_kv': nrm(ks[9], (DEPTH_2, D_MODEL, 2 * MEM_WIDTH), D_MODEL ** -0.5),
        'g_qn_mem': gain(ks[10], MEM_HEAD_DIM_2),
        'g_kn_mem': gain(ks[11], MEM_HEAD_DIM_2),
        'w_proj_attn': nrm(ks[12], (DEPTH_2, ATTN_OUT, D_MODEL), ATTN_OUT ** -0.5),
        'w_proj_conv': nrm(ks[13], (DEPTH_2, CONV_WIDTH_2, D_MODEL), CONV_WIDTH_2 ** -0.5),
        'w_proj_mem': nrm(ks[14], (DEPTH_2, MEM_WIDTH, D_MODEL), MEM_WIDTH ** -0.5),
        'w_out': nrm(ks[15], (DEPTH_2, D_MODEL, D_MODEL), D_MODEL ** -0.5),
        'g_ffn': gain(ks[16], D_MODEL),
        'w_router_group': nrm(ks[17], (DEPTH_2, D_MODEL, N_EXPERT_GROUPS), D_MODEL ** -0.5),
        'b_router_group': nrm(ks[18], (DEPTH_2, N_EXPERT_GROUPS), 0.01),
        'w_router_expert': nrm(ks[19], (DEPTH_2, D_MODEL, N_EXPERTS), D_MODEL ** -0.5),
        'b_router_expert': nrm(ks[20], (DEPTH_2, N_EXPERTS), 0.01),
        'w_gate': nrm(ks[21], (DEPTH_2, N_EXPERTS, D_MODEL, EXPERT_FF), D_MODEL ** -0.5),
        'w_up': nrm(ks[22], (DEPTH_2, N_EXPERTS, D_MODEL, EXPERT_FF), D_MODEL ** -0.5),
        'w_down': nrm(ks[23], (DEPTH_2, N_EXPERTS, EXPERT_FF, D_MODEL), EXPERT_FF ** -0.5),
    }

def second_block(x, mem, positions, g_mix, g_mem, w_in, g_qn_attn, g_kn_attn, w_conv,
              w_mem_kv, g_qn_mem, g_kn_mem, w_proj_attn, w_proj_conv, w_proj_mem, w_out,
              g_ffn, w_router_group, b_router_group, w_router_expert, b_router_expert,
              w_gate, w_up, w_down):
    b, s, d = x.shape
    cos, sin = _rope_tables(positions)
    cos, sin = cos.astype(x.dtype), sin.astype(x.dtype)
    for l in range(DEPTH_2):
        h = _rmsnorm(x, g_mix[l])
        proj = h @ w_in[l]
        q_a, k_a, v_a, cx, cb, cc, q_m, gate_logits = jnp.split(proj, IN_SPLITS, axis=-1)

        q_a = _partial_rope(_rmsnorm(q_a.reshape(b, s, ATTN_HEADS, HEAD_DIM), g_qn_attn[l]), cos, sin)
        k_a = _partial_rope(_rmsnorm(k_a.reshape(b, s, ATTN_HEADS, HEAD_DIM), g_kn_attn[l]), cos, sin)
        v_a = v_a.reshape(b, s, ATTN_HEADS, HEAD_DIM)
        q_a = q_a.reshape(b, s, N_GROUPS, ATTN_SLOTS, HEAD_DIM)
        k_a = k_a.reshape(b, s, N_GROUPS, ATTN_SLOTS, HEAD_DIM)
        v_a = v_a.reshape(b, s, N_GROUPS, ATTN_SLOTS, HEAD_DIM)
        outs, lses = [], []
        for gi, (window, dilation) in enumerate(DIL_PATTERNS):
            o_g, lse_g = _dilated_attention(q_a[:, :, gi], k_a[:, :, gi], v_a[:, :, gi], window, dilation)
            outs.append(o_g)
            lses.append(lse_g)
        alpha = jax.nn.softmax(jnp.stack(lses, axis=2), axis=2)
        o_attn = jnp.einsum('bsgh,bsghd->bshd', alpha.astype(x.dtype),
                            jnp.stack(outs, axis=2)).reshape(b, s, ATTN_OUT)

        u = cc * cx
        up = jnp.pad(u, ((0, 0), (1, 1), (0, 0)))
        wc = w_conv[l]
        y_conv = wc[0] * up[:, :-2] + wc[1] * up[:, 1:-1] + wc[2] * up[:, 2:]
        z_conv = cb * y_conv

        mkv = _rmsnorm(mem, g_mem[l]) @ w_mem_kv[l]
        k_m, v_m = jnp.split(mkv, 2, axis=-1)
        k_m = _rmsnorm(k_m.reshape(b, N_MEM, MEM_HEADS, MEM_HEAD_DIM_2), g_kn_mem[l])
        v_m = v_m.reshape(b, N_MEM, MEM_HEADS, MEM_HEAD_DIM_2)
        q_m = _rmsnorm(q_m.reshape(b, s, MEM_HEADS, MEM_HEAD_DIM_2), g_qn_mem[l])
        sm = jnp.einsum('bshd,bmhd->bhsm', q_m, k_m).astype(jnp.float32) * (MEM_HEAD_DIM_2 ** -0.5)
        pm = jax.nn.softmax(sm, axis=-1).astype(v_m.dtype)
        o_mem = jnp.einsum('bhsm,bmhd->bshd', pm, v_m).reshape(b, s, MEM_WIDTH)

        gates = jax.nn.sigmoid(gate_logits).reshape(b, s, N_BRANCH, d)
        merged = (gates[:, :, 0] * (o_attn @ w_proj_attn[l])
                  + gates[:, :, 1] * (z_conv @ w_proj_conv[l])
                  + gates[:, :, 2] * (o_mem @ w_proj_mem[l]))
        x = x + merged @ w_out[l]

        h2 = _rmsnorm(x, g_ffn[l])
        x = x + _hierarchical_moe(h2, w_router_group[l], b_router_group[l], w_router_expert[l],
                                  b_router_expert[l], w_gate[l], w_up[l], w_down[l])
    return x


def setup_inputs(seed=0):
    out = dict(first_inputs(seed))
    for name, value in second_inputs(seed + 1).items():
        if name != "x":
            out[name + "_2"] = value
    return out


def reference(
    x, mem, ln_gains, mem_norm, a_conv_w, a_conv_b, a_w_in, a_b_in, a_gate_w, a_gate_b,
    a_lambda, a_w_out, a_b_out, b_mu, b_w_rkv, b_w0, b_w1, b_w2, b_a0, b_a1, b_a2, b_g1, b_g2,
    b_k_k, b_k_a, b_r_k, b_gn_g, b_gn_b, b_w_o, c_w_q, c_w_kv, c_w_o, m_w_up, m_w_down, mem_2,
    positions_2, g_mix_2, g_mem_2, w_in_2, g_qn_attn_2, g_kn_attn_2, w_conv_2, w_mem_kv_2,
    g_qn_mem_2, g_kn_mem_2, w_proj_attn_2, w_proj_conv_2, w_proj_mem_2, w_out_2, g_ffn_2,
    w_router_group_2, b_router_group_2, w_router_expert_2, b_router_expert_2, w_gate_2, w_up_2,
    w_down_2,
):
    x = first_block(
        x, mem, ln_gains, mem_norm, a_conv_w, a_conv_b, a_w_in, a_b_in, a_gate_w, a_gate_b,
        a_lambda, a_w_out, a_b_out, b_mu, b_w_rkv, b_w0, b_w1, b_w2, b_a0, b_a1, b_a2, b_g1,
        b_g2, b_k_k, b_k_a, b_r_k, b_gn_g, b_gn_b, b_w_o, c_w_q, c_w_kv, c_w_o, m_w_up,
        m_w_down,
    )
    return second_block(
        x, mem_2, positions_2, g_mix_2, g_mem_2, w_in_2, g_qn_attn_2, g_kn_attn_2, w_conv_2,
        w_mem_kv_2, g_qn_mem_2, g_kn_mem_2, w_proj_attn_2, w_proj_conv_2, w_proj_mem_2, w_out_2,
        g_ffn_2, w_router_group_2, b_router_group_2, w_router_expert_2, b_router_expert_2,
        w_gate_2, w_up_2, w_down_2,
    )


_drawn_inputs = setup_inputs


def setup_inputs(seed=0):
    import zlib

    import numpy as np

    out = dict(_drawn_inputs(seed))
    spreads = {}
    factors = {'a_gate_b': 7.372,
     'b_w1': 8.0,
     'b_w2': 8.0,
     'b_gn_b': 8.0,
     'g_mem_2': 8.0,
     'g_qn_attn_2': 8.0,
     'g_kn_attn_2': 8.0,
     'g_qn_mem_2': 8.0,
     'g_kn_mem_2': 8.0,
     'b_router_group_2': 33.897,
     'b_router_expert_2': 42.78,
     'g_ffn_2': 5.077}
    for name, (base, spread) in spreads.items():
        noise = np.random.default_rng([zlib.crc32(name.encode()), seed]).standard_normal(out[name].shape)
        drawn = base * np.exp(spread * noise) if base else spread * noise
        out[name] = __import__('jax').numpy.asarray(drawn.astype(out[name].dtype))
    for name, factor in factors.items():
        out[name] = (out[name] * factor).astype(out[name].dtype)
    return out
```

```python
from contextlib import ExitStack

import numpy as np

import concourse.bass as bass
from concourse import mybir

F32 = mybir.dt.float32
I32 = mybir.dt.int32
U32 = mybir.dt.uint32
ALU = mybir.AluOpType
ACT = mybir.ActivationFunctionType
AX_X = mybir.AxisListType.X

P = 128
D = 1024
T = 512
DT = D // P
TT = T // P
M = 256
MT = M // P
FF = 4096
EPS = 1e-6
RING = 4
SLOT = 2048
NH = 16
HD = 64
CH = 32
GN_EPS = 64e-5
DECAY = float(np.exp(np.float32(-0.5)))
BIG = 1e30
NE = 32
NG = 4
EF = 512
NBLK = NE + (2 * T - NE) // P


def param_columns():
    cols, at = {}, 0
    for name, n in [
        ("ln", 2 * 6 * 8), ("mem_norm", 8), ("conv_w", 32), ("conv_b", 8), ("b_in", 16),
        ("gate_b", 16), ("lam", 8), ("b_out", 8), ("mu", 48), ("w0", 8), ("a0", 8), ("k_k", 8),
        ("k_a", 8), ("r_k", 8), ("gn_g", 8), ("gn_b", 8), ("g_mix", 8), ("g_mem", 8),
        ("g_ffn", 8), ("qn", 1), ("kn", 1), ("qnm", 1), ("knm", 1), ("conv2", 18),
    ]:
        cols[name] = (at, n)
        at += n
    return cols, at


PCOL, NPAR = param_columns()


def const_columns():
    cols, width = {}, {}
    for region, name, n in [
        ("all", "ident", 128), ("all", "ones", 128), ("all", "blk", 128),
        ("B", "reset", 512), ("B", "gmask", 512), ("B", "lmask", 128),
        ("C", "rot", 128), ("C", "inv", 1), ("C", "ropeon", 1), ("C", "ropeoff", 1),
        ("C", "m1", 384), ("C", "m2", 896), ("C", "m3", 512),
        ("D", "tri", 128), ("D", "tie", 32), ("D", "blkid", NBLK), ("D", "etri", 32),
    ]:
        cols[name] = (region, width.get(region, 0), n)
        width[region] = width.get(region, 0) + n
    return cols, width


CCOL, CWIDTH = const_columns()


def constants():
    c = {r: np.zeros((P, w), np.float32) for r, w in CWIDTH.items()}

    def put(name, a):
        region, at, n = CCOL[name]
        c[region][:, at:at + n] = a

    i = np.arange(P)
    put("ident", np.eye(P))
    put("ones", 1.0)
    put("blk", (i[:, None] // HD == i[None] // HD))
    put("reset", (np.arange(T) % CH != 0)[None].repeat(P, 0))
    same = i[:, None] // CH == i[None] // CH
    strict = same & (i[:, None] < i[None])
    incl = same & (i[:, None] <= i[None])
    put("gmask", np.concatenate([strict, incl, strict, incl], 1))
    put("lmask", strict.T)
    rot = np.zeros((P, P))
    for h in (0, HD):
        for d in range(8):
            rot[h + 8 + d, h + d] = -1.0
            rot[h + d, h + 8 + d] = 1.0
    put("rot", rot)
    d = i % HD
    inv = np.float32(500000.0) ** (-np.arange(0, 16, 2, dtype=np.float32) / np.float32(16))
    put("inv", np.where(d < 16, inv[d % 8], 0.0)[:, None])
    put("ropeon", (d < 16)[:, None])
    put("ropeoff", (d >= 16)[:, None])
    put("tri", i[:, None] < i[None])
    delta = np.arange(384)[None] - 128 - i[:, None]
    put("m1", np.where(np.abs(delta) <= 64, 0.0, -BIG))
    delta = np.arange(896)[None] - 384 - i[:, None]
    put("m2", np.where((np.abs(delta) <= 256) & (delta % 4 == 0), 0.0, -BIG))
    delta = np.arange(512)[None] - i[:, None]
    put("m3", np.where(delta % 16 == 0, 0.0, -BIG))
    put("tie", (64.0 - np.arange(32))[None].repeat(P, 0))
    put("blkid", np.arange(NBLK)[None].repeat(P, 0))
    put("etri", np.pad(np.arange(32)[:, None] <= np.arange(32)[None], ((0, 96), (0, 0))))
    return c


class Lin:

    def __init__(self, name, src, cols, k=D, kind="chan", evac="act", w=None, rows=TT,
                 after=None):
        self.name, self.src, self.cols, self.kind, self.evac = name, src, cols, kind, evac
        self.kp = min(k, P)
        self.kt = k // self.kp
        kc = min(self.kt, 8)
        w = w or min(SLOT // kc, cols)
        self.kc, self.w = kc, w
        self.after = after
        self.chunks, self.tiles = [], 0
        for c0 in range(0, cols, w):
            ww = min(w, cols - c0)
            for kg in range(self.kt // kc):
                self.chunks.append((kg, c0, ww))
            self.tiles += -(-ww // P) if kind == "chan" else rows
        self.rows = rows

    def dram(self, kg, c0, w):
        v = self.src.rearrange("(kt p) n -> p kt n", p=self.kp)
        return v[:, kg * self.kc:(kg + 1) * self.kc, c0:c0 + w]


SHARED = {
    "rwkv_prepared_by_vector": ["kk_raw", "kk_ready", "k_ready", "b_ready", "log_decay_ready",
                                "bonus_raw", "bonus_ready", "a_tilde", "tilde_ready",
                                "complements_ready", "y_centred", "y_normed"],
    "rwkv_prepared_by_scalar": ["kk_square", "kk_root", "decays_ready", "chunk_decay_ready",
                                "y_square", "y_root"],
    "rwkv_summed": ["kk_summed", "bonus_summed", "y_summed", "y_square_summed"],
    "rwkv_pair_by_vector": ["strict_ready", "grams_masked", "start_ready", "av_ready",
                            "inverse_ready", "w2_ready"],
    "rwkv_pair_by_scalar": ["rb_kept", "powers_ready", "w1_ready"],
    "rwkv_pair_products": ["grams_done", "low_done", "level_done", "pair_done"],
    "rwkv_chunk_by_vector": ["u_ready", "state_summed", "state_ready", "wkv_added"],
    "rwkv_chunk_products": ["u_part_done", "state_part_done", "wkv_done"],
    "dilated_by_vector": ["masked", "dil_max_ready", "dil_normed", "slot_out_read"],
    "dilated_by_scalar": ["dil_exp_ready", "dil_turned_read"],
    "dilated_products": ["dil_scores_done", "dil_turned", "slot_out"],
    "heads_by_vector": ["head_normed", "residual_free", "angle_ready", "rotated_read", "roped",
                        "conv2_ready", "merged"],
    "heads_by_scalar": ["head_square", "head_root", "half_sine_ready", "sine_ready"],
    "heads_products": ["head_summed", "rotated"],
    "routing_by_vector": ["group_shifted", "margin_ready", "choices_ready",
                          "block_experts_ready", "rows_known", "token_done"],
    "routing_by_scalar": ["group_exp_ready", "margin_exp_ready"],
    "routing_products": ["router_done", "ranks_done"],
    **{f"tokens_moved{j}": [f"scattered{j}", f"gathered{j}"] for j in range(8)},
    **{f"sync_moved{j}": [f"weights_in_slot{j}", f"output_stored{j}"] for j in range(RING)},
}
GROUP = {kind: group for group, kinds in SHARED.items() for kind in kinds}


def program(nc, a, out, phases, known):
    ctx = ExitStack()
    with ctx:
        sems, given, marked = {}, {}, {}

        def sem(name):
            name = GROUP.get(name, name)
            if name not in sems:
                sems[name] = ctx.enter_context(nc.semaphore(name))
                given[name] = 0
            return sems[name]

        def mark(name, key, by=1):
            s = sem(name)
            given[GROUP.get(name, name)] += by
            assert (name, key) not in marked, (name, key)
            marked[name, key] = given[GROUP.get(name, name)]
            return s, by

        def at(name, key):
            if known is None:
                return sem(name), 1
            v = known[name, key]
            return at(*v) if isinstance(v, tuple) else (sem(name), v)

        def sb(name, shape, dt=F32):
            return ctx.enter_context(nc.sbuf_tensor(name, shape, dt))

        X = sb("X", [P, DT, T])
        H = sb("H", [P, DT, T + 4])
        Wr = sb("Wr", [P, RING, SLOT])
        A = sb("A", [P, 7 * 8, T])
        par = sb("par", [P, NPAR])
        con = {"all": sb("con", [P, CWIDTH["all"]])}
        shared = sb("shared_con", [P, max(CWIDTH[r] for r in "BCD")])
        for r in "BCD":
            con[r] = shared
        SC = sb("SC", [P, 6, T])
        SQ = SC[:, 0:2, :]
        TMP = SC[:, 2:4, :]
        RS = SC[:, 4, :]
        LW = SC[:, 5, :]
        LB = sb("LB", [P, 2, T])
        comp = sb("comp", [P, 56])
        Pc = sb("Pc", [P, 8, T // CH])
        small = sb("small", [P, 256])
        eps_sb = sb("eps_sb", [P, 8])
        BK = ctx.enter_context(nc.psum_tensor("product_banks", [P, 4, T], F32))
        banks = [BK[:, i, :] for i in range(4)]
        wts = sb("wts", [P, 8])
        rows_of = sb("rows_of", [P, 8], I32)
        bexp = sb("bexp", [P, NBLK + 1], I32)
        if "D" in phases:
            xs_dram = nc.dram_tensor("expert_rows", (NBLK * P, D), F32, kind="Internal").ap()
            ys_dram = nc.dram_tensor("expert_outputs", (NBLK * P, D), F32, kind="Internal").ap()
        S2 = ctx.enter_context(nc.psum_tensor("score_banks", [P, 2, T], F32))
        B6 = ctx.enter_context(nc.psum_tensor("turn_bank", [P, T], F32))
        B7 = ctx.enter_context(nc.psum_tensor("stat_bank", [P, T], F32))

        flat = Wr.rearrange("p r n -> p (r n)")

        def tile(n, k=None):
            return A[:, n, :] if k is None else A[:, n:n + k, :]

        def pc(name, j=0, n=1):
            first, _ = PCOL[name]
            return par[:, first + j:first + j + n]

        def cc(name, a0=0, n=None):
            r, first, m = CCOL[name]
            return con[r][:, first + a0:first + a0 + (m if n is None else n)]

        EPSC = {EPS: 0, 1e-24: 1, GN_EPS: 2, 1.0: 3, 0.0: 4}

        def eps_col(v):
            return eps_sb[:, EPSC[v]:EPSC[v] + 1]

        def hn(k):
            return H[:, k, 4:]

        ident, ones = cc("ident"), cc("ones")

        plan = []

        def lin(*args, **kw):
            plan.append(Lin(*args, **kw))

        def attention_plan(i, tag):
            lin(tag + "k", a.c_w_kv[i][:, 0:D], D)
            lin(tag + "v", a.c_w_kv[i][:, D:2 * D], D, kind="row", rows=MT, w=256)
            lin(tag + "q", a.c_w_q[i], D)
            lin(tag + "ov", None, D, kind="attn", w=D)
            lin(tag + "o", a.c_w_o[i], D)

        def mlp_plan(i, tag):
            lin(tag + "up", a.m_w_up[i], FF)
            lin(tag + "down", a.m_w_down[i], D, k=FF)

        if "A" in phases:
            lin("w_in", a.a_w_in[0], 2 * D)
            lin("gates", None, 2 * D, kind="gates", w=D)
            lin("w_out", a.a_w_out[0], D)
            attention_plan(0, "a0")
            mlp_plan(0, "m0")

        if "B" in phases:
            lin("r", a.b_w_rkv[0, 0], D)
            lin("w1", a.b_w1[0], 64)
            lin("w2", a.b_w2[0], D, k=64)
            lin("k_", a.b_w_rkv[0, 1], D)
            lin("a1", a.b_a1[0], 64)
            lin("a2", a.b_a2[0], D, k=64)
            lin("v_", a.b_w_rkv[0, 2], D)
            lin("g1", a.b_g1[0], 128)
            lin("g2", a.b_g2[0], D, k=128, evac="dve", after=("wkv_added", (TT - 1, 1)))
            lin("w_o", a.b_w_o[0], D)
            attention_plan(1, "a1_")
            mlp_plan(1, "m1")

        if "C" in phases:
            wi = a.w_in_2[0]
            lin("ck", a.w_mem_kv_2[0][:, 0:512], 512)
            lin("cv", a.w_mem_kv_2[0][:, 512:1024], 512, kind="row", rows=MT, w=256)
            lin("cq", wi[:, 4608:5120], 512)
            lin("cov", None, 512, kind="attn", w=512)
            lin("qa", wi[:, 0:768], 768)
            lin("ka", wi[:, 768:1536], 768)
            lin("va", wi[:, 1536:2304], 768, kind="row", rows=TT, w=256)
            for n, c in (("cx", 2304), ("cc", 3840), ("cb", 3072)):
                lin(n, wi[:, c:c + 768], 768)
            for b, (w, k) in enumerate(((a.w_proj_attn_2, 256), (a.w_proj_conv_2, 768),
                                        (a.w_proj_mem_2, 512))):
                lin(f"gate{b}", wi[:, 5120 + b * D:5120 + (b + 1) * D], D)
                lin(f"proj{b}", w[0], D, k=k, w=256, evac="dve")
            lin("wout2", a.w_out_2[0], D, evac="dve")

        by_name, tile0, chunk0, tiles, nchunk = {}, {}, {}, [], 0
        for L in plan:
            by_name[L.name] = L
            tile0[L.name], chunk0[L.name] = len(tiles), nchunk
            if L.kind == "gates":
                L.chunks, L.tiles = [(g, 0, 256) for g in range(2)], 16
            if L.kind == "attn":
                L.chunks, L.tiles = [], L.cols // P
            tiles += [(L.evac, (L.name, j)) for j in range(L.tiles)]
            nchunk += len(L.chunks)

        def chunk_source(L, c):
            if L.kind == "gates":
                return a.a_gate_w[0, c[0]].rearrange("h (kt p) j -> p (h kt) j", p=P)
            return L.dram(*c)

        def last_use(L, n):
            if L.kind == "gates":
                return L.name, 8 * n + 7
            if L.kind == "row":
                return L.name, (n + 1) * L.rows - 1
            kg, c0, ww = L.chunks[n]
            t = -(-(c0 + ww) // P) - 1
            return (L.name, t) if kg == L.kt // L.kc - 1 else (L.name, t, kg)

        chunk_uses = [last_use(L, n) for L in plan for n in range(len(L.chunks))]

        def load_weights(sp, names=None):
            g = 0
            for L in plan:
                for n, c in enumerate(L.chunks):
                    if g >= RING:
                        sp.wait_ge(*at("products_done", chunk_uses[g - RING]))
                    if L.after:
                        sp.wait_ge(*at(*L.after))
                    src = chunk_source(L, c)
                    kp, kk, ww = src.shape
                    dst = Wr[0:kp, g % RING, 0:kk * ww].rearrange("p (k n) -> p k n", k=kk)
                    sp.dma_start(dst, src).then_inc(*mark(f"weights_in_slot{g % RING}", g, 16))
                    g += 1

        def bank_for(pe, name, j):
            g = tile0[name] + j
            if g >= 4:
                who, key = tiles[g - 4]
                pe.wait_ge(*at("products_read_by_" + who, key))
            return banks[g % 4]

        def psum_of(name, j):
            return banks[(tile0[name] + j) % 4]

        def slot_of(pe, name, n, kk, ww):
            g = chunk0[name] + n
            pe.wait_ge(*at(f"weights_in_slot{g % RING}", g))
            return Wr[0:by_name[name].kp, g % RING, 0:kk * ww].rearrange("p (k n) -> p k n", k=kk)

        def product(pe, name, rhs, ready, width=T):
            L = by_name[name]
            j0, last_kg = 0, L.kt // L.kc - 1
            for n, (kg, c0, ww) in enumerate(L.chunks):
                w = slot_of(pe, name, n, L.kc, ww)
                for j in range(-(-ww // P)):
                    t, m = c0 // P + j, min(P, ww - j * P)
                    bank = bank_for(pe, name, t) if kg == 0 else psum_of(name, t)
                    for k in range(L.kc):
                        kk = kg * L.kc + k
                        for r in ready(kk):
                            pe.wait_ge(*at(*r))
                        mm = pe.matmul(bank[0:m, 0:width], w[:, k, j * P:j * P + m], rhs(kk),
                                       start=(kk == 0), stop=(kk == L.kt - 1))
                    mm.then_inc(
                        *mark("products_done", (name, t) if kg == last_kg else (name, t, kg)))

        def await_product(eng, name, t):
            eng.wait_ge(*at("products_done", (name, t)))
            return psum_of(name, t)

        def product_rows(pe, name, lhs, ready):
            L = by_name[name]
            for n, (kg, c0, ww) in enumerate(L.chunks):
                w = slot_of(pe, name, n, L.kc, ww)
                for m in range(L.rows):
                    bank = bank_for(pe, name, n * L.rows + m)
                    for k in range(L.kc):
                        for r in ready(k):
                            pe.wait_ge(*at(*r))
                        mm = pe.matmul(bank[:, 0:ww], lhs(k, m), w[:, k, :],
                                       start=(k == 0), stop=(k == L.kc - 1))
                    mm.then_inc(*mark("products_done", (name, n * L.rows + m)))

        def chan_ready(names):
            return lambda k: names

        norms = []

        def norm_squares(act, n, src, ready, tiles_=DT, width=T, dim=D, eps=EPS):
            for t in range(tiles_):
                for r in ready(t):
                    act.wait_ge(*at(*r))
                if t >= 2:
                    act.wait_ge(*at("squares_summed", (n, t - 2)))
                elif norms_before(n):
                    act.wait_ge(*at("squares_summed", norms_before(n)))
                nc.scalar.activation(SQ[:, t % 2, 0:width], src(t), ACT.Square).then_inc(
                    *mark("squares_ready", (n, t)))
            norm_root(act, n, tiles_, width, dim, eps)

        order = []

        def norms_before(n):
            i = [x[0] for x in order].index(n)
            return order[i - 1] if i else None

        def norm_sum(pe, n, tiles_=DT, width=T):
            i = [x[0] for x in order].index(n)
            if i:
                pe.wait_ge(*at("root_ready", order[i - 1][0]))
            for t in range(tiles_):
                pe.wait_ge(*at("squares_ready", (n, t)))
                pe.matmul(B7[:, 0:width], ones, SQ[:, t % 2, 0:width], start=(t == 0),
                          stop=(t == tiles_ - 1)).then_inc(*mark("squares_summed", (n, t)))

        def norm_root(act, n, tiles_=DT, width=T, dim=D, eps=EPS):
            act.wait_ge(*at("squares_summed", (n, tiles_ - 1)))
            if norms_before(n):
                act.wait_ge(*at("norm_applied", norms_before(n)[0]))
            nc.scalar.activation(RS[:, 0:width], B7[:, 0:width], ACT.Sqrt, scale=1.0 / dim,
                                 bias=eps_col(eps)).then_inc(*mark("root_ready", n))

        def norm_rstd(dve, n, width=T):
            dve.wait_ge(*at("root_ready", n))
            nc.vector.reciprocal(RS[:, 0:width], RS[:, 0:width]).then_inc(*mark("rstd_ready", n))
            dve.wait_ge(*at("rstd_ready", n))

        def norm_apply(dve, n, src, dst, gain, tiles_=DT, width=T):
            norm_rstd(dve, n, width)
            for t in range(tiles_):
                nc.vector.scalar_tensor_tensor(out=dst(t), in0=src(t), scalar=gain(t),
                                               in1=RS[:, 0:width], op0=ALU.mult, op1=ALU.mult).then_inc(
                    *mark("normed_ready", (n, t)))
            marked["norm_applied", n] = ("normed_ready", (n, tiles_ - 1))

        def norm_add(dve, n, src, gain):
            norm_rstd(dve, n)
            for t in range(DT):
                nc.vector.scalar_tensor_tensor(out=TMP[:, t % 2, :], in0=src(t), scalar=gain(t),
                                               in1=RS[:, :], op0=ALU.mult, op1=ALU.mult).then_inc(
                    *mark("branch_normed", (n, t)))
                dve.wait_ge(*at("branch_normed", (n, t)))
                nc.vector.tensor_tensor(X[:, t, :], X[:, t, :], TMP[:, t % 2, :], ALU.add).then_inc(
                    *mark("residual_ready", (n, t)))
            marked["norm_applied", n] = ("branch_normed", (n, DT - 1))

        def gain(i, j):
            return lambda t: pc("ln", (i * 6 + j) * 8 + t)

        def xt(t):
            return X[:, t, :]

        def arena(first):
            return lambda t: A[:, first + t, :]

        chain = [0]

        def link(dve, ins):
            chain[0] += 1
            ins.then_inc(sem("vector_step"), 1)
            dve.wait_ge(sem("vector_step"), chain[0])

        achain = [0]

        def alink(act, ins):
            achain[0] += 1
            ins.then_inc(sem("scalar_step"), 1)
            act.wait_ge(sem("scalar_step"), achain[0])

        def x_ready(n):
            return (lambda t: [("loaded_x", 0)]) if n is None else \
                (lambda t: [("residual_ready", (n, t))])

        def norm_order(names):
            for n in names:
                order.append(n)

        def lru_act(act):
            norm_squares(act, "l0n", xt, x_ready(None))
            for j in range(16):
                ps = await_product(act, "w_in", j)
                if j < 8:
                    ins = nc.scalar.activation(tile(j), ps[:, :], ACT.Gelu_apprx_tanh,
                                               bias=pc("b_in", j))
                else:
                    ins = nc.scalar.activation(tile(j), ps[:, :], ACT.Identity,
                                               bias=pc("b_in", j))
                ins.then_inc(*mark("products_read_by_act", ("w_in", j)))
            for j in range(16):
                ps = await_product(act, "gates", j)
                nc.scalar.activation(tile(24 + j), ps[:, :], ACT.Sigmoid,
                                     bias=pc("gate_b", j)).then_inc(
                    *mark("products_read_by_act", ("gates", j)))
            alink(act, nc.scalar.activation(small[:, 0:8], pc("lam", 0, 8), ACT.Exp, scale=-1.0))
            alink(act, nc.scalar.activation(small[:, 8:16], small[:, 0:8], ACT.Ln,
                                             bias=eps_col(1.0)))
            alink(act, nc.scalar.activation(small[:, 16:24], small[:, 8:16], ACT.Copy, scale=-8.0))
            for j in range(8):
                alink(act, nc.scalar.activation(tile(40 + j), tile(24 + j), ACT.Tanh,
                                                scale=small[:, 16 + j:17 + j]))
                nc.scalar.activation(tile(24 + j), tile(24 + j), ACT.Exp,
                                     scale=small[:, 16 + j:17 + j]).then_inc(
                    *mark("decay_ready", j))
            for j in range(8):
                act.wait_ge(*at("gain_squared_ready", j))
                nc.scalar.activation(tile(40 + j), tile(40 + j), ACT.Sqrt).then_inc(
                    *mark("gain_ready", j))
            for j in range(8):
                ps = await_product(act, "w_out", j)
                nc.scalar.activation(tile(24 + j), ps[:, :], ACT.Identity,
                                     bias=pc("b_out", j)).then_inc(
                    *mark("products_read_by_act", ("w_out", j)))
            norm_squares(act, "l0o", arena(24), lambda t: [("products_read_by_act", ("w_out", t))])

        def gates_pe(pe):
            for g in range(2):
                w = slot_of(pe, "gates", g, 8, 256)
                for h in range(4):
                    for j in range(2):
                        t = g * 8 + h * 2 + j
                        bank = bank_for(pe, "gates", t)
                        for k in range(2):
                            pe.wait_ge(*at("conv_ready", 2 * h + k))
                            mm = pe.matmul(bank[:, :], w[:, 2 * h + k, j * P:(j + 1) * P],
                                           tile(16 + 2 * h + k), start=(k == 0), stop=(k == 1))
                        mm.then_inc(*mark("products_done", ("gates", t)))

        def lru_pe(pe):
            norm_sum(pe, "l0n")
            product(pe, "w_in", hn, lambda k: [("normed_ready", ("l0n", k))])
            gates_pe(pe)
            product(pe, "w_out", arena(40), lambda k: [("gated_ready", k)])
            norm_sum(pe, "l0o")

        def lru_dve(dve):
            norm_apply(dve, "l0n", xt, hn, gain(0, 0))
            for j in range(8):
                dve.wait_ge(*at("products_read_by_act", ("w_in", 8 + j)))
                u, c = tile(8 + j), tile(16 + j)
                link(dve, nc.vector.tensor_scalar(c, u, pc("conv_w", 24 + j), pc("conv_b", j),
                                                  ALU.mult, ALU.add))
                for s in (1, 2, 3):
                    ins = nc.vector.scalar_tensor_tensor(
                        out=c[:, s:T], in0=u[:, 0:T - s], scalar=pc("conv_w", (3 - s) * 8 + j),
                        in1=c[:, s:T], op0=ALU.mult, op1=ALU.add)
                    if s < 3:
                        link(dve, ins)
                    else:
                        ins.then_inc(*mark("conv_ready", j))
            for j in range(8):
                dve.wait_ge(*at("decay_ready", j))
                dve.wait_ge(*at("conv_ready", j))
                th, rec = tile(40 + j), TMP[:, j % 2, :]
                link(dve, nc.vector.tensor_scalar(rec, th, -1.0, 1.0, ALU.mult, ALU.add))
                link(dve, nc.vector.reciprocal(rec, rec))
                nc.vector.scalar_tensor_tensor(out=th, in0=th, scalar=-2.0, in1=rec,
                                               op0=ALU.mult, op1=ALU.mult).then_inc(
                    *mark("gain_squared_ready", j))
            for j in range(8):
                th = tile(40 + j)
                dve.wait_ge(*at("gain_ready", j))
                link(dve, nc.vector.tensor_tensor(th, th, tile(32 + j), ALU.mult))
                link(dve, nc.vector.tensor_tensor(th, th, tile(16 + j), ALU.mult))
                link(dve, nc.vector.tensor_tensor_scan(tile(8 + j), tile(24 + j), th, 0.0,
                                                       ALU.mult, ALU.add))
                nc.vector.tensor_tensor(tile(40 + j), tile(8 + j), tile(j), ALU.mult).then_inc(
                    *mark("gated_ready", j))
            norm_add(dve, "l0o", arena(24), gain(0, 1))

        half = A.rearrange("p n (h t) -> p (n h) t", h=2)

        def mem_tile(k):
            return half[:, 8 + k, :]

        def attend_act(act, i, tag, prev, scale, heads, dt, g_in, g_out, own_mem):
            norm_squares(act, tag + "m", lambda t: half[:, t, :], lambda t: [("loaded_" + tag, 0)],
                         width=M)
            norm_squares(act, tag + "n", xt, x_ready(prev))
            for j in range(8):
                ps = await_product(act, tag + "k", j)
                nc.scalar.activation(half[:, 16 + j, :], ps[:, 0:M], ACT.Copy).then_inc(
                    *mark("products_read_by_act", (tag + "k", j)))
            for j in range(8):
                ps = await_product(act, tag + "v", j)
                nc.scalar.activation(vmem(j % 2, (j // 2) * 256, 256), ps[:, 0:256], ACT.Copy).then_inc(
                    *mark("products_read_by_act", (tag + "v", j)))
            for j in range(8):
                ps = await_product(act, tag + "q", j)
                nc.scalar.activation(tile(16 + j), ps[:, :], ACT.Copy).then_inc(
                    *mark("products_read_by_act", (tag + "q", j)))
            for h in range(heads):
                softmax_act(act, tag, h, scale)
                if h:
                    turned_act(act, tag, h - 1, dt)
            turned_act(act, tag, heads - 1, dt)
            for j in range(8):
                ps = await_product(act, tag + "o", j)
                nc.scalar.activation(tile(40 + j), ps[:, :], ACT.Copy).then_inc(
                    *mark("products_read_by_act", (tag + "o", j)))
            norm_squares(act, tag + "x", arena(40),
                         lambda t: [("products_read_by_act", (tag + "o", t))])

        V0 = 12

        def vmem(m, c0, n):
            v = A[:, V0:V0 + 4, :].rearrange("p (m a) t -> p m (a t)", m=2)
            return v[:, m, c0:c0 + n]

        def probs(h):
            return A[:, 32 + 2 * (h % 2):34 + 2 * (h % 2), :].rearrange("p a (b m) -> p (a b) m", b=2)

        def turned(h, m):
            return A[:, 36 + 2 * (h % 2) + m, :]

        scores = S2.rearrange("p a (b m) -> p (a b) m", b=2)

        def softmax_act(act, tag, h, scale):
            act.wait_ge(*at("row_max_ready", (tag, h)))
            if h >= 2:
                act.wait_ge(*at("probs_turned", (tag, h - 2, 1)))
            for q in range(TT):
                nc.scalar.activation(probs(h)[:, q, :], scores[:, q, :], ACT.Exp,
                                     bias=small[:, 32 + 4 * (h % 2) + q:33 + 4 * (h % 2) + q],
                                     scale=scale,
                                     accum_out=small[:, 40 + 4 * (h % 2) + q:41 + 4 * (h % 2) + q]).then_inc(
                    *mark("probs_ready", (tag, h, q)))

        def turned_act(act, tag, h, dt):
            for m in range(MT):
                act.wait_ge(*at("probs_turned", (tag, h, m)))
                if h >= 2 and m == 0:
                    act.wait_ge(*at("products_done", (tag + "ov", (h - 1) * dt - 1)))
                nc.scalar.activation(turned(h, m), (B6 if m == 0 else B7)[:, :], ACT.Copy).then_inc(
                    *mark("turned_ready", (tag, h, m)))
            for d in range(dt):
                j = h * dt + d
                act.wait_ge(*at("products_done", (tag + "ov", j)))
                nc.scalar.activation(tile(24 + j), psum_of(tag + "ov", j)[:, :], ACT.Copy).then_inc(
                    *mark("products_read_by_act", (tag + "ov", j)))

        def attend_pe(pe, tag, heads, dt):
            norm_sum(pe, tag + "m", width=M)
            norm_sum(pe, tag + "n")
            product(pe, tag + "k", mem_tile, lambda k: [("normed_ready", (tag + "m", k))], width=M)
            product_rows(pe, tag + "v", lambda k, m: mem_tile(k)[:, m * P:(m + 1) * P],
                         lambda k: [])
            product(pe, tag + "q", hn, lambda k: [("normed_ready", (tag + "n", k))])
            for h in range(heads + 1):
                if h < heads:
                    scores_pe(pe, tag, h, dt)
                if h:
                    mix_pe(pe, tag, h - 1, dt)
            product(pe, tag + "o", arena(24), lambda k: [("products_read_by_act", (tag + "ov", k))])
            norm_sum(pe, tag + "x")

        def scores_pe(pe, tag, h, dt):
            if h:
                pe.wait_ge(*at("probs_ready", (tag, h - 1, TT - 1)))
            own = tag == "c"
            pe.wait_ge(
                *at(*(("head_normed", 3) if own else ("products_read_by_act", (tag + "k", 7)))))
            for q in range(TT):
                for d in range(dt):
                    pe.wait_ge(
                        *at(*(("head_normed", 4 + h) if own else ("products_read_by_act", (tag + "q", h * dt + d)))))
                    mm = pe.matmul(scores[:, q, :], tile(16 + h * dt + d)[:, q * P:(q + 1) * P],
                                   half[:, 16 + h * dt + d, :], start=(d == 0), stop=(d == dt - 1))
            mm.then_inc(*mark("scores_ready", (tag, h)))

        def mix_pe(pe, tag, h, dt):
            pe.wait_ge(*at("probs_normed", (tag, h)))
            pe.wait_ge(*at("products_read_by_act", (tag + "v", by_name[tag + "v"].tiles - 1)))
            for m in range(MT):
                if h:
                    pe.wait_ge(*at("turned_ready", (tag, h - 1, m)))
                for q in range(TT):
                    mm = pe.transpose((B6 if m == 0 else B7)[:, q * P:(q + 1) * P],
                                      probs(h)[:, q, m * P:(m + 1) * P], ident)
                mm.then_inc(*mark("probs_turned", (tag, h, m)))
            for d in range(dt):
                j = h * dt + d
                bank = bank_for(pe, tag + "ov", j)
                for m in range(MT):
                    pe.wait_ge(*at("turned_ready", (tag, h, m)))
                    mm = pe.matmul(bank[:, :], vmem(m, j * P, P), turned(h, m),
                                   start=(m == 0), stop=(m == MT - 1))
                mm.then_inc(*mark("products_done", (tag + "ov", j)))

        def softmax_dve(dve, tag, h, scale):
            m0, d0 = 32 + 4 * (h % 2), 40 + 4 * (h % 2)
            dve.wait_ge(*at("scores_ready", (tag, h)))
            link(dve, nc.vector.tensor_reduce(small[:, m0:m0 + 4], scores, AX_X, ALU.max))
            nc.vector.tensor_scalar(small[:, m0:m0 + 4], small[:, m0:m0 + 4], -scale, None,
                                    ALU.mult).then_inc(*mark("row_max_ready", (tag, h)))
            dve.wait_ge(*at("probs_ready", (tag, h, TT - 1)))
            link(dve, nc.vector.reciprocal(small[:, d0:d0 + 4], small[:, d0:d0 + 4]))
            for q in range(TT):
                ins = nc.vector.tensor_scalar(probs(h)[:, q, :], probs(h)[:, q, :],
                                              small[:, d0 + q:d0 + q + 1], None, ALU.mult)
            ins.then_inc(*mark("probs_normed", (tag, h)))

        def attend_dve(dve, i, tag):
            norm_apply(dve, tag + "m", lambda t: half[:, t, :], mem_tile, lambda t: pc("mem_norm", t),
                       width=M)
            norm_apply(dve, tag + "n", xt, hn, gain(i, 2))
            for h in range(4):
                softmax_dve(dve, tag, h, 1.0 / 16)
            norm_add(dve, tag + "x", arena(40), gain(i, 3))

        ROPE_C1, ROPE_C2 = 6.28125, 0.0019350051879882812
        ROPE_C3 = 2 * np.pi - ROPE_C1 - ROPE_C2
        MAGIC = 12582912.0
        HNORM = [(half[:, 16 + j, :], M, "ones", P, pc("knm")) for j in range(4)] + \
                [(tile(16 + j), T, "ones", P, pc("qnm")) for j in range(4)] + \
                [(tile(j), T, "blk", HD, pc("qn")) for j in range(6)] + \
                [(tile(6 + j), T, "blk", HD, pc("kn")) for j in range(6)]
        HREADY = [("ck", j) for j in range(4)] + [("cq", j) for j in range(4)] + \
                 [("qa", j) for j in range(6)] + [("ka", j) for j in range(6)]

        def hnorm_act(act, lo, hi):
            def square(i):
                src, w = HNORM[i][0], HNORM[i][1]
                act.wait_ge(*at("products_read_by_act", HREADY[i]))
                if i >= lo + 2:
                    act.wait_ge(*at("head_summed", i - 2))
                elif lo == 0:
                    act.wait_ge(*at("squares_summed", ("cn", 7)))
                nc.scalar.activation(SQ[:, i % 2, 0:w], src, ACT.Square).then_inc(
                    *mark("head_square", i))
            square(lo)
            for i in range(lo, hi):
                if i + 1 < hi:
                    square(i + 1)
                act.wait_ge(*at("head_summed", i))
                w = HNORM[i][1]
                if i >= lo + 2:
                    act.wait_ge(*at("head_normed", i - 2))
                elif lo == 0:
                    act.wait_ge(*at("residual_free", 0))
                nc.scalar.activation(TMP[:, i % 2, 0:w], (B6, B7)[i % 2][:, 0:w], ACT.Sqrt,
                                     scale=1.0 / HNORM[i][3], bias=eps_col(EPS)).then_inc(
                    *mark("head_root", i))

        def hnorm_pe(pe, lo, hi):
            for i in range(lo, hi):
                pe.wait_ge(*at("head_square", i))
                if i >= lo + 2:
                    pe.wait_ge(*at("head_root", i - 2))
                elif lo == 0:
                    pe.wait_ge(*at("root_ready", "cn"))
                else:
                    pe.wait_ge(*at("turned_ready", ("c", 3, MT - 1)))
                w = HNORM[i][1]
                pe.matmul((B6, B7)[i % 2][:, 0:w], cc(HNORM[i][2]), SQ[:, i % 2, 0:w],
                          start=True, stop=True).then_inc(*mark("head_summed", i))

        def hnorm_dve(dve, lo, hi):
            for i in range(lo, hi):
                src, w, _, _, g = HNORM[i]
                dve.wait_ge(*at("head_root", i))
                s = TMP[:, i % 2, 0:w]
                link(dve, nc.vector.reciprocal(s, s))
                nc.vector.scalar_tensor_tensor(out=src, in0=src, scalar=g, in1=s, op0=ALU.mult,
                                               op1=ALU.mult).then_inc(*mark("head_normed", i))

        def angles_dve(dve):
            dve.wait_ge(*at("loaded_conC", 0))
            dve.wait_ge(*at("loaded_positions", 0))
            dve.wait_ge(*at("head_normed", 7))
            ang, k = TMP[:, 0, :], TMP[:, 1, :]
            link(dve, nc.vector.tensor_copy(ang, tile(20).bitcast(I32)))
            link(dve, nc.vector.tensor_scalar(ang, ang, cc("inv"), None, ALU.mult))
            link(dve, nc.vector.tensor_scalar(k, ang, 1.0 / (2 * np.pi), MAGIC, ALU.mult, ALU.add))
            link(dve, nc.vector.tensor_scalar(k, k, -MAGIC, None, ALU.add))
            for c in (ROPE_C1, ROPE_C2, ROPE_C3):
                link(dve, nc.vector.scalar_tensor_tensor(out=ang, in0=k, scalar=-c, in1=ang,
                                                         op0=ALU.mult, op1=ALU.add))
            nc.vector.tensor_scalar(tile(19), ang, 3.1415925, -3.1415925, ALU.min, ALU.max).then_inc(
                *mark("angle_ready", 0))
            dve.wait_ge(*at("half_sine_ready", 0))
            link(dve, nc.vector.tensor_tensor(tile(18), tile(18), tile(18), ALU.mult))
            link(dve, nc.vector.tensor_scalar(tile(18), tile(18), -2.0, 1.0, ALU.mult, ALU.add))

        def angles_act(act):
            act.wait_ge(*at("angle_ready", 0))
            nc.scalar.activation(tile(18), tile(19), ACT.Sin, scale=0.5).then_inc(
                *mark("half_sine_ready", 0))
            nc.scalar.activation(tile(19), tile(19), ACT.Sin).then_inc(*mark("sine_ready", 0))

        def rope_pe(pe):
            for i in range(12):
                pe.wait_ge(*at("head_normed", 8 + i))
                pe.wait_ge(*at("head_root", 19))
                if i >= 2:
                    pe.wait_ge(*at("rotated_read", i - 2))
                pe.matmul((B6, B7)[i % 2][:, :], cc("rot"), tile(i), start=True, stop=True).then_inc(
                    *mark("rotated", i))

        def rope_dve(dve):
            dve.wait_ge(*at("sine_ready", 0))
            dve.wait_ge(*at("head_normed", 19))
            for i in range(12):
                dve.wait_ge(*at("rotated", i))
                nc.vector.tensor_tensor(TMP[:, i % 2, :], (B6, B7)[i % 2][:, :], tile(19),
                                        ALU.mult).then_inc(*mark("rotated_read", i))
                link(dve, nc.vector.tensor_tensor(tile(i), tile(i), tile(18), ALU.mult))
                nc.vector.tensor_tensor(tile(i), tile(i), TMP[:, i % 2, :], ALU.add).then_inc(
                    *mark("roped", i))

        UNITS = [(s, n) for s in range(4) for n in range(TT)]
        VA = A[:, 12:18, :].rearrange("p a t -> p (a t)").rearrange("p (m c) -> p m c", m=TT)

        def near(n):
            return max(0, n - 1), min(TT - 1, n + 1)

        def score_set(i):
            return [BK[:, 0, :], BK[:, 1, :], BK[:, 2, :]] if i % 2 == 0 else \
                [BK[:, 3, :], S2[:, 0, :], S2[:, 1, :]]

        def key_blocks(n):
            lo, hi = near(n)
            return [(0, m) for m in range(lo, hi + 1)] + [(g, m) for g in (1, 2) for m in range(TT)]

        def unit_scores(i, n):
            w = P * len(key_blocks(n))
            v = A[:, 34 + 3 * (i % 2):37 + 3 * (i % 2), :].rearrange("p a t -> p (a t)")
            return v[:, 0:w]

        def unit_turned(i):
            return A[:, 40 + 3 * (i % 2):43 + 3 * (i % 2), :].rearrange("p a t -> p (a t)")

        def fills(n):
            b = key_blocks(n)
            return [b[k:k + 4] for k in range(0, len(b), 4)]

        def dil_scores_pe(pe, i):
            s, n = UNITS[i]
            pe.wait_ge(*at("roped", 11))
            if i >= 2:
                pe.wait_ge(*at("slot_out_read", i - 2))
                pe.wait_ge(*at("masked", (i - 2, 2)))
            else:
                pe.wait_ge(*at("products_read_by_act", ("va", 11)))
                pe.wait_ge(*at("probs_ready", ("c", 3, TT - 1)))
            lo, hi = near(n)
            r = slice(64 * (s % 2), 64 * (s % 2) + 64)
            for g in range(3):
                k0, k1 = (lo * P, (hi + 1) * P) if g == 0 else (0, T)
                t = 2 * g + s // 2
                mm = pe.matmul(score_set(i)[g][:, 0:k1 - k0], tile(t)[r, n * P:(n + 1) * P],
                               tile(6 + t)[r, k0:k1], start=True, stop=True)
            mm.then_inc(*mark("dil_scores_done", i))

        def dil_mix_pe(pe, i):
            s, n = UNITS[i]
            pe.wait_ge(*at("dil_normed", i))
            for f, blocks in enumerate(fills(n)):
                g = 3 * i + f
                if g >= 2:
                    pe.wait_ge(*at("dil_turned_read", divmod(g - 2, 3)))
                else:
                    pe.wait_ge(*at("rotated_read", 11))
                bank = (B6, B7)[g % 2]
                for k in range(len(blocks)):
                    c = (4 * f + k) * P
                    mm = pe.transpose(bank[:, k * P:(k + 1) * P], unit_scores(i, n)[:, c:c + P],
                                      ident)
                mm.then_inc(*mark("dil_turned", (i, f)))
            out_ = score_set(i)[0][64 * (s % 2):64 * (s % 2) + 64, 0:P]
            blocks = key_blocks(n)
            for k, (g, m) in enumerate(blocks):
                pe.wait_ge(*at("dil_turned_read", (i, k // 4)))
                h = 4 * g + s
                mm = pe.matmul(out_, VA[:, m, h * HD:(h + 1) * HD],
                               unit_turned(i)[:, k * P:(k + 1) * P],
                               start=(k == 0), stop=(k == len(blocks) - 1))
            mm.then_inc(*mark("slot_out", i))

        def dil_mask_dve(dve, i):
            s, n = UNITS[i]
            dve.wait_ge(*at("dil_scores_done", i))
            if i >= 2:
                dve.wait_ge(*at("dil_turned", (i - 2, 2)))
            lo, hi = near(n)
            sc_ = unit_scores(i, n)
            w0 = (hi + 1 - lo) * P
            c0 = 64 + 8 * (i % 2)
            for g in range(3):
                a0, w = (0, w0) if g == 0 else (w0 + (g - 1) * T, T)
                mask = (cc("m1", (lo - n + 1) * P, w0), cc("m2", (3 - n) * P, T), cc("m3"))[g]
                ins = nc.vector.tensor_tensor_reduce(out=sc_[:, a0:a0 + w], in0=score_set(i)[g][:, 0:w],
                                               in1=mask, scale=1.0, scalar=-3e38, op0=ALU.add,
                                               op1=ALU.max, accum_out=small[:, c0 + g:c0 + g + 1])
                ins.then_inc(*mark("masked", (i, g)))
            dve.wait_ge(*at("masked", (i, 2)))
            link(dve, nc.vector.tensor_reduce(small[:, c0 + 3:c0 + 4], small[:, c0:c0 + 3], AX_X,
                                              ALU.max))
            nc.vector.tensor_scalar(small[:, c0 + 4:c0 + 5], small[:, c0 + 3:c0 + 4], -0.125,
                                    None, ALU.mult).then_inc(*mark("dil_max_ready", i))

        def dil_norm_dve(dve, i):
            s, n = UNITS[i]
            c0 = 64 + 8 * (i % 2)
            dve.wait_ge(*at("dil_exp_ready", i))
            link(dve, nc.vector.reciprocal(small[:, c0 + 5:c0 + 6], small[:, c0 + 5:c0 + 6]))
            nc.vector.tensor_scalar(unit_scores(i, n), unit_scores(i, n),
                                    small[:, c0 + 5:c0 + 6], None, ALU.mult).then_inc(
                *mark("dil_normed", i))

        def dil_out_dve(dve, i):
            s, n = UNITS[i]
            r = slice(64 * (s % 2), 64 * (s % 2) + 64)
            dve.wait_ge(*at("slot_out", i))
            nc.vector.tensor_copy(tile(32 + s // 2)[r, n * P:(n + 1) * P],
                                  score_set(i)[0][r, 0:P]).then_inc(*mark("slot_out_read", i))

        def dil_exp_act(act, i):
            s, n = UNITS[i]
            c0 = 64 + 8 * (i % 2)
            act.wait_ge(*at("dil_max_ready", i))
            nc.scalar.activation(unit_scores(i, n), unit_scores(i, n), ACT.Exp,
                                 bias=small[:, c0 + 4:c0 + 5], scale=0.125,
                                 accum_out=small[:, c0 + 5:c0 + 6]).then_inc(
                *mark("dil_exp_ready", i))

        def dil_turn_act(act, i):
            s, n = UNITS[i]
            for f, blocks in enumerate(fills(n)):
                g = 3 * i + f
                act.wait_ge(*at("dil_turned", (i, f)))
                if i >= 2:
                    act.wait_ge(*at("slot_out", i - 2))
                w = P * len(blocks)
                nc.scalar.activation(unit_turned(i)[:, 4 * f * P:4 * f * P + w],
                                     (B6, B7)[g % 2][:, 0:w], ACT.Copy).then_inc(
                    *mark("dil_turned_read", (i, f)))

        NU = len(UNITS)

        def second_act(act, prev):
            norm_squares(act, "cm", lambda t: half[:, t, :], lambda t: [("loaded_c", 0)], width=M)
            norm_squares(act, "cn", xt, x_ready(prev))
            for j in range(4):
                ps = await_product(act, "ck", j)
                nc.scalar.activation(half[:, 16 + j, :], ps[:, 0:M], ACT.Copy).then_inc(
                    *mark("products_read_by_act", ("ck", j)))
            for j in range(4):
                ps = await_product(act, "cv", j)
                nc.scalar.activation(vmem(j % 2, (j // 2) * 256, 256), ps[:, 0:256], ACT.Copy).then_inc(
                    *mark("products_read_by_act", ("cv", j)))
            take(act, "cq", arena(16), ACT.Copy, n=4)
            hnorm_act(act, 0, 8)
            for h in range(4):
                softmax_act(act, "c", h, P ** -0.5)
                if h:
                    turned_act(act, "c", h - 1, 1)
            turned_act(act, "c", 3, 1)
            take(act, "qa", arena(0), ACT.Copy, n=6)
            take(act, "ka", arena(6), ACT.Copy, n=6)
            for j in range(12):
                ps = await_product(act, "va", j)
                nc.scalar.activation(VA[:, j % TT, (j // TT) * 256:(j // TT + 1) * 256],
                                     ps[:, 0:256], ACT.Copy).then_inc(
                    *mark("products_read_by_act", ("va", j)))
            hnorm_act(act, 8, 20)
            angles_act(act)
            for i in range(NU + 1):
                if i < NU:
                    dil_exp_act(act, i)
                if i:
                    dil_turn_act(act, i - 1)
            act.wait_ge(*at("slot_out", NU - 1))
            for n, first in (("cx", 0), ("cc", 6), ("cb", 12)):
                take(act, n, arena(first), ACT.Copy, n=6)
            for b in range(3):
                for j in range(8):
                    ps = await_product(act, f"gate{b}", j)
                    if b:
                        act.wait_ge(*at("products_read_by_dve", (f"proj{b - 1}", j)))
                    nc.scalar.activation(tile(34 + j), ps[:, :], ACT.Sigmoid).then_inc(
                        *mark("products_read_by_act", (f"gate{b}", j)))

        def second_pe(pe):
            norm_sum(pe, "cm", width=M)
            norm_sum(pe, "cn")
            product(pe, "ck", mem_tile, lambda k: [("normed_ready", ("cm", k))], width=M)
            product_rows(pe, "cv", lambda k, m: mem_tile(k)[:, m * P:(m + 1) * P], lambda k: [])
            product(pe, "cq", hn, lambda k: [("normed_ready", ("cn", k))])
            hnorm_pe(pe, 0, 8)
            for h in range(5):
                if h < 4:
                    scores_pe(pe, "c", h, 1)
                if h:
                    mix_pe(pe, "c", h - 1, 1)
            product(pe, "qa", hn, lambda k: [])
            product(pe, "ka", hn, lambda k: [])
            product_rows(pe, "va", lambda k, m: hn(k)[:, m * P:(m + 1) * P], lambda k: [])
            hnorm_pe(pe, 8, 20)
            rope_pe(pe)
            for i in range(NU + 1):
                if i < NU:
                    dil_scores_pe(pe, i)
                if i:
                    dil_mix_pe(pe, i - 1)
            pe.wait_ge(*at("slot_out_read", NU - 1))
            for n in ("cx", "cc", "cb"):
                product(pe, n, hn, lambda k: [])
            branch = (arena(32), arena(18), arena(24))
            ready = (lambda k: [("slot_out_read", NU - 1)], lambda k: [("conv2_ready", k)],
                     lambda k: [("products_read_by_act", ("cov", k))])
            for b in range(3):
                product(pe, f"gate{b}", hn, lambda k: [])
                product(pe, f"proj{b}", branch[b], ready[b])
            product(pe, "wout2", arena(42), lambda k: [("merged", k)])

        def second_dve(dve):
            norm_apply(dve, "cm", lambda t: half[:, t, :], mem_tile, lambda t: pc("g_mem", t),
                       width=M)
            norm_apply(dve, "cn", xt, hn, lambda t: pc("g_mix", t))
            nc.vector.memset(small[:, 254:255], 0.0).then_inc(*mark("residual_free", 0))
            hnorm_dve(dve, 0, 8)
            for h in range(4):
                softmax_dve(dve, "c", h, P ** -0.5)
            hnorm_dve(dve, 8, 20)
            angles_dve(dve)
            rope_dve(dve)
            for i in range(NU + 2):
                if i < NU:
                    dil_mask_dve(dve, i)
                if 1 <= i <= NU:
                    dil_norm_dve(dve, i - 1)
                    dil_out_dve(dve, i - 1)
            for j in range(6):
                u, y = tile(j), tile(18 + j)
                for n in ("cx", "cc", "cb"):
                    dve.wait_ge(*at("products_read_by_act", (n, j)))
                link(dve, nc.vector.tensor_tensor(u, u, tile(6 + j), ALU.mult))
                link(dve, nc.vector.tensor_scalar(y, u, pc("conv2", 6 + j), None, ALU.mult))
                link(dve, nc.vector.scalar_tensor_tensor(
                    out=y[:, 1:T], in0=u[:, 0:T - 1], scalar=pc("conv2", j), in1=y[:, 1:T],
                    op0=ALU.mult, op1=ALU.add))
                link(dve, nc.vector.scalar_tensor_tensor(
                    out=y[:, 0:T - 1], in0=u[:, 1:T], scalar=pc("conv2", 12 + j), in1=y[:, 0:T - 1],
                    op0=ALU.mult, op1=ALU.add))
                nc.vector.tensor_tensor(y, y, tile(12 + j), ALU.mult).then_inc(
                    *mark("conv2_ready", j))
            for b in range(3):
                for j in range(8):
                    dve.wait_ge(*at("products_read_by_act", (f"gate{b}", j)))
                    ps = await_product(dve, f"proj{b}", j)
                    dst = tile(42 + j) if b == 0 else TMP[:, j % 2, :]
                    nc.vector.tensor_tensor(dst, ps[:, :], tile(34 + j), ALU.mult).then_inc(
                        *mark("products_read_by_dve", (f"proj{b}", j)))
                    if b:
                        dve.wait_ge(*at("products_read_by_dve", (f"proj{b}", j)))
                        ins = nc.vector.tensor_tensor(tile(42 + j), tile(42 + j), dst, ALU.add)
                        if b == 1:
                            link(dve, ins)
                        else:
                            ins.then_inc(*mark("merged", j))
            for j in range(8):
                ps = await_product(dve, "wout2", j)
                nc.vector.tensor_tensor(X[:, j, :], ps[:, :], X[:, j, :], ALU.add).then_inc(
                    *mark("products_read_by_dve", ("wout2", j)))

        RT = A[:, 32, 0:288].rearrange("p (k n) -> p k n", k=8)
        BR = A[:, 33, 0:36]
        r4 = lambda t, c, n: A[:, t, c:c + 4 * n].rearrange("p (m n) -> p m n", m=4)
        LG = r4(34, 0, 36)
        SHG, EXG, OG = r4(34, 144, 4), r4(34, 160, 4), r4(34, 176, 4)
        MXG, SMG = A[:, 34, 192:196], A[:, 34, 196:200]
        SEL, SEL2, O1, O2 = (r4(34, 200 + 32 * i, 8) for i in range(4))
        M1, M2, DM, EX = (A[:, 34, 328 + 4 * i:332 + 4 * i] for i in range(4))
        TIEV = r4(34, 352, 8)
        TIEM = A[:, 34, 384:388]
        PROD = A[:, 35, 0:128].rearrange("p (m g e) -> p m g e", m=4, g=4)
        OE = [A[:, 35, 128 + 128 * i:256 + 128 * i].rearrange("p (m g e) -> p m g e", m=4, g=4)
              for i in range(2)]
        OM = A[:, 35, 384:512].rearrange("p (m n) -> p m n", m=4)
        CNT, NB, BEND, BST = (A[:, 36, 32 * i:32 * i + 32] for i in range(4))
        TMPB = A[:, 36, 128:256].rearrange("p (c n) -> p c n", c=4)
        DEST = A[:, 36, 256:384].rearrange("p (m n) -> p m n", m=4)
        DSUM = A[:, 36, 384:388]
        BF_ = A[0:1, 36, 392:392 + NBLK]
        CMP = A[0:1, 37:40, :].rearrange("p a t -> p (a t)")[:, 0:NBLK * NE]\
            .rearrange("p (b e) -> p b e", b=NBLK)
        XR = A[:, 48:56, :].rearrange("p (m a) t -> p m (a t)", m=TT)
        HR = A[:, 40:48, :].rearrange("p (m a) t -> p m (a t)", m=TT)
        WG = [A[:, 24 * s:24 * s + 8, :] for s in range(2)]
        WU = [A[:, 24 * s + 8:24 * s + 16, :] for s in range(2)]
        WD = [A[:, 24 * s + 16:24 * s + 24, :].rearrange("p (k a) t -> p k (a t)", k=4)
              for s in range(2)]
        XT = [flat[:, 1024 * s:1024 * s + 1024] for s in range(2)]
        XS = [flat[:, 2048 + 1024 * s:3072 + 1024 * s] for s in range(2)]
        HROW = [flat[:, 4096 + 512 * s:4608 + 512 * s] for s in range(2)]
        HT = [flat[:, 5120 + 512 * s:5632 + 512 * s] for s in range(2)]
        YR = [flat[:, 6144 + 1024 * s:7168 + 1024 * s] for s in range(2)]

        def onehot_dve(dve, shifted, n, dst):
            v = TIEV[:, :, 0:n]
            link(dve, nc.vector.tensor_scalar(v, shifted, 0.0, None, ALU.is_equal))
            link(dve, nc.vector.tensor_tensor(
                v, v, cc("tie", 0, n)[:, None, :].broadcast_to([P, 4, n]), ALU.mult))
            link(dve, nc.vector.tensor_reduce(TIEM, v, AX_X, ALU.max))
            link(dve, nc.vector.tensor_tensor(dst, v, TIEM[:, :, None].broadcast_to([P, 4, n]),
                                              ALU.is_equal))

        def wide(v, n):
            return v[:, :, None].broadcast_to([P, 4, n])

        def route_dve(dve):
            norm_apply(dve, "h2", xt, hn, lambda t: pc("g_ffn", t))
            dve.wait_ge(*at("loaded_conD", 0))
            dve.wait_ge(*at("loaded_router_bias", 0))
            dve.wait_ge(*at("loaded_router_bias2", 0))
            dve.wait_ge(*at("router_done", 0))
            link(dve, nc.vector.tensor_tensor(
                LG, BK[:, 0, 0:144].rearrange("p (m n) -> p m n", m=4),
                BR[:, None, :].broadcast_to([P, 4, 36]), ALU.add))
            link(dve, nc.vector.tensor_reduce(MXG, LG[:, :, 0:4], AX_X, ALU.max))
            nc.vector.tensor_tensor(SHG, LG[:, :, 0:4], wide(MXG, 4), ALU.subtract).then_inc(
                *mark("group_shifted", 0))
            dve.wait_ge(*at("group_shifted", 0))
            onehot_dve(dve, SHG, 4, OG)
            link(dve, nc.vector.tensor_tensor(
                PROD, LG[:, :, 4:36].rearrange("p m (g e) -> p m g e", g=4),
                OG[:, :, :, None].broadcast_to([P, 4, 4, 8]), ALU.mult))
            link(dve, nc.vector.tensor_reduce(SEL, PROD.rearrange("p m g e -> p m e g"), AX_X,
                                              ALU.add))
            link(dve, nc.vector.tensor_reduce(M1, SEL, AX_X, ALU.max))
            link(dve, nc.vector.tensor_tensor(SEL2, SEL, wide(M1, 8), ALU.subtract))
            onehot_dve(dve, SEL2, 8, O1)
            link(dve, nc.vector.scalar_tensor_tensor(out=SEL2, in0=O1, scalar=-BIG, in1=SEL,
                                                     op0=ALU.mult, op1=ALU.add))
            link(dve, nc.vector.tensor_reduce(M2, SEL2, AX_X, ALU.max))
            nc.vector.tensor_tensor(DM, M2, M1, ALU.subtract).then_inc(*mark("margin_ready", 0))
            link(dve, nc.vector.tensor_tensor(SEL2, SEL2, wide(M2, 8), ALU.subtract))
            onehot_dve(dve, SEL2, 8, O2)
            for k, o in enumerate((O1, O2)):
                link(dve, nc.vector.tensor_tensor(
                    OE[k], OG[:, :, :, None].broadcast_to([P, 4, 4, 8]),
                    o[:, :, None, :].broadcast_to([P, 4, 4, 8]), ALU.mult))
            oe = [v.rearrange("p m g e -> p m (g e)") for v in OE]
            nc.vector.tensor_tensor(OM, oe[0], oe[1], ALU.add).then_inc(*mark("choices_ready", 0))
            dve.wait_ge(*at("margin_exp_ready", 0))
            link(dve, nc.vector.tensor_reduce(SMG, EXG, AX_X, ALU.add))
            link(dve, nc.vector.tensor_scalar(wts[:, 0:4], EX, 1.0, None, ALU.add))
            link(dve, nc.vector.tensor_tensor(wts[:, 0:4], wts[:, 0:4], SMG, ALU.mult))
            link(dve, nc.vector.reciprocal(wts[:, 0:4], wts[:, 0:4]))
            link(dve, nc.vector.tensor_tensor(wts[:, 4:8], wts[:, 0:4], EX, ALU.mult))
            dve.wait_ge(*at("ranks_done", 0))
            link(dve, nc.vector.tensor_copy(CNT, BK[:, 1, 128:160]))
            for c in range(4):
                ins = nc.vector.tensor_scalar(TMPB[:, c, :], CNT, float(P * c), None, ALU.is_gt)
            link(dve, ins)
            link(dve, nc.vector.tensor_reduce(NB, TMPB.rearrange("p c n -> p n c"), AX_X, ALU.add))
            link(dve, nc.vector.tensor_tensor_scan(BEND, ones[:, 0:32], NB, 0.0, ALU.mult, ALU.add))
            link(dve, nc.vector.tensor_tensor(BST, BEND, NB, ALU.subtract))
            link(dve, nc.vector.tensor_tensor(
                CMP, BEND[0:1, None, :].broadcast_to([1, NBLK, NE]),
                cc("blkid")[0:1, :, None].broadcast_to([1, NBLK, NE]), ALU.is_le))
            link(dve, nc.vector.tensor_reduce(BF_, CMP, AX_X, ALU.add))
            link(dve, nc.vector.tensor_scalar(BF_, BF_, float(NE - 1), None, ALU.min))
            nc.vector.tensor_copy(bexp[0:1, 0:NBLK], BF_).then_inc(
                *mark("block_experts_ready", 0))
            link(dve, nc.vector.scalar_tensor_tensor(
                out=DEST, in0=BST[:, None, :].broadcast_to([P, 4, 32]), scalar=float(P),
                in1=BK[:, 1, 0:128].rearrange("p (m n) -> p m n", m=4), op0=ALU.mult, op1=ALU.add))
            for k in range(2):
                link(dve, nc.vector.tensor_tensor(oe[k], oe[k], DEST, ALU.mult))
                link(dve, nc.vector.tensor_reduce(DSUM, oe[k], AX_X, ALU.add))
                link(dve, nc.vector.tensor_copy(rows_of[:, 4 * k:4 * k + 4], DSUM))
            nc.vector.memset(small[:, 253:254], 0.0).then_inc(*mark("rows_known", 0))

        def route_act(act, prev):
            norm_squares(act, "h2", xt, prev)
            act.wait_ge(*at("group_shifted", 0))
            nc.scalar.activation(EXG, SHG, ACT.Exp).then_inc(*mark("group_exp_ready", 0))
            act.wait_ge(*at("margin_ready", 0))
            nc.scalar.activation(EX, DM, ACT.Exp).then_inc(*mark("margin_exp_ready", 0))
            act.wait_ge(*at("scratch_cleared", 0))
            for key, dst in (("h2", HR), ("xr", XR)):
                for m in range(TT):
                    for g in range(2):
                        act.wait_ge(*at("turned", (key, m, g)))
                        nc.scalar.activation(dst[:, m, g * 512:(g + 1) * 512],
                                             (B6, B7)[g][:, :], ACT.Copy).then_inc(
                            *mark("rows_ready", (key, m, g)))

        def turn_rows_pe(pe, src, key, ready):
            for m in range(TT):
                for g in range(2):
                    for r in ready(m, g):
                        pe.wait_ge(*at(*r))
                    for i in range(4):
                        mm = pe.transpose((B6, B7)[g][:, i * P:(i + 1) * P],
                                          src(4 * g + i)[:, m * P:(m + 1) * P], ident)
                    mm.then_inc(*mark("turned", (key, m, g)))

        def route_pe(pe):
            norm_sum(pe, "h2")
            pe.wait_ge(*at("loaded_router0", 0))
            pe.wait_ge(*at("loaded_router1", 0))
            for m in range(TT):
                for k in range(8):
                    pe.wait_ge(*at("normed_ready", ("h2", k)))
                    mm = pe.matmul(BK[:, 0, 36 * m:36 * m + 36], hn(k)[:, m * P:(m + 1) * P],
                                   RT[:, k, :], start=(k == 0), stop=(k == 7))
            mm.then_inc(*mark("router_done", 0))
            turn_rows_pe(pe, hn, "h2", lambda m, g: [("root_ready", "h2")] +
                         ([("rows_ready", ("h2", m - 1, g))] if m else []))
            turn_rows_pe(pe, xt, "xr", lambda m, g: [("rows_ready", ("xr", m - 1, g) if m else
                                                      ("h2", 3, g))])
            pe.wait_ge(*at("choices_ready", 0))
            for m in range(TT):
                for k in range(m + 1):
                    pe.matmul(BK[:, 1, 32 * m:32 * m + 32], ones if k < m else cc("tri"),
                              OM[:, k, :], start=(k == 0), stop=(k == m))
            for k in range(TT):
                mm = pe.matmul(BK[:, 1, 128:160], ones, OM[:, k, :], start=(k == 0), stop=(k == 3))
            mm.then_inc(*mark("ranks_done", 0))

        def scatter_pool(pool):
            pool.wait_ge(*at("rows_known", 0))
            pool.wait_ge(*at("rows_ready", ("h2", 3, 1)))
            pool.wait_ge(*at("scratch_cleared", 0))
            for k in range(2):
                for m in range(TT):
                    j = 4 * k + m
                    pool.indirect_dma_start(
                    out=xs_dram, out_offset=bass.IndirectOffsetOnAxis(
                        ap=rows_of[:, j:j + 1].bitcast(U32), axis=0),
                    in_=HR[:, m, :], in_offset=None).then_inc(*mark(f"scattered{j}", 0, 16))

        if "D" in phases:
            s_x = [sem(f"block_rows_loaded{s}") for s in range(2)]
            s_g = [sem(f"block_gate_loaded{s}") for s in range(2)]
            s_u = [sem(f"block_up_loaded{s}") for s in range(2)]
            s_d = [sem(f"block_down_loaded{s}") for s in range(2)]
            s_y = [sem(f"block_stored{s}") for s in range(2)]
            s_xturned = sem("block_rows_turned")
            s_xt = sem("block_rows_ready")
            s_gate, s_up, s_down = (sem("block_" + n) for n in
                                    ("gate_done", "up_done", "down_done"))
            s_silu, s_h = sem("block_silu_ready"), sem("block_hidden_ready")
            s_hturned, s_ht = sem("block_hidden_turned"), sem("block_turned_ready")
            s_yr = sem("block_output_ready")

        def over(count):
            return count // 2 + 1

        def block_loads(sp, b, s, uses, first):
            e = sp.value_load(bexp[0:1, b:b + 1] if isinstance(b, int)
                              else bexp[0:1, bass.ds(b, 1)], min_val=0, max_val=NE - 1)
            if not first:
                sp.wait_ge(s_xturned, b - 1)
            sp.dma_start(XS[s], xs_dram[bass.ds(b * P, P), :]).then_inc(s_x[s], 16)
            if not first:
                sp.wait_ge(s_gate, b - 1)
            sp.dma_start(WG[s], a.w_gate_2[0][bass.ds(e, 1)].rearrange(
                "o (k p) n -> p (o k) n", p=P)).then_inc(s_g[s], 16)
            if not first:
                sp.wait_ge(s_up, b - 1)
            sp.dma_start(WU[s], a.w_up_2[0][bass.ds(e, 1)].rearrange(
                "o (k p) n -> p (o k) n", p=P)).then_inc(s_u[s], 16)
            if not first:
                sp.wait_ge(s_down, b - 1)
            sp.dma_start(WD[s], a.w_down_2[0][bass.ds(e, 1)].rearrange(
                "o (k p) n -> p (o k) n", p=P)).then_inc(s_d[s], 16)

        def block_turn_pe(pe, b, s, uses, first):
            pe.wait_ge(s_x[s], 16 * uses)
            if not first:
                pe.wait_ge(s_xt, 2 * b)
            for g in range(2):
                for i in range(4):
                    mm = pe.transpose((B6, B7)[g][:, i * P:(i + 1) * P],
                                      XS[s][:, (4 * g + i) * P:(4 * g + i + 1) * P], ident)
            mm.then_inc(s_xturned, 1)

        def block_up_pe(pe, b, s, uses, first):
            pe.wait_ge(s_xt, 2 * b + 2)
            pe.wait_ge(s_g[s], 16 * uses)
            if not first:
                pe.wait_ge(s_silu, b)
            for k in range(8):
                mm = pe.matmul(BK[:, 0, :], XT[s][:, k * P:(k + 1) * P], WG[s][:, k, :],
                               start=(k == 0), stop=(k == 7))
            mm.then_inc(s_gate, 1)
            pe.wait_ge(s_u[s], 16 * uses)
            if not first:
                pe.wait_ge(s_h, b)
            for k in range(8):
                mm = pe.matmul(BK[:, 1, :], XT[s][:, k * P:(k + 1) * P], WU[s][:, k, :],
                               start=(k == 0), stop=(k == 7))
            mm.then_inc(s_up, 1)

        def block_down_pe(pe, b, s, uses, first):
            pe.wait_ge(s_h, b + 1)
            if not first:
                pe.wait_ge(s_ht, b)
            for k in range(4):
                mm = pe.transpose(S2[:, 0, k * P:(k + 1) * P], HROW[s][:, k * P:(k + 1) * P], ident)
            mm.then_inc(s_hturned, 1)
            pe.wait_ge(s_ht, b + 1)
            pe.wait_ge(s_d[s], 16 * uses)
            if not first:
                pe.wait_ge(s_yr, 2 * b)
            for n in range(2):
                for k in range(4):
                    mm = pe.matmul(BK[:, 2 + n, :], HT[s][:, k * P:(k + 1) * P],
                                   WD[s][:, k, n * T:(n + 1) * T], start=(k == 0), stop=(k == 3))
            mm.then_inc(s_down, 1)

        def block_rows_act(act, b, s):
            act.wait_ge(s_xturned, b + 1)
            for g in range(2):
                nc.scalar.activation(XT[s][:, g * T:(g + 1) * T], (B6, B7)[g][:, :], ACT.Copy)\
                    .then_inc(s_xt, 1)

        def block_silu_act(act, b, s, first):
            act.wait_ge(s_gate, b + 1)
            if not first:
                act.wait_ge(s_hturned, b - 1)
            nc.scalar.activation(HROW[s], BK[:, 0, :], ACT.Silu).then_inc(s_silu, 1)

        def block_out_act(act, b, s, uses, first):
            act.wait_ge(s_hturned, b + 1)
            nc.scalar.activation(HT[s], S2[:, 0, :], ACT.Copy).then_inc(s_ht, 1)
            act.wait_ge(s_down, b + 1)
            if not first:
                act.wait_ge(s_y[s], 16 * (uses - 1))
            for n in range(2):
                nc.scalar.activation(YR[s][:, n * T:(n + 1) * T], BK[:, 2 + n, :], ACT.Copy)\
                    .then_inc(s_yr, 1)
            act.wait_ge(s_yr, 2 * b + 2)
            act.dma_start(ys_dram[bass.ds(b * P, P), :], YR[s]).then_inc(s_y[s], 16)

        def block_hidden_dve(dve, b, s):
            dve.wait_ge(s_silu, b + 1)
            dve.wait_ge(s_up, b + 1)
            nc.vector.tensor_tensor(HROW[s], BK[:, 1, :], HROW[s], ALU.mult).then_inc(s_h, 1)

        LOOPED = (NBLK - 3) // 2

        def experts_sp(sp):
            sp.wait_ge(*at("block_experts_ready", 0))
            for j in range(8):
                sp.wait_ge(*at(f"scattered{j}", 0))
            sp.wait_ge(*at("rows_ready", ("h2", 3, 1)))
            block_loads(sp, 0, 0, 1, True)
            block_loads(sp, 1, 1, 1, True)
            with sp.Fori(0, LOOPED) as i:
                block_loads(sp, 2 * i + 2, 0, i + 2, False)
                block_loads(sp, 2 * i + 3, 1, i + 2, False)
            block_loads(sp, NBLK - 1, 0, NBLK // 2 + 1, False)

        def experts_pe(pe):
            pe.wait_ge(*at("rows_ready", ("xr", 3, 1)))
            pe.wait_ge(*at("block_experts_ready", 0))
            pe.wait_ge(*at("rows_known", 0))
            block_turn_pe(pe, 0, 0, 1, True)
            block_up_pe(pe, 0, 0, 1, True)
            block_turn_pe(pe, 1, 1, 1, False)

            def step(b, s, uses, before, first=False, last=False):
                block_up_pe(pe, b, s, uses, False)
                if not last:
                    block_turn_pe(pe, b + 1, 1 - s, before + 1, False)
                block_down_pe(pe, b - 1, 1 - s, before, first)
            step(1, 1, 1, 1, first=True)
            step(2, 0, 2, 1)
            with pe.Fori(1, LOOPED) as i:
                step(2 * i + 1, 1, i + 1, i + 1)
                step(2 * i + 2, 0, i + 2, i + 1)
            step(NBLK - 2, 1, NBLK // 2, NBLK // 2)
            step(NBLK - 1, 0, NBLK // 2 + 1, NBLK // 2, last=True)
            block_down_pe(pe, NBLK - 1, 0, NBLK // 2 + 1, False)

        def experts_act(act):
            block_rows_act(act, 0, 0)
            block_silu_act(act, 0, 0, True)
            block_rows_act(act, 1, 1)

            def step(b, s, uses, first=False, last=False):
                block_silu_act(act, b, s, first)
                if not last:
                    block_rows_act(act, b + 1, 1 - s)
                block_out_act(act, b - 1, 1 - s, uses, first)
            step(1, 1, 1, first=True)
            block_silu_act(act, 2, 0, False)
            block_rows_act(act, 3, 1)
            block_out_act(act, 1, 1, 1, True)
            with act.Fori(1, LOOPED) as i:
                step(2 * i + 1, 1, i + 1)
                step(2 * i + 2, 0, i + 1)
            step(NBLK - 2, 1, NBLK // 2)
            step(NBLK - 1, 0, NBLK // 2, last=True)
            block_out_act(act, NBLK - 1, 0, NBLK // 2 + 1, False)

        def experts_dve(dve):
            block_hidden_dve(dve, 0, 0)
            with dve.Fori(0, NBLK // 2) as i:
                block_hidden_dve(dve, 2 * i + 1, 1)
                block_hidden_dve(dve, 2 * i + 2, 0)

        def got(k, m):
            return A[:, 8 * k:8 * k + 8, :].rearrange("p (m a) t -> p m (a t)", m=TT)[:, m, :]

        def gather_pool(pool):
            pool.wait_ge(s_y[0], 16 * (NBLK // 2 + 1))
            pool.wait_ge(s_y[1], 16 * (NBLK // 2))
            for m in range(TT):
                for k in range(2):
                    j = 4 * k + m
                    pool.indirect_dma_start(
                    out=got(k, m), out_offset=None, in_=ys_dram,
                    in_offset=bass.IndirectOffsetOnAxis(ap=rows_of[:, j:j + 1].bitcast(U32),
                                                        axis=0)).then_inc(
                        *mark(f"gathered{j}", 0, 16))

        def combine_dve(dve):
            for m in range(TT):
                for k in range(2):
                    dve.wait_ge(*at(f"gathered{4 * k + m}", 0))
                    dve.wait_ge(*at("rows_ready", ("xr", 3, 1)))
                    ins = nc.vector.scalar_tensor_tensor(
                        out=XR[:, m, :], in0=got(k, m), scalar=wts[:, 4 * k + m:4 * k + m + 1],
                        in1=XR[:, m, :], op0=ALU.mult, op1=ALU.add)
                    if k == 0:
                        link(dve, ins)
                    else:
                        ins.then_inc(*mark("token_done", m))

        def store_sp(sp):
            for m in range(TT):
                sp.wait_ge(*at("token_done", m))
                sp.dma_start(out[m * P:(m + 1) * P, :], XR[:, m, :]).then_inc(
                    *mark(f"output_stored{m}", 0, 16))
            for m in range(TT):
                sp.wait_ge(*at(f"output_stored{m}", 0))

        def mlp_act(act, tag, prev):
            norm_squares(act, tag + "n", xt, x_ready(prev))
            for j in range(32):
                ps = await_product(act, tag + "up", j)
                nc.scalar.activation(tile(j), ps[:, :], ACT.Relu).then_inc(
                    *mark("products_read_by_act", (tag + "up", j)))
                act.wait_ge(*at("products_read_by_act", (tag + "up", j)))
                nc.scalar.activation(tile(j), tile(j), ACT.Square).then_inc(
                    *mark("hidden_ready", (tag, j)))
            for j in range(8):
                ps = await_product(act, tag + "down", j)
                nc.scalar.activation(tile(32 + j), ps[:, :], ACT.Copy).then_inc(
                    *mark("products_read_by_act", (tag + "down", j)))
            norm_squares(act, tag + "x", arena(32),
                         lambda t: [("products_read_by_act", (tag + "down", t))])

        def mlp_pe(pe, tag):
            norm_sum(pe, tag + "n")
            product(pe, tag + "up", hn, lambda k: [("normed_ready", (tag + "n", k))])
            product(pe, tag + "down", arena(0), lambda k: [("hidden_ready", (tag, k))])
            norm_sum(pe, tag + "x")

        def mlp_dve(dve, i, tag):
            norm_apply(dve, tag + "n", xt, hn, gain(i, 4))
            norm_add(dve, tag + "x", arena(32), gain(i, 5))

        MIX = [(0, "r"), (1, "w"), (2, "k"), (4, "a"), (3, "v"), (5, "g")]
        LASTMM = {"r": ("r", 7), "w": ("w1", 0), "k": ("k_", 7), "a": ("a1", 0), "v": ("v_", 7),
                  "g": ("g1", 0)}
        RB = flat[:, 0:2048].rearrange("p (h t) -> p h t", h=NH)
        W1T = flat[:, 2048:3072].rearrange("p (q t) -> p q t", q=8)
        W2 = flat[:, 3072:4096].rearrange("p (u q i) -> p u q i", u=2, q=8)
        ST = flat[:, 4096:6656].rearrange("p (s q i) -> p s q i", s=5, q=8)
        scf = SC.rearrange("p a t -> p (a t)")
        NXA = [v.rearrange("p (pp u c) -> p pp u c", pp=2, u=2)
               for v in (flat[:, 6656:8192], scf[:, 1536:3072])]
        GM = [scf[:, 768 * i:768 * (i + 1)].rearrange("p (u c) -> p u c", u=2) for i in range(2)]
        AV = [LB[:, 0, 128 * i:128 * (i + 1)].rearrange("p (u c) -> p u c", u=2) for i in range(2)]
        VR = A[:, 40:48, :].rearrange("p (m a) t -> p m (a t)", m=TT)
        ROW = A[:, 16:24, :].rearrange("p (m a) t -> p m (a t)", m=4)
        U = ROW[:, 3, :].rearrange("p (u q i) -> p u q i", u=2, q=8)
        Y0 = 24
        KT_, RT_, BT_, AT_ = 8, 0, 32, 48

        def mixbuf(m, t):
            return tile((48 if m % 2 == 0 else 40) + t)

        def mix_act(act, m):
            i, name = MIX[m]
            for t in range(8):
                act.wait_ge(*at("normed_ready", ("l1n", t)))
                act.wait_ge(*at("complements_ready", 0))
                if m >= 2:
                    act.wait_ge(*at("products_done", LASTMM[MIX[m - 2][1]]))
                nc.scalar.activation(mixbuf(m, t), hn(t), ACT.Copy,
                                     scale=comp[:, i * 8 + t:i * 8 + t + 1]).then_inc(
                    *mark("mix_started", (m, t)))

        def take(act, name, dst, func, bias=None, n=8, rows=P):
            for j in range(n):
                ps = await_product(act, name, j)
                kw = {} if bias is None else {"bias": pc(bias, j)}
                nc.scalar.activation(dst(j), ps[0:rows, :], func, **kw).then_inc(
                    *mark("products_read_by_act", (name, j)))

        def rwkv_act(act, prev):
            norm_squares(act, "l1n", xt, x_ready(prev))
            if "D" in phases:
                act.wait_ge(*at("scratch_cleared", 0))
            mix_act(act, 0)
            mix_act(act, 1)
            take(act, "r", arena(0), ACT.Copy)
            mix_act(act, 2)
            take(act, "w1", lambda j: LW[0:64, :], ACT.Tanh, n=1, rows=64)
            mix_act(act, 3)
            take(act, "w2", arena(24), ACT.Sigmoid, "w0")
            take(act, "k_", arena(8), ACT.Copy)
            mix_act(act, 4)
            take(act, "a1", lambda j: LB[0:64, 0, :], ACT.Copy, n=1, rows=64)
            mix_act(act, 5)
            take(act, "a2", arena(32), ACT.Sigmoid, "a0")
            take(act, "v_", arena(16), ACT.Copy)
            take(act, "g1", lambda j: LB[:, 1, :], ACT.Sigmoid, n=1)
            def square(j):
                act.wait_ge(*at("kk_raw", j))
                if j >= 2:
                    act.wait_ge(*at("kk_summed", j - 2))
                nc.scalar.activation(SQ[:, j % 2, :], tile(48 + j), ACT.Square).then_inc(
                    *mark("kk_square", j))
            square(0)
            for j in range(8):
                if j < 7:
                    square(j + 1)
                act.wait_ge(*at("kk_summed", j))
                if j >= 2:
                    act.wait_ge(*at("kk_ready", j - 2))
                nc.scalar.activation(TMP[:, j % 2, :], (B6, B7)[j % 2][:, :], ACT.Sqrt).then_inc(
                    *mark("kk_root", j))
            for j in range(8):
                act.wait_ge(*at("log_decay_ready", j))
                act.wait_ge(*at("kk_ready", 7))
                if j >= 2:
                    act.wait_ge(*at("tilde_ready", j - 2))
                nc.scalar.activation(tile(24 + j), tile(24 + j), ACT.Exp, scale=-DECAY).then_inc(
                    *mark("decays_ready", (j, 0)))
                nc.scalar.activation(TMP[:, j % 2, :], tile(40 + j), ACT.Exp, scale=DECAY).then_inc(
                    *mark("decays_ready", (j, 1)))
                nc.scalar.activation(tile(40 + j), tile(40 + j), ACT.Exp, scale=-DECAY).then_inc(
                    *mark("decays_ready", (j, 2)))
                act.wait_ge(*at("decays_ready", (j, 2)))
                nc.scalar.activation(Pc[:, j, :], tile(40 + j)[:, CH - 1:T:CH], ACT.Copy).then_inc(
                    *mark("chunk_decay_ready", j))
            for m in range(TT):
                for g in range(2):
                    act.wait_ge(*at("turned", ("v", m, g)))
                    if m == 0 and g == 0:
                        act.wait_ge(*at("tilde_ready", 7))
                    nc.scalar.activation(VR[:, m, g * 512:(g + 1) * 512],
                                         (B6, B7)[g][:, :], ACT.Copy).then_inc(
                        *mark("rows_ready", ("v", m, g)))
            for tl in range(TT):
                rows_act(act, tl)
                for q0 in range(0, 8, 2):
                    for step in range(len(PAIR_ACT)):
                        for q in (q0, q0 + 1):
                            PAIR_ACT[step](act, tl, q)
            gn_act(act)
            take(act, "w_o", arena(40), ACT.Copy)
            norm_squares(act, "l1o", arena(40), lambda t: [("products_read_by_act", ("w_o", t))])

        def rows_act(act, tl):
            for n in range(3):
                for g in range(2):
                    act.wait_ge(*at("turned", (tl, n, g)))
                    nc.scalar.activation(ROW[:, n, g * 512:(g + 1) * 512],
                                         (B6, B7)[g][:, :], ACT.Copy).then_inc(
                        *mark("rows_ready", (tl, n, g)))

        def pair_banks(q):
            return BK[:, 2 * (q % 2):2 * (q % 2) + 2, :]

        def pa_keep(act, tl, q):
            act.wait_ge(*at("grams_masked", (tl, q, 1)))
            nc.scalar.activation(RB[:, 2 * q:2 * q + 2, :], GM[q % 2][:, :, 0:128], ACT.Copy).then_inc(
                *mark("rb_kept", (tl, q)))

        def pa_level(level):
            def f(act, tl, q):
                act.wait_ge(*at("level_done", (tl, q, level)))
                dst = NXA[q % 2][:, level % 2, :, :]
                src = pair_banks(q)[:, 0, :].rearrange("p (x u c) -> p u x c", x=2, u=2)
                v = dst.rearrange("p u (x c) -> p u x c", x=3)
                if level < 4:
                    for u in range(2):
                        ins = nc.scalar.activation(v[:, u, 0:3:2, :], src[:, u, :, :], ACT.Copy)
                    ins.then_inc(*mark("powers_ready", (tl, q, level)))
                else:
                    nc.scalar.activation(v[:, :, 2, :], src[:, :, 1, :], ACT.Copy).then_inc(
                        *mark("powers_ready", (tl, q, level)))
            return f

        def pa_w1(act, tl, q):
            act.wait_ge(*at("pair_done", (tl, q)))
            nc.scalar.activation(W1T[:, q, :], pair_banks(q)[:, 0, 128:256], ACT.Copy).then_inc(
                *mark("w1_ready", (tl, q)))

        PAIR_ACT = [pa_keep, pa_level(1), pa_level(2), pa_level(3), pa_level(4), pa_w1]

        def head(n, q, u, tl):
            return tile(n + q)[64 * u:64 * u + 64, tl * P:(tl + 1) * P]

        def pp_gram(pe, tl, q):
            if q >= 2:
                pe.wait_ge(*at("w2_ready", (tl, q - 2)))
                pe.wait_ge(*at("w1_ready", (tl, q - 2)))
            elif tl:
                pe.wait_ge(*at("wkv_added", (tl - 1, 1)))
            for u in range(2):
                bank = pair_banks(q)[:, u, :]
                for j, n in enumerate((BT_, KT_)):
                    for i, r in enumerate((AT_, RT_)):
                        mm = pe.matmul(bank[:, (2 * j + i) * P:(2 * j + i + 1) * P],
                                       head(n, q, u, tl), head(r, q, u, tl),
                                       start=True, stop=True)
            mm.then_inc(*mark("grams_done", (tl, q)))

        def pp_low(pe, tl, q):
            pe.wait_ge(*at("grams_masked", (tl, q, 1)))
            for u in range(2):
                mm = pe.matmul(pair_banks(q)[:, u, 384:512], head(AT_, q, u, tl),
                               head(BT_, q, u, tl), start=True, stop=True)
            mm.then_inc(*mark("low_done", (tl, q)))

        def pp_level(level):
            def f(pe, tl, q):
                b = NXA[q % 2][:, (level - 1) % 2, :, :]
                if level == 1:
                    pe.wait_ge(*at("start_ready", (tl, q)))
                else:
                    pe.wait_ge(*at("powers_ready", (tl, q, level - 1)))
                    if level > 2:
                        pe.wait_ge(*at("inverse_ready", (tl, q, level - 1)))
                    else:
                        pe.wait_ge(*at("av_ready", (tl, q)))
                bank = pair_banks(q)
                for u in range(2):
                    N, X_, A_ = b[:, u, 0:128], b[:, u, 128:256], b[:, u, 256:384]
                    if level < 4:
                        pe.matmul(bank[:, 0, u * P:(u + 1) * P], A_, N, start=True, stop=True)
                    if level > 1:
                        pe.matmul(bank[:, 1, u * P:(u + 1) * P], A_, X_, start=True, stop=True)
                    else:
                        h = 2 * q + u
                        v = VR[:, tl, h * 64:(h + 1) * 64]
                        pe.matmul(bank[:, 1, 256 + 64 * u:320 + 64 * u], GM[q % 2][:, u, 128:256], v,
                                  start=True, stop=True)
                        pe.matmul(bank[64 * u:64 * u + 64, 1, 384:512], v,
                                  GM[q % 2][:, u, 256:384], start=True, stop=True)
                    mm = pe.matmul(bank[:, 0, 256 + u * P:256 + (u + 1) * P], N, A_,
                                   start=True, stop=True)
                mm.then_inc(*mark("level_done", (tl, q, level)))
            return f

        def pp_last(pe, tl, q):
            pe.wait_ge(*at("powers_ready", (tl, q, 4)))
            pe.wait_ge(*at("inverse_ready", (tl, q, 4)))
            b = NXA[q % 2][:, 0, :, :]
            for u in range(2):
                mm = pe.matmul(pair_banks(q)[:, 1, u * P:(u + 1) * P], b[:, u, 256:384],
                               b[:, u, 128:256],
                               start=True, stop=True)
            mm.then_inc(*mark("level_done", (tl, q, 5)))

        def pp_end(pe, tl, q):
            pe.wait_ge(*at("inverse_ready", (tl, q, 5)))
            for u in range(2):
                h = 2 * q + u
                X_ = NXA[q % 2][:, 1, u, 128:256]
                pe.matmul(pair_banks(q)[:, 1, u * 64:(u + 1) * 64], X_, AV[q % 2][:, u, :], start=True, stop=True)
                mm = pe.matmul(pair_banks(q)[64 * u:64 * u + 64, 0, 128:256],
                               ROW[:, 0, h * 64:(h + 1) * 64], X_, start=True, stop=True)
            mm.then_inc(*mark("pair_done", (tl, q)))

        PAIR_PE = [pp_gram, pp_low, pp_level(1), pp_level(2), pp_level(3), pp_level(4), pp_last,
                   pp_end]

        def pd_mask(dve, tl, q):
            dve.wait_ge(*at("grams_done", (tl, q)))
            src = pair_banks(q)
            for u in range(2):
                nc.vector.tensor_tensor(NXA[q % 2][:, 0, u, 0:128], src[:, u, 0:128],
                                        cc("gmask", 0, 128), ALU.mult).then_inc(
                    *mark("strict_ready", (tl, q, u)))
                if u == 0 and tl + q >= 2 or tl:
                    who = (tl, q - 2) if q >= 2 else (tl - 1, q + 6)
                    if who[0] >= 0:
                        dve.wait_ge(*at("rb_kept", who))
                nc.vector.tensor_tensor(GM[q % 2][:, u, :], src[:, u, 128:512],
                                        cc("gmask", 128, 384), ALU.mult).then_inc(
                    *mark("grams_masked", (tl, q, u)))

        def pd_low(dve, tl, q):
            dve.wait_ge(*at("low_done", (tl, q)))
            dve.wait_ge(*at("strict_ready", (tl, q, 1)))
            for u in range(2):
                nc.vector.tensor_tensor(NXA[q % 2][:, 1, u, 128:256], NXA[q % 2][:, 0, u, 0:128],
                                        ident, ALU.add)
                ins = nc.vector.tensor_tensor(NXA[q % 2][:, 0, u, 256:384],
                                              pair_banks(q)[:, u, 384:512], cc("lmask"), ALU.mult)
            ins.then_inc(*mark("start_ready", (tl, q)))

        def pd_av(dve, tl, q):
            dve.wait_ge(*at("level_done", (tl, q, 1)))
            nc.vector.tensor_copy(tile(Y0 + q)[:, tl * P:(tl + 1) * P],
                                  pair_banks(q)[:, 1, 384:512])
            nc.vector.tensor_copy(AV[q % 2].rearrange("p u c -> p (u c)"),
                                  pair_banks(q)[:, 1, 256:384]).then_inc(
                *mark("av_ready", (tl, q)))

        def pd_level(level):
            def f(dve, tl, q):
                dve.wait_ge(*at("level_done", (tl, q, level)))
                if level > 2:
                    dve.wait_ge(*at("inverse_ready", (tl, q, level - 1)))
                else:
                    dve.wait_ge(*at("start_ready", (tl, q)))
                old, new = NXA[q % 2][:, (level - 1) % 2], NXA[q % 2][:, level % 2]
                nc.vector.tensor_tensor(new[:, :, 128:256], 
                                        pair_banks(q)[:, 1, 0:256].rearrange(
                                            "p (u c) -> p u c", u=2),
                                        old[:, :, 128:256], ALU.add).then_inc(
                    *mark("inverse_ready", (tl, q, level)))
            return f

        def pd_w2(dve, tl, q):
            dve.wait_ge(*at("pair_done", (tl, q)))
            nc.vector.tensor_copy(W2[:, :, q, :], pair_banks(q)[:, 1, 0:128].rearrange(
            "p (u c) -> p u c", u=2)).then_inc(*mark("w2_ready", (tl, q)))

        PAIR_DVE = [pd_mask, pd_low, pd_av, pd_level(2), pd_level(3), pd_level(4), pd_level(5),
                    pd_w2]

        def chunk_pe(pe, tl, c):
            n = tl * 4 + c
            r0 = CH * c
            rows = slice(r0, r0 + CH)
            pe.wait_ge(*at("w1_ready", (tl, 7)))
            pe.wait_ge(*at("state_ready", n))
            if c:
                pe.wait_ge(*at("u_ready", n - 1))
            for q in range(8):
                for u in range(2):
                    mm = pe.matmul(S2[rows, u, q * 64:(q + 1) * 64],
                                   W1T[64 * u:64 * u + 64, q, rows], ST[64 * u:64 * u + 64, n % 5, q, :],
                                   start=True, stop=True)
            mm.then_inc(*mark("u_part_done", n))
            for q in range(8):
                for u in range(2):
                    h = 2 * q + u
                    pe.matmul(B6[64 * u:64 * u + 64, q * 64:(q + 1) * 64],
                              ROW[rows, 2, h * 64:(h + 1) * 64], VR[rows, tl, h * 64:(h + 1) * 64],
                              start=(q == 0), stop=False, skip_group_check=True,
                              tile_position=(r0, 64 * u))
            pe.wait_ge(*at("u_ready", n))
            for q in range(8):
                for u in range(2):
                    h = 2 * q + u
                    mm = pe.matmul(B6[64 * u:64 * u + 64, q * 64:(q + 1) * 64],
                                   ROW[rows, 1, h * 64:(h + 1) * 64], U[rows, u, q, :],
                                   start=False, stop=True, skip_group_check=True,
                                   tile_position=(r0, 64 * u))
            mm.then_inc(*mark("state_part_done", n))

        def y_pe(pe, tl):
            pe.wait_ge(*at("rb_kept", (tl, 7)))
            pe.wait_ge(*at("w2_ready", (tl, 7)))
            for u in range(2):
                for q in range(8):
                    out_ = BK[64 * u:64 * u + 64, 2 * u + q // 4, (q % 4) * P:(q % 4 + 1) * P]
                    pe.matmul(out_, U[:, u, q, :], RB[:, 2 * q + u, :], start=True, stop=False)
                    for c in range(4):
                        mm = pe.matmul(out_[:, c * CH:(c + 1) * CH],
                                       ST[64 * u:64 * u + 64, (tl * 4 + c) % 5, q, :],
                                       head(RT_, q, u, tl)[:, c * CH:(c + 1) * CH],
                                       start=False, stop=(c == 3))
                mm.then_inc(*mark("wkv_done", (tl, u)))

        def chunk_dve(dve, tl, c):
            n = tl * 4 + c
            rows = slice(CH * c, CH * c + CH)
            dve.wait_ge(*at("u_part_done", n))
            dve.wait_ge(*at("w2_ready", (tl, 7)))
            if tl:
                dve.wait_ge(*at("wkv_done", (tl - 1, 1)))
            nc.vector.tensor_tensor(U[rows, :, :, :].rearrange("p u q i -> p u (q i)"),
                                    S2[rows, :, :],
                                    W2[rows, :, :, :].rearrange("p u q i -> p u (q i)"), ALU.add).then_inc(
                *mark("u_ready", n))
            dve.wait_ge(*at("state_part_done", n))
            dve.wait_ge(*at("state_ready", n))
            new = ST[:, (n + 1) % 5, :, :]
            nc.vector.tensor_tensor(new, B6.rearrange("p (q i) -> p q i", q=8),
                                    ST[:, n % 5, :, :], ALU.add).then_inc(
                *mark("state_summed", n))
            dve.wait_ge(*at("state_summed", n))
            nc.vector.tensor_tensor(new, new, Pc[:, :, n:n + 1].broadcast_to([P, 8, HD]),
                                    ALU.mult).then_inc(*mark("state_ready", n + 1))

        def y_dve(dve, tl):
            dve.wait_ge(*at("av_ready", (tl, 7)))
            for u in range(2):
                dve.wait_ge(*at("wkv_done", (tl, u)))
                y = A[64 * u:64 * u + 64, Y0:Y0 + 8, tl * P:(tl + 1) * P]
                for g in range(2):
                    ins = nc.vector.tensor_tensor(
                        y[:, 4 * g:4 * g + 4, :],
                        BK[64 * u:64 * u + 64, 2 * u + g, :].rearrange("p (q t) -> p q t", q=4),
                        y[:, 4 * g:4 * g + 4, :], ALU.add)
                ins.then_inc(*mark("wkv_added", (tl, u)))

        def rwkv_pe(pe):
            norm_sum(pe, "l1n")
            for m, (i, name) in enumerate(MIX):
                ready = (lambda m: lambda k: [("mix_ready", (m, k))])(m)
                rhs = (lambda m: lambda k: mixbuf(m, k))(m)
                first = {"r": "r", "w": "w1", "k": "k_", "a": "a1", "v": "v_", "g": "g1"}[name]
                product(pe, first, rhs, ready)
                if name == "w":
                    product(pe, "w2", lambda k: LW[0:64, :],
                            lambda k: [("products_read_by_act", ("w1", 0))])
                if name == "a":
                    product(pe, "a2", lambda k: LB[0:64, 0, :],
                            lambda k: [("products_read_by_act", ("a1", 0))])
            for j in range(8):
                pe.wait_ge(*at("kk_square", j))
                if j >= 2:
                    pe.wait_ge(*at("kk_root", j - 2))
                pe.matmul((B6, B7)[j % 2][:, :], cc("blk"), SQ[:, j % 2, :], start=True,
                          stop=True).then_inc(*mark("kk_summed", j))
            for j in range(8):
                pe.wait_ge(*at("bonus_raw", j))
                pe.wait_ge(*at("kk_root", 7))
                if j >= 2:
                    pe.wait_ge(*at("bonus_ready", j - 2))
                pe.matmul((B6, B7)[j % 2][:, :], cc("blk"), SQ[:, j % 2, :], start=True,
                          stop=True).then_inc(*mark("bonus_summed", j))
            turn_pe(pe, 16, lambda g: [("bonus_ready", 7)], None, "v")
            for tl in range(TT):
                for n, src in enumerate((AT_, BT_, KT_)):
                    for g in range(2):
                        pe.wait_ge(*at("tilde_ready", 7))
                        if tl:
                            pe.wait_ge(*at("state_ready", 4 * tl))
                        if n:
                            pe.wait_ge(*at("rows_ready", (tl, n - 1, g)))
                        elif tl == 0:
                            pe.wait_ge(*at("rows_ready", ("v", TT - 1, g)))
                        for i in range(4):
                            mm = pe.transpose((B6, B7)[g][:, i * P:(i + 1) * P],
                                              tile(src + 4 * g + i)[:, tl * P:(tl + 1) * P], ident)
                        mm.then_inc(*mark("turned", (tl, n, g)))
                pe.wait_ge(*at("rows_ready", (tl, 2, 1)))
                pe.wait_ge(*at("rows_ready", ("v", TT - 1, 1)))
                for q0 in range(0, 8, 2):
                    for f in PAIR_PE:
                        for q in (q0, q0 + 1):
                            f(pe, tl, q)
                for c in range(4):
                    chunk_pe(pe, tl, c)
                y_pe(pe, tl)
            gn_pe(pe)
            product(pe, "w_o", arena(24), lambda k: [("products_read_by_dve", ("g2", k))])
            norm_sum(pe, "l1o")

        def turn_pe(pe, src, ready, _, key):
            for m in range(TT):
                for g in range(2):
                    for r in ready(g):
                        pe.wait_ge(*at(*r))
                    if m:
                        pe.wait_ge(*at("rows_ready", (key, m - 1, g)))
                    for i in range(4):
                        mm = pe.transpose((B6, B7)[g][:, i * P:(i + 1) * P],
                                          tile(src + 4 * g + i)[:, m * P:(m + 1) * P], ident)
                    mm.then_inc(*mark("turned", (key, m, g)))

        def rwkv_dve(dve):
            nc.vector.tensor_scalar(comp[:, 0:48], pc("mu", 0, 48), -1.0, 1.0, ALU.mult, ALU.add)
            nc.vector.memset(H[:, :, 3:4], 0.0)
            link(dve, nc.vector.tensor_scalar(comp[:, 48:56], pc("k_a", 0, 8), -1.0, 1.0, ALU.mult,
                                              ALU.add))
            nc.vector.memset(small[:, 255:256], 0.0).then_inc(*mark("complements_ready", 0))
            norm_apply(dve, "l1n", xt, hn, gain(1, 0))
            for m, (i, name) in enumerate(MIX):
                for t in range(8):
                    dve.wait_ge(*at("normed_ready", ("l1n", t)))
                    dve.wait_ge(*at("mix_started", (m, t)))
                    nc.vector.scalar_tensor_tensor(out=mixbuf(m, t), in0=H[:, t, 3:3 + T],
                                                   scalar=pc("mu", i * 8 + t), in1=mixbuf(m, t),
                                                   op0=ALU.mult, op1=ALU.add).then_inc(
                        *mark("mix_ready", (m, t)))
            dve.wait_ge(*at("products_done", ("v_", 7)))
            for j in range(8):
                dve.wait_ge(*at("products_read_by_act", ("k_", j)))
                nc.vector.tensor_scalar(tile(48 + j), tile(8 + j), pc("k_k", j), None,
                                        ALU.mult).then_inc(*mark("kk_raw", j))
            dve.wait_ge(*at("products_read_by_act", ("g1", 0)))
            dve.wait_ge(*at("loaded_conB", 0))
            for j in range(8):
                link(dve, nc.vector.tensor_scalar(RS[:, :], tile(32 + j), pc("k_a", j),
                                                  comp[:, 48 + j:49 + j], ALU.mult, ALU.add))
                nc.vector.tensor_tensor(tile(8 + j), tile(8 + j), RS[:, :], ALU.mult).then_inc(
                    *mark("k_ready", j))
                dve.wait_ge(*at("kk_root", j))
                s = TMP[:, j % 2, :]
                link(dve, nc.vector.tensor_scalar(s, s, 1e-12, None, ALU.max))
                link(dve, nc.vector.reciprocal(s, s))
                nc.vector.tensor_tensor(tile(48 + j), tile(48 + j), s, ALU.mult).then_inc(
                    *mark("kk_ready", j))
                dve.wait_ge(*at("kk_ready", j))
                nc.vector.tensor_tensor(tile(32 + j), tile(32 + j), tile(48 + j), ALU.mult).then_inc(
                    *mark("b_ready", j))
                link(dve, nc.vector.tensor_tensor_scan(tile(40 + j), cc("reset"), tile(24 + j), 0.0,
                                                       ALU.mult, ALU.add))
                nc.vector.tensor_tensor(tile(24 + j), tile(40 + j), tile(24 + j),
                                        ALU.subtract).then_inc(*mark("log_decay_ready", j))
            def bonus(j):
                dve.wait_ge(*at("bonus_summed", j))
                nc.vector.tensor_tensor(hn(j), (B6, B7)[j % 2][:, :], tile(16 + j), ALU.mult).then_inc(
                    *mark("bonus_ready", j))
            for j in range(8):
                if j >= 2:
                    dve.wait_ge(*at("bonus_summed", j - 2))
                dve.wait_ge(*at("kk_summed", 7))
                dve.wait_ge(*at("k_ready", j))
                nc.vector.scalar_tensor_tensor(out=SQ[:, j % 2, :], in0=tile(j),
                                               scalar=pc("r_k", j), in1=tile(8 + j),
                                               op0=ALU.mult, op1=ALU.mult).then_inc(
                    *mark("bonus_raw", j))
                if j:
                    bonus(j - 1)
            bonus(7)
            for j in range(8):
                dve.wait_ge(*at("b_ready", j))
                dve.wait_ge(*at("decays_ready", (j, 0)))
                nc.vector.scalar_tensor_tensor(out=tile(48 + j), in0=tile(48 + j), scalar=-1.0,
                                               in1=tile(24 + j), op0=ALU.mult, op1=ALU.mult).then_inc(
                    *mark("a_tilde", j))
                dve.wait_ge(*at("decays_ready", (j, 1)))
                nc.vector.tensor_tensor(tile(32 + j), tile(32 + j), TMP[:, j % 2, :], ALU.mult)
                nc.vector.tensor_tensor(tile(8 + j), tile(8 + j), TMP[:, j % 2, :], ALU.mult)
                dve.wait_ge(*at("chunk_decay_ready", j))
                nc.vector.tensor_tensor(tile(j), tile(j), tile(40 + j), ALU.mult).then_inc(
                    *mark("tilde_ready", j))
            dve.wait_ge(*at("turned", ("v", TT - 1, 1)))
            nc.vector.memset(ST[:, 0, :, :], 0.0).then_inc(*mark("state_ready", 0))
            for tl in range(TT):
                for q0 in range(0, 8, 2):
                    for f in PAIR_DVE:
                        for q in (q0, q0 + 1):
                            f(dve, tl, q)
                for c in range(4):
                    chunk_dve(dve, tl, c)
                y_dve(dve, tl)
            gn_dve(dve)
            norm_add(dve, "l1o", arena(40), gain(1, 1))

        def gn_pe(pe):
            for j in range(8):
                pe.wait_ge(*at("wkv_added", (TT - 1, 1)))
                if j >= 2:
                    pe.wait_ge(*at("y_centred", j - 2))
                pe.matmul((B6, B7)[j % 2][:, :], cc("blk"), tile(Y0 + j), start=True,
                          stop=True).then_inc(*mark("y_summed", j))
            for j in range(8):
                pe.wait_ge(*at("y_square", j))
                pe.wait_ge(*at("y_centred", 7))
                if j >= 2:
                    pe.wait_ge(*at("y_root", j - 2))
                pe.matmul((B6, B7)[j % 2][:, :], cc("blk"), SQ[:, j % 2, :], start=True,
                          stop=True).then_inc(*mark("y_square_summed", j))
            product(pe, "g2", lambda k: LB[:, 1, :], lambda k: [])

        def gn_act(act):
            def square(j):
                act.wait_ge(*at("y_centred", j))
                if j >= 2:
                    act.wait_ge(*at("y_square_summed", j - 2))
                else:
                    act.wait_ge(*at("wkv_added", (TT - 1, 1)))
                nc.scalar.activation(SQ[:, j % 2, :], tile(Y0 + j), ACT.Square).then_inc(
                    *mark("y_square", j))
            square(0)
            for j in range(8):
                if j < 7:
                    square(j + 1)
                act.wait_ge(*at("y_square_summed", j))
                if j >= 2:
                    act.wait_ge(*at("y_normed", j - 2))
                nc.scalar.activation(TMP[:, j % 2, :], (B6, B7)[j % 2][:, :], ACT.Sqrt,
                                     scale=1.0 / HD, bias=eps_col(GN_EPS)).then_inc(
                    *mark("y_root", j))

        def gn_dve(dve):
            for j in range(8):
                dve.wait_ge(*at("y_summed", j))
                dve.wait_ge(*at("wkv_added", (TT - 1, 1)))
                nc.vector.scalar_tensor_tensor(out=tile(Y0 + j), in0=(B6, B7)[j % 2][:, :],
                                               scalar=-1.0 / HD, in1=tile(Y0 + j),
                                               op0=ALU.mult, op1=ALU.add).then_inc(
                    *mark("y_centred", j))
            for j in range(8):
                dve.wait_ge(*at("y_root", j))
                s, y = TMP[:, j % 2, :], tile(Y0 + j)
                link(dve, nc.vector.reciprocal(s, s))
                nc.vector.scalar_tensor_tensor(out=y, in0=y, scalar=pc("gn_g", j), in1=s,
                                               op0=ALU.mult, op1=ALU.mult).then_inc(
                    *mark("y_normed", j))
                dve.wait_ge(*at("y_normed", j))
                link(dve, nc.vector.scalar_tensor_tensor(out=y, in0=y, scalar=pc("gn_b", j),
                                                         in1=hn(j), op0=ALU.add, op1=ALU.add))
            for j in range(8):
                ps = await_product(dve, "g2", j)
                nc.vector.tensor_tensor(tile(Y0 + j), ps[:, :], tile(Y0 + j), ALU.mult).then_inc(
                    *mark("products_read_by_dve", ("g2", j)))

        if "A" in phases:
            for n in ("l0n", "l0o", "a0m", "a0n", "a0x", "m0n", "m0x"):
                order.append((n, DT - 1))

        if "B" in phases:
            for n in ("l1n", "l1o", "a1_m", "a1_n", "a1_x", "m1n", "m1x"):
                order.append((n, DT - 1))
        if "C" in phases:
            order.append(("cm", DT - 1))
            order.append(("cn", DT - 1))
        if "D" in phases:
            order.append(("h2", DT - 1))

        block = ctx.enter_context(nc.Block())

        @block.sync
        def _(sp):
            load_weights(sp)
            if "D" in phases:
                experts_sp(sp)
                store_sp(sp)

        @block.gpsimd
        def _(pool):
            pool.dma_start(par[:, :], a.par).then_inc(*mark("loaded_par", 0, 16))
            pool.dma_start(con["all"][:, :], a.conall).then_inc(*mark("loaded_conall", 0, 16))
            pool.dma_start(X[:, :, :], a.xT).then_inc(*mark("loaded_x", 0, 16))
            if "A" in phases:
                pool.wait_ge(*at("products_done", ("w_out", 6)))
                pool.dma_start(half[:, 0:8, :], a.memT).then_inc(*mark("loaded_a0", 0, 16))

            if "B" in phases:
                pool.dma_start(shared[:, 0:CWIDTH["B"]], a.conB).then_inc(
                    *mark("loaded_conB", 0, 16))
                pool.wait_ge(*at("products_done", ("w_o", 6)))
                pool.dma_start(half[:, 0:8, :], a.memT).then_inc(*mark("loaded_a1_", 0, 16))

            if "C" in phases:
                if "B" in phases:
                    pool.wait_ge(*at("products_done", ("m1down", 7)))
                pool.dma_start(shared[:, 0:CWIDTH["C"]], a.conC).then_inc(
                    *mark("loaded_conC", 0, 16))
                pool.dma_start(half[:, 0:8, :], a.mem2T).then_inc(*mark("loaded_c", 0, 16))
                pos = a.positions_2.broadcast_to([P, T])
                pool.dma_start(tile(20).bitcast(I32), pos).then_inc(
                    *mark("loaded_positions", 0, 16))

            if "D" in phases:
                if "C" in phases:
                    pool.wait_ge(*at("products_read_by_dve", ("wout2", 7)))
                pool.dma_start(shared[:, 0:CWIDTH["D"]], a.conD).then_inc(
                    *mark("loaded_conD", 0, 16))
                for n, (w, c, k) in enumerate(((a.w_router_group_2, 0, 4),
                                               (a.w_router_expert_2, 4, 32))):
                    pool.dma_start(RT[:, :, c:c + k], w[0].rearrange("(k p) n -> p k n", p=P)).then_inc(
                        *mark(f"loaded_router{n}", 0, 16))
                pool.dma_start(BR[:, 0:4], a.b_router_group_2.broadcast_to([P, 4])).then_inc(
                    *mark("loaded_router_bias", 0, 16))
                pool.dma_start(BR[:, 4:36], a.b_router_expert_2.broadcast_to([P, 32])).then_inc(
                    *mark("loaded_router_bias2", 0, 16))
                scatter_pool(pool)
                gather_pool(pool)

        @block.scalar
        def _(act):
            if "D" in phases:
                act.wait_ge(*at("zeros_set", 0))
                act.dma_start(xs_dram.rearrange("(b p) n -> p b n", p=P),
                              A[:, 54:56, :].rearrange("p a t -> p (a t)")[:, None, :]
                              .broadcast_to([P, NBLK, D])).then_inc(
                    *mark("scratch_cleared", 0, 16))
            act.wait_ge(*at("constants_set", 0))
            act.wait_ge(*at("loaded_par", 0))
            act.wait_ge(*at("loaded_x", 0))
            if "A" in phases:
                lru_act(act)
                attend_act(act, 0, "a0", "l0o", 1.0 / 16, 4, 2, None, None, None)
                mlp_act(act, "m0", "a0x")
            if "B" in phases:
                rwkv_act(act, "m0x" if "A" in phases else None)
                attend_act(act, 1, "a1_", "l1o", 1.0 / 16, 4, 2, None, None, None)
                mlp_act(act, "m1", "a1_x")
            if "C" in phases:
                second_act(act, "m1x" if "B" in phases else None)
            if "D" in phases:
                route_act(act, (lambda t: [("products_read_by_dve", ("wout2", t))])
                          if "C" in phases else x_ready(None))
                experts_act(act)
            if phases[-1] == "C":
                act.wait_ge(*at("products_read_by_dve", ("wout2", 7)))
                act.dma_start(out, X[:, :, :]).then_inc(*mark("output_stored", 0, 16))
                act.wait_ge(*at("output_stored", 0))
            elif phases[-1] != "D":
                act.wait_ge(*at("residual_ready", ({"A": "m0x", "B": "m1x"}[phases[-1]], 7)))
                act.dma_start(out, X[:, :, :]).then_inc(*mark("output_stored", 0, 16))
                act.wait_ge(*at("output_stored", 0))

        @block.tensor
        def _(pe):
            pe.wait_ge(*at("loaded_conall", 0))
            if "A" in phases:
                lru_pe(pe)
                attend_pe(pe, "a0", 4, 2)
                mlp_pe(pe, "m0")
            if "B" in phases:
                rwkv_pe(pe)
                attend_pe(pe, "a1_", 4, 2)
                mlp_pe(pe, "m1")
            if "C" in phases:
                second_pe(pe)
            if "D" in phases:
                route_pe(pe)
                experts_pe(pe)

        @block.vector
        def _(dve):
            if "D" in phases:
                nc.vector.memset(A[:, 54:56, :], 0.0).then_inc(*mark("zeros_set", 0))
            for v, j in EPSC.items():
                ins = nc.vector.memset(eps_sb[:, j:j + 1], v)
            ins.then_inc(*mark("constants_set", 0))
            dve.wait_ge(*at("loaded_par", 0))
            dve.wait_ge(*at("loaded_conall", 0))
            dve.wait_ge(*at("loaded_x", 0))
            if "A" in phases:
                lru_dve(dve)
                attend_dve(dve, 0, "a0")
                mlp_dve(dve, 0, "m0")
            if "B" in phases:
                rwkv_dve(dve)
                attend_dve(dve, 1, "a1_")
                mlp_dve(dve, 1, "m1")
            if "C" in phases:
                second_dve(dve)
            if "D" in phases:
                route_dve(dve)
                experts_dve(dve)
                combine_dve(dve)

    return marked


def host_layout(inp):
    f = {n: np.asarray(v) for n, v in inp.items()}

    def cols(v):
        return np.ascontiguousarray(v).reshape(-1, P).T

    par = np.concatenate([
        cols(f["ln_gains"]), cols(f["mem_norm"]), cols(f["a_conv_w"]), cols(f["a_conv_b"]),
        cols(f["a_b_in"]), cols(f["a_gate_b"]), cols(f["a_lambda"]), cols(f["a_b_out"]),
        cols(f["b_mu"]), cols(f["b_w0"]), cols(f["b_a0"]), cols(f["b_k_k"]), cols(f["b_k_a"]),
        cols(f["b_r_k"]), cols(f["b_gn_g"]), cols(f["b_gn_b"]), cols(f["g_mix_2"]),
        cols(f["g_mem_2"]), cols(f["g_ffn_2"]), cols(np.tile(f["g_qn_attn_2"][0], 2)),
        cols(np.tile(f["g_kn_attn_2"][0], 2)), cols(f["g_qn_mem_2"]), cols(f["g_kn_mem_2"]),
        cols(f["w_conv_2"]),
    ], 1)

    def channels_first(v):
        return np.ascontiguousarray(v.reshape(-1, DT, P).transpose(2, 1, 0))

    arrays = {"par": par, **{"con" + r: v for r, v in constants().items()}, "xT": channels_first(f["x"][0]),
              "memT": channels_first(f["mem"][0]), "mem2T": channels_first(f["mem_2"][0])}
    for n in WEIGHTS:
        arrays[n] = f[n]
    return arrays


WEIGHTS = ["a_w_in", "a_gate_w", "a_w_out", "b_w_rkv", "b_w1", "b_w2", "b_a1", "b_a2", "b_g1",
           "b_g2", "b_w_o", "c_w_q", "c_w_kv", "c_w_o", "m_w_up", "m_w_down", "positions_2",
           "w_in_2", "w_mem_kv_2", "w_proj_attn_2", "w_proj_conv_2", "w_proj_mem_2", "w_out_2",
           "w_router_group_2", "b_router_group_2", "w_router_expert_2", "b_router_expert_2",
           "w_gate_2", "w_up_2", "w_down_2"]
PHASES = "ABCD"


def kernel(**inputs):
    from types import SimpleNamespace

    import concourse.bacc as bacc
    from concourse.bass_utils import run_bass_kernel_spmd

    arrays = {n: np.ascontiguousarray(v) for n, v in host_layout(inputs).items()}

    def build(known):
        nc = bacc.Bacc("TRN2", target_bir_lowering=False, num_devices=1)
        a = SimpleNamespace(**{n: nc.dram_tensor(f"in_{n}", v.shape, mybir.dt.from_np(v.dtype),
                                                 kind="ExternalInput").ap()
                               for n, v in arrays.items()})
        shape = (T, D) if PHASES[-1] == "D" else (P, DT, T)
        out = nc.dram_tensor("out_dram", shape, F32, kind="ExternalOutput").ap()
        return nc, program(nc, a, out, PHASES, known)

    _, counts = build(None)
    nc, _ = build(counts)
    r = run_bass_kernel_spmd(nc, [{f"in_{n}": v for n, v in arrays.items()}], core_ids=[0])
    got = r.results[0]["out_dram"]
    if PHASES[-1] == "D":
        return got.reshape(1, T, D)
    return got.transpose(2, 1, 0).reshape(1, T, D)
```

```python
from contextlib import ExitStack

import numpy as np

import concourse.bass as bass
from concourse import mybir

F32 = mybir.dt.float32
I32 = mybir.dt.int32
F32R = mybir.dt.float32r
U32 = mybir.dt.uint32
ALU = mybir.AluOpType
ACT = mybir.ActivationFunctionType
AX_X = mybir.AxisListType.X

P = 128
D = 1024
T = 512
DT = D // P
TT = T // P
M = 256
MT = M // P
FF = 4096
EPS = 1e-6
RING = 2
SLOT = 2048
NH = 16
HD = 64
CH = 32
GN_EPS = 64e-5
DECAY = float(np.exp(np.float32(-0.5)))
BIG = 1e30
NE = 32
NG = 4
EF = 512
NBLK = NE + (2 * T - NE) // P


def param_columns():
    cols, at = {}, 0
    for name, n in [
        ("ln", 2 * 6 * 8), ("mem_norm", 8), ("conv_w", 32), ("conv_b", 8), ("b_in", 16),
        ("gate_b", 16), ("lam", 8), ("b_out", 8), ("mu", 48), ("w0", 8), ("a0", 8), ("k_k", 8),
        ("k_a", 8), ("r_k", 8), ("gn_g", 8), ("gn_b", 8), ("g_mix", 8), ("g_mem", 8),
        ("g_ffn", 8), ("qn", 1), ("kn", 1), ("qnm", 1), ("knm", 1), ("conv2", 18),
    ]:
        cols[name] = (at, n)
        at += n
    return cols, at


PCOL, NPAR = param_columns()


def const_columns():
    cols, width = {}, {}
    for region, name, n in [
        ("all", "ident", 128), ("all", "ones", 128), ("all", "blk", 128),
        ("B", "reset", 512), ("B", "gmask", 512), ("B", "lmask", 128),
        ("C", "rot", 128), ("C", "inv", 1), ("C", "ropeon", 1), ("C", "ropeoff", 1),
        ("C", "m1", 384), ("C", "m2", 896), ("C", "m3", 512),
        ("D", "tri", 128), ("D", "tie", 32), ("D", "blkid", NBLK), ("D", "etri", 32),
    ]:
        cols[name] = (region, width.get(region, 0), n)
        width[region] = width.get(region, 0) + n
    return cols, width


CCOL, CWIDTH = const_columns()


def constants():
    c = {r: np.zeros((P, w), np.float32) for r, w in CWIDTH.items()}

    def put(name, a):
        region, at, n = CCOL[name]
        c[region][:, at:at + n] = a

    i = np.arange(P)
    put("ident", np.eye(P))
    put("ones", 1.0)
    put("blk", (i[:, None] // HD == i[None] // HD))
    put("reset", (np.arange(T) % CH != 0)[None].repeat(P, 0))
    same = i[:, None] // CH == i[None] // CH
    strict = same & (i[:, None] < i[None])
    incl = same & (i[:, None] <= i[None])
    put("gmask", np.concatenate([strict, incl, strict, incl], 1))
    put("lmask", strict.T)
    rot = np.zeros((P, P))
    for h in (0, HD):
        for d in range(8):
            rot[h + 8 + d, h + d] = -1.0
            rot[h + d, h + 8 + d] = 1.0
    put("rot", rot)
    d = i % HD
    inv = np.float32(500000.0) ** (-np.arange(0, 16, 2, dtype=np.float32) / np.float32(16))
    put("inv", np.where(d < 16, inv[d % 8], 0.0)[:, None])
    put("ropeon", (d < 16)[:, None])
    put("ropeoff", (d >= 16)[:, None])
    put("tri", i[:, None] < i[None])
    delta = np.arange(384)[None] - 128 - i[:, None]
    put("m1", np.where(np.abs(delta) <= 64, 0.0, -BIG))
    delta = np.arange(896)[None] - 384 - i[:, None]
    put("m2", np.where((np.abs(delta) <= 256) & (delta % 4 == 0), 0.0, -BIG))
    delta = np.arange(512)[None] - i[:, None]
    put("m3", np.where(delta % 16 == 0, 0.0, -BIG))
    put("tie", (64.0 - np.arange(32))[None].repeat(P, 0))
    put("blkid", np.arange(NBLK)[None].repeat(P, 0))
    put("etri", np.pad(np.arange(32)[:, None] <= np.arange(32)[None], ((0, 96), (0, 0))))
    return c


class Lin:

    def __init__(self, name, src, cols, k=D, kind="chan", evac="act", w=None, rows=TT,
                 after=None, split=False):
        self.split = split
        self.name, self.src, self.cols, self.kind, self.evac = name, src, cols, kind, evac
        self.kp = min(k, P)
        self.kt = k // self.kp
        kc = min(self.kt, 8)
        w = w or min(SLOT // kc, cols)
        self.kc, self.w = kc, w
        self.after = after
        self.chunks, self.tiles = [], 0
        for c0 in range(0, cols, w):
            ww = min(w, cols - c0)
            for kg in range(self.kt // kc):
                self.chunks.append((kg, c0, ww))
            self.tiles += -(-ww // P) if kind == "chan" else rows
        self.rows = rows

    def dram(self, kg, c0, w):
        v = self.src.rearrange("(kt p) n -> p kt n", p=self.kp)
        return v[:, kg * self.kc:(kg + 1) * self.kc, c0:c0 + w]


SHARED = {
    "rwkv_prepared_by_vector": ["kk_raw", "kk_ready", "k_ready", "b_ready", "log_decay_ready",
                                "bonus_raw", "bonus_ready", "a_tilde", "tilde_ready",
                                "complements_ready", "y_centred", "y_normed"],
    "rwkv_prepared_by_scalar": ["kk_square", "kk_root", "decays_ready", "chunk_decay_ready",
                                "y_square", "y_root"],
    "rwkv_summed": ["kk_summed", "bonus_summed", "y_summed", "y_square_summed"],
    "rwkv_pair_by_vector": ["strict_ready", "grams_masked", "start_ready", "av_ready",
                            "inverse_ready", "w2_ready"],
    "rwkv_pair_by_scalar": ["rb_kept", "powers_ready", "w1_ready"],
    "rwkv_pair_products": ["grams_done", "low_done", "level_done", "pair_done"],
    "rwkv_chunk_by_vector": ["u_ready", "state_summed", "state_ready", "wkv_added"],
    "rwkv_chunk_products": ["u_part_done", "state_part_done", "wkv_done"],
    "dilated_by_vector": ["masked", "dil_max_ready", "dil_normed", "slot_out_read"],
    "dilated_by_scalar": ["dil_exp_ready", "dil_turned_read"],
    "dilated_products": ["dil_scores_done", "dil_turned", "slot_out"],
    "heads_by_vector": ["head_normed", "residual_free", "angle_ready", "rotated_read", "roped",
                        "conv2_ready", "merged"],
    "heads_by_scalar": ["head_square", "head_root", "half_sine_ready", "sine_ready"],
    "heads_products": ["head_summed", "rotated"],
    "routing_by_vector": ["group_shifted", "margin_ready", "choices_ready",
                          "block_experts_ready", "rows_known", "token_done"],
    "routing_by_scalar": ["group_exp_ready", "margin_exp_ready"],
    "routing_products": ["router_done", "ranks_done"],
    **{f"tokens_moved{j}": [f"scattered{j}", f"gathered{j}"] for j in range(8)},
    **{f"sync_moved{j}": [f"weights_in_slot{j}", f"output_stored{j}"] for j in range(TT)},
    "parts_by_vector": ["part_source_ready", "low_part_ready"],
}
GROUP = {kind: group for group, kinds in SHARED.items() for kind in kinds}


def program(nc, a, out, phases, known):
    ctx = ExitStack()
    with ctx:
        sems, given, marked = {}, {}, {}

        def sem(name):
            name = GROUP.get(name, name)
            if name not in sems:
                sems[name] = ctx.enter_context(nc.semaphore(name))
                given[name] = 0
            return sems[name]

        def mark(name, key, by=1):
            s = sem(name)
            given[GROUP.get(name, name)] += by
            assert (name, key) not in marked, (name, key)
            marked[name, key] = given[GROUP.get(name, name)]
            return s, by

        def at(name, key):
            if known is None:
                return sem(name), 1
            v = known[name, key]
            return at(*v) if isinstance(v, tuple) else (sem(name), v)

        def sb(name, shape, dt=F32):
            return ctx.enter_context(nc.sbuf_tensor(name, shape, dt))

        def both(name, shape, pieces=1):
            with nc.sbuf_tensor(name, shape, F32) as plain:
                pass
            small_ = [shape[0], shape[1] // pieces, shape[2]]
            parts_ = [sb(f"{name}_parts{i}", small_, F32R) for i in range(pieces)]
            return plain, parts_ if pieces > 1 else parts_[0]

        X = sb("X", [P, DT, T])
        H, HP = both("H", [P, DT, T + 4])
        Wr, WP = both("Wr", [P, 4, SLOT])
        A, AP = both("A", [P, 7 * 8, T], 7)
        par = sb("par", [P, NPAR])
        con = {"all": sb("con", [P, CWIDTH["all"]])}
        shared = sb("shared_con", [P, max(CWIDTH[r] for r in "BCD")])
        for r in "BCD":
            con[r] = shared
        SC, SCP = both("SC", [P, 6, T])
        SQ = SC[:, 0:2, :]
        TMP = SC[:, 2:4, :]
        RS = SC[:, 4, :]
        LW = SC[:, 5, :]
        LB = sb("LB", [P, 2, T])
        comp = sb("comp", [P, 56])
        Pc = sb("Pc", [P, 8, T // CH])
        small = sb("small", [P, 256])
        eps_sb = sb("eps_sb", [P, 8])
        BK = ctx.enter_context(nc.psum_tensor("product_banks", [P, 4, T], F32))
        banks = [BK[:, i, :] for i in range(4)]
        wts = sb("wts", [P, 8])
        rows_of = sb("rows_of", [P, 8], I32)
        bexp = sb("bexp", [P, NBLK + 1], I32)
        if "D" in phases:
            xs_dram = nc.dram_tensor("expert_rows", (NBLK * P, D), F32, kind="Internal").ap()
            ys_dram = nc.dram_tensor("expert_outputs", (NBLK * P, D), F32, kind="Internal").ap()
        S2 = ctx.enter_context(nc.psum_tensor("score_banks", [P, 2, T], F32))
        B6 = ctx.enter_context(nc.psum_tensor("turn_bank", [P, T], F32))
        B7 = ctx.enter_context(nc.psum_tensor("stat_bank", [P, T], F32))

        flat = Wr.rearrange("p r n -> p (r n)")

        def tile(n, k=None):
            return A[:, n, :] if k is None else A[:, n:n + k, :]

        def pc(name, j=0, n=1):
            first, _ = PCOL[name]
            return par[:, first + j:first + j + n]

        def cc(name, a0=0, n=None):
            r, first, m = CCOL[name]
            return con[r][:, first + a0:first + a0 + (m if n is None else n)]

        EPSC = {EPS: 0, 1e-24: 1, GN_EPS: 2, 1.0: 3, 0.0: 4}

        def eps_col(v):
            return eps_sb[:, EPSC[v]:EPSC[v] + 1]

        def hn(k):
            return H[:, k, 4:]

        def high(n):
            return AP[n // 8][:, n % 8, :]

        def hn_parts(k):
            return HP[:, k, 4:], high(48 + k)

        def hn_parts_attn(k):
            return HP[:, k, 4:], high(40 + k)

        def parts(first_high, first_low):
            return lambda k: (high(first_high + k), high(first_low + k))

        ident, ones = cc("ident"), cc("ones")

        plan = []

        def lin(*args, **kw):
            plan.append(Lin(*args, **kw))

        def memory_plan(i, tag, after=None):
            lin(tag + "k", a.c_w_kv[i][:, 0:D], D, after=after)
            lin(tag + "v", a.c_w_kv[i][:, D:2 * D], D, kind="row", rows=MT, w=256)

        def attention_plan(i, tag):
            lin(tag + "q", a.c_w_q[i], D, split=True)
            lin(tag + "ov", None, D, kind="attn", w=D, evac="dve")
            lin(tag + "o", a.c_w_o[i], D, split=True)

        def mlp_plan(i, tag):
            for h in range(2):
                c = slice(h * FF // 2, (h + 1) * FF // 2)
                lin(f"{tag}up{h}", a.m_w_up[i][:, c], FF // 2, split=True)
                lin(f"{tag}down{h}", a.m_w_down[i][c, :], D, k=FF // 2, split=True,
                    evac=("act", "dve")[h])

        if "A" in phases:
            lin("w_in", a.a_w_in[0], 2 * D, split=True)
            lin("gates", None, 2 * D, kind="gates", w=D)
            memory_plan(0, "a0")
            lin("w_out", a.a_w_out[0], D, split=True)
            attention_plan(0, "a0")
            mlp_plan(0, "m0")

        if "B" in phases:
            lin("r", a.b_w_rkv[0, 0], D, split=True)
            lin("w1", a.b_w1[0], 64)
            lin("w2", a.b_w2[0], D, k=64)
            lin("k_", a.b_w_rkv[0, 1], D, split=True)
            lin("a1", a.b_a1[0], 64)
            lin("a2", a.b_a2[0], D, k=64)
            lin("g1", a.b_g1[0], 128)
            lin("v_", a.b_w_rkv[0, 2], D, split=True)
            memory_plan(1, "a1_", after=("wkv_done", (TT - 1, 1)))
            lin("g2", a.b_g2[0], D, k=128, evac="dve")
            lin("w_o", a.b_w_o[0], D, split=True)
            attention_plan(1, "a1_")
            mlp_plan(1, "m1")

        if "C" in phases:
            wi = a.w_in_2[0]
            lin("ck", a.w_mem_kv_2[0][:, 0:512], 512)
            lin("cv", a.w_mem_kv_2[0][:, 512:1024], 512, kind="row", rows=MT, w=256)
            lin("cq", wi[:, 4608:5120], 512)
            lin("qa", wi[:, 0:768], 768)
            lin("ka", wi[:, 768:1536], 768)
            lin("cov", None, 512, kind="attn", w=512)
            lin("va", wi[:, 1536:2304], 768, kind="row", rows=TT, w=256)
            for n, c in (("cx", 2304), ("cc", 3840), ("cb", 3072)):
                lin(n, wi[:, c:c + 768], 768, split=True)
            for b, (w, k) in enumerate(((a.w_proj_attn_2, 256), (a.w_proj_conv_2, 768),
                                        (a.w_proj_mem_2, 512))):
                lin(f"gate{b}", wi[:, 5120 + b * D:5120 + (b + 1) * D], D, split=True)
                lin(f"proj{b}", w[0], D, k=k, w=256, evac="dve")
            lin("wout2", a.w_out_2[0], D, evac="dve", split=True)

        by_name, tile0, chunk0, tiles, nchunk = {}, {}, {}, [], 0
        for L in plan:
            by_name[L.name] = L
            tile0[L.name], chunk0[L.name] = len(tiles), nchunk
            if L.kind == "gates":
                L.chunks, L.tiles = [(g, 0, 256) for g in range(2)], 16
            if L.kind == "attn":
                L.chunks, L.tiles = [], L.cols // P
            tiles += [(L.evac, (L.name, j)) for j in range(L.tiles)]
            nchunk += len(L.chunks)

        def chunk_source(L, c):
            if L.kind == "gates":
                return a.a_gate_w[0, c[0]].rearrange("h (kt p) j -> p (h kt) j", p=P)
            return L.dram(*c)

        def last_use(L, n):
            if L.kind == "gates":
                return L.name, 8 * n + 7
            if L.kind == "row":
                return L.name, (n + 1) * L.rows - 1
            kg, c0, ww = L.chunks[n]
            t = -(-(c0 + ww) // P) - 1
            return (L.name, t) if kg == L.kt // L.kc - 1 else (L.name, t, kg)

        split_uses, split_from, run_of, split0, chunk_uses, run = [], [], [], {}, [], 0
        for L in plan:
            run += bool(L.chunks) and not L.split
            split0[L.name] = len(split_uses)
            for n in range(len(L.chunks)):
                if not L.split:
                    chunk_uses.append(("products_done", last_use(L, n)))
                    continue
                kg, c0, ww = L.chunks[n]
                for j in range(ww // P):
                    t = c0 // P + j
                    split_uses.append((L.name, t) if kg == L.kt // L.kc - 1 else (L.name, t, kg))
                    split_from.append((chunk0[L.name] + n, ww, j))
                    run_of.append(run)
                chunk_uses.append(("weights_split", len(split_uses) - 1))

        def weight_parts(s):
            v = WP[:, 2 + s % 2, :].rearrange("p (a k n) -> p a k n", a=2, k=8)
            return v[:, 0], v[:, 1]

        def loaded_part(s):
            g, ww, j = split_from[s]
            raw = Wr[:, g % RING, 0:8 * ww].rearrange("p (k n) -> p k n", k=8)
            return raw[:, :, j * P:(j + 1) * P]

        highs = [0]

        def weights_high(act, upto):
            for s in range(highs[0], min(upto + 1, len(split_uses))):
                g = split_from[s][0]
                act.wait_ge(*at(f"weights_in_slot{g % RING}", g))
                if s >= 2:
                    act.wait_ge(*at("products_done", split_uses[s - 2]))
                nc.scalar.activation(weight_parts(s)[0], loaded_part(s), ACT.Copy).then_inc(
                    *mark("weights_high", s))
            highs[0] = max(highs[0], upto + 1)

        def weights_ahead(act, s):
            while s >= 0 and s + 2 < len(split_uses) and highs[0] <= s + 2 \
                    and run_of[highs[0]] == run_of[s]:
                weights_high(act, highs[0])

        def first_highs(act, name):
            weights_high(act, split0[name] + 1)

        def split_weights(pool, names):
            for s, use in enumerate(split_uses):
                if use[0] not in names:
                    continue
                hi, lo = weight_parts(s)
                pool.wait_ge(*at("weights_high", s))
                nc.gpsimd.tensor_tensor(lo, loaded_part(s), hi, ALU.subtract).then_inc(
                    *mark("weights_split", s))

        def high_part(act, key, dst, src, ready):
            for r in ready:
                act.wait_ge(*at(*r))
            nc.scalar.activation(dst, src, ACT.Copy).then_inc(*mark("high_part_ready", key))

        def low_part(dve, key, dst, src, hi):
            dve.wait_ge(*at("high_part_ready", key))
            nc.vector.tensor_tensor(dst, src, hi, ALU.subtract).then_inc(
                *mark("low_part_ready", key))

        def load_weights(sp, names=None):
            g = 0
            for L in plan:
                for n, c in enumerate(L.chunks):
                    if g >= RING:
                        sp.wait_ge(*at(*chunk_uses[g - RING]))
                    if L.after:
                        sp.wait_ge(*at(*L.after))
                    src = chunk_source(L, c)
                    kp, kk, ww = src.shape
                    dst = Wr[0:kp, g % RING, 0:kk * ww].rearrange("p (k n) -> p k n", k=kk)
                    sp.dma_start(dst, src).then_inc(*mark(f"weights_in_slot{g % RING}", g, 16))
                    g += 1

        def bank_for(pe, name, j):
            g = tile0[name] + j
            if g >= 4:
                who, key = tiles[g - 4]
                pe.wait_ge(*at("products_read_by_" + who, key))
            return banks[g % 4]

        def psum_of(name, j):
            return banks[(tile0[name] + j) % 4]

        def slot_of(pe, name, n, kk, ww):
            g = chunk0[name] + n
            pe.wait_ge(*at(f"weights_in_slot{g % RING}", g))
            return Wr[0:by_name[name].kp, g % RING, 0:kk * ww].rearrange("p (k n) -> p k n", k=kk)

        def product(pe, name, rhs, ready, width=T, then=lambda t: None):
            L = by_name[name]
            if L.split:
                return split_product(pe, L, rhs, ready, then)
            j0, last_kg = 0, L.kt // L.kc - 1
            for n, (kg, c0, ww) in enumerate(L.chunks):
                w = slot_of(pe, name, n, L.kc, ww)
                for j in range(-(-ww // P)):
                    t, m = c0 // P + j, min(P, ww - j * P)
                    bank = bank_for(pe, name, t) if kg == 0 else psum_of(name, t)
                    for k in range(L.kc):
                        kk = kg * L.kc + k
                        for r in ready(kk):
                            pe.wait_ge(*at(*r))
                        mm = pe.matmul(bank[0:m, 0:width], w[:, k, j * P:j * P + m], rhs(kk),
                                       start=(kk == 0), stop=(kk == L.kt - 1))
                    mm.then_inc(
                        *mark("products_done", (name, t) if kg == last_kg else (name, t, kg)))
                    if kg == last_kg:
                        then(t)

        def split_product(pe, L, rhs, ready, then):
            s, last_kg = split0[L.name], L.kt // L.kc - 1
            for kg, c0, ww in L.chunks:
                for j in range(ww // P):
                    hi, lo = weight_parts(s)
                    pe.wait_ge(*at("weights_split", s))
                    t = c0 // P + j
                    bank = bank_for(pe, L.name, t) if kg == 0 else psum_of(L.name, t)
                    for k in range(L.kc):
                        kk = kg * L.kc + k
                        for r in ready(kk):
                            pe.wait_ge(*at(*r))
                        x_hi, x_lo = rhs(kk)
                        pe.matmul(bank[:, :], hi[:, k, :], x_hi, start=(kk == 0), stop=False)
                        pe.matmul(bank[:, :], hi[:, k, :], x_lo, start=False, stop=False)
                        mm = pe.matmul(bank[:, :], lo[:, k, :], x_hi, start=False,
                                       stop=(kk == L.kt - 1))
                    mm.then_inc(*mark("products_done",
                                      (L.name, t) if kg == last_kg else (L.name, t, kg)))
                    if kg == last_kg:
                        then(t)
                    s += 1

        def await_product(eng, name, t):
            eng.wait_ge(*at("products_done", (name, t)))
            return psum_of(name, t)

        def take_product(act, name, t):
            if not by_name[name].split:
                return await_product(act, name, t)
            s = split_uses.index((name, t))
            weights_high(act, s)
            weights_ahead(act, s - 1)
            act.wait_ge(*at("products_done", (name, t)))
            weights_ahead(act, s)
            return psum_of(name, t)

        def product_rows(pe, name, lhs, ready, then=lambda t: None):
            L = by_name[name]
            for n, (kg, c0, ww) in enumerate(L.chunks):
                w = slot_of(pe, name, n, L.kc, ww)
                for m in range(L.rows):
                    bank = bank_for(pe, name, n * L.rows + m)
                    for k in range(L.kc):
                        for r in ready(k):
                            pe.wait_ge(*at(*r))
                        mm = pe.matmul(bank[:, 0:ww], lhs(k, m), w[:, k, :],
                                       start=(k == 0), stop=(k == L.kc - 1))
                    mm.then_inc(*mark("products_done", (name, n * L.rows + m)))
                    then(n * L.rows + m)

        def chan_ready(names):
            return lambda k: names

        norms = []

        def norm_squares(act, n, src, ready, tiles_=DT, width=T, dim=D, eps=EPS):
            for t in range(tiles_):
                norm_square(act, n, t, src(t), ready(t), width)
            norm_root(act, n, tiles_, width, dim, eps)

        def norm_square(act, n, t, src, ready, width=T):
            for r in ready:
                act.wait_ge(*at(*r))
            if t >= 2:
                act.wait_ge(*at("squares_summed", (n, t - 2)))
            elif norms_before(n):
                act.wait_ge(*at("squares_summed", norms_before(n)))
            nc.scalar.activation(SQ[:, t % 2, 0:width], src, ACT.Square).then_inc(
                *mark("squares_ready", (n, t)))

        order = []

        def norms_before(n):
            i = [x[0] for x in order].index(n)
            return order[i - 1] if i else None

        def norm_sum(pe, n, first=0, last=DT - 1, width=T):
            for t in range(first, last + 1):
                if t == 0 and norms_before(n):
                    pe.wait_ge(*at("root_ready", norms_before(n)[0]))
                pe.wait_ge(*at("squares_ready", (n, t)))
                pe.matmul(B7[:, 0:width], ones, SQ[:, t % 2, 0:width], start=(t == 0),
                          stop=(t == DT - 1)).then_inc(*mark("squares_summed", (n, t)))

        def sum_behind(pe, n, behind=1, **kw):
            return lambda t: t >= behind and norm_sum(pe, n, t - behind, t - behind, **kw)

        def norm_root(act, n, tiles_=DT, width=T, dim=D, eps=EPS):
            act.wait_ge(*at("squares_summed", (n, tiles_ - 1)))
            if norms_before(n):
                act.wait_ge(*at("norm_applied", norms_before(n)[0]))
            nc.scalar.activation(RS[:, 0:width], B7[:, 0:width], ACT.Sqrt, scale=1.0 / dim,
                                 bias=eps_col(eps)).then_inc(*mark("root_ready", n))

        def norm_rstd(dve, n, width=T):
            dve.wait_ge(*at("root_ready", n))
            nc.vector.reciprocal(RS[:, 0:width], RS[:, 0:width]).then_inc(*mark("rstd_ready", n))
            dve.wait_ge(*at("rstd_ready", n))

        def norm_apply(dve, n, src, dst, gain, tiles_=DT, width=T):
            norm_rstd(dve, n, width)
            for t in range(tiles_):
                nc.vector.scalar_tensor_tensor(out=dst(t), in0=src(t), scalar=gain(t),
                                               in1=RS[:, 0:width], op0=ALU.mult, op1=ALU.mult).then_inc(
                    *mark("normed_ready", (n, t)))
            marked["norm_applied", n] = ("normed_ready", (n, tiles_ - 1))

        def norm_parts_act(act, n):
            for t in range(DT):
                high_part(act, (n, t), HP[:, t, 4:], TMP[:, t % 2, :], [("part_source_ready", (n, t))])

        def norm_parts_dve(dve, n, src, gain, low0=48):
            norm_rstd(dve, n)
            for t in range(DT + 1):
                if 2 <= t < DT:
                    dve.wait_ge(*at("low_part_ready", (n, t - 2)))
                if t < DT:
                    nc.vector.scalar_tensor_tensor(
                        out=TMP[:, t % 2, :], in0=src(t), scalar=gain(t), in1=RS[:, :],
                        op0=ALU.mult, op1=ALU.mult).then_inc(*mark("part_source_ready", (n, t)))
                if t:
                    low_part(dve, (n, t - 1), high(low0 + t - 1), TMP[:, (t - 1) % 2, :],
                             HP[:, t - 1, 4:])
            marked["norm_applied", n] = ("part_source_ready", (n, DT - 1))

        def low_ready(n):
            return lambda k: [("low_part_ready", (n, k))]

        def norm_add(dve, n, src, gain):
            norm_rstd(dve, n)
            for t in range(DT):
                nc.vector.scalar_tensor_tensor(out=TMP[:, t % 2, :], in0=src(t), scalar=gain(t),
                                               in1=RS[:, :], op0=ALU.mult, op1=ALU.mult).then_inc(
                    *mark("branch_normed", (n, t)))
                dve.wait_ge(*at("branch_normed", (n, t)))
                nc.vector.tensor_tensor(X[:, t, :], X[:, t, :], TMP[:, t % 2, :], ALU.add).then_inc(
                    *mark("residual_ready", (n, t)))
            marked["norm_applied", n] = ("branch_normed", (n, DT - 1))

        def gain(i, j):
            return lambda t: pc("ln", (i * 6 + j) * 8 + t)

        def xt(t):
            return X[:, t, :]

        def arena(first):
            return lambda t: A[:, first + t, :]

        chain = [0]

        def link(dve, ins):
            chain[0] += 1
            ins.then_inc(sem("vector_step"), 1)
            dve.wait_ge(sem("vector_step"), chain[0])

        achain = [0]

        def alink(act, ins):
            achain[0] += 1
            ins.then_inc(sem("scalar_step"), 1)
            act.wait_ge(sem("scalar_step"), achain[0])

        def x_ready(n):
            return (lambda t: [(f"loaded_x{t // 2}", 0)]) if n is None else \
                (lambda t: [("residual_ready", (n, t))])

        def norm_order(names):
            for n in names:
                order.append(n)

        def lru_act(act):
            first_highs(act, "w_in")
            norm_squares(act, "l0n", xt, x_ready(None))
            norm_parts_act(act, "l0n")
            for j in range(16):
                ps = take_product(act, "w_in", j)
                if j < 8:
                    ins = nc.scalar.activation(tile(j), ps[:, :], ACT.Gelu_apprx_tanh,
                                               bias=pc("b_in", j))
                else:
                    ins = nc.scalar.activation(tile(j), ps[:, :], ACT.Identity,
                                               bias=pc("b_in", j))
                ins.then_inc(*mark("products_read_by_act", ("w_in", j)))
            for j in range(16):
                if j == 8:
                    memory_squares(act, "a0")
                ps = take_product(act, "gates", j)
                nc.scalar.activation(tile(24 + j), ps[:, :], ACT.Sigmoid,
                                     bias=pc("gate_b", j)).then_inc(
                    *mark("products_read_by_act", ("gates", j)))
            alink(act, nc.scalar.activation(small[:, 0:8], pc("lam", 0, 8), ACT.Exp, scale=-1.0))
            alink(act, nc.scalar.activation(small[:, 8:16], small[:, 0:8], ACT.Ln,
                                             bias=eps_col(1.0)))
            alink(act, nc.scalar.activation(small[:, 16:24], small[:, 8:16], ACT.Copy, scale=-8.0))
            for j in range(8):
                alink(act, nc.scalar.activation(tile(40 + j), tile(24 + j), ACT.Tanh,
                                                scale=small[:, 16 + j:17 + j]))
                nc.scalar.activation(tile(24 + j), tile(24 + j), ACT.Exp,
                                     scale=small[:, 16 + j:17 + j]).then_inc(
                    *mark("decay_ready", j))
            for j in range(8):
                act.wait_ge(*at("gain_squared_ready", j))
                nc.scalar.activation(tile(40 + j), tile(40 + j), ACT.Sqrt).then_inc(
                    *mark("gain_ready", j))
                take_key(act, "a0", j)
            for j in range(8):
                take_value(act, "a0", j)
                high_part(act, ("gated", j), high(j), tile(40 + j), [("gated_ready", j)])
            for j in range(8):
                ps = take_product(act, "w_out", j)
                nc.scalar.activation(tile(24 + j), ps[:, :], ACT.Identity,
                                     bias=pc("b_out", j)).then_inc(
                    *mark("products_read_by_act", ("w_out", j)))
                norm_square(act, "l0o", j, tile(24 + j), [("products_read_by_act", ("w_out", j))])
            norm_root(act, "l0o")

        def gates_pe(pe):
            for g in range(2):
                if g:
                    norm_sum(pe, "a0m", width=M)
                w = slot_of(pe, "gates", g, 8, 256)
                for h in range(4):
                    for j in range(2):
                        t = g * 8 + h * 2 + j
                        bank = bank_for(pe, "gates", t)
                        for k in range(2):
                            pe.wait_ge(*at("conv_ready", 2 * h + k))
                            mm = pe.matmul(bank[:, :], w[:, 2 * h + k, j * P:(j + 1) * P],
                                           tile(16 + 2 * h + k), start=(k == 0), stop=(k == 1))
                        mm.then_inc(*mark("products_done", ("gates", t)))

        def lru_pe(pe):
            norm_sum(pe, "l0n")
            product(pe, "w_in", hn_parts, low_ready("l0n"))
            gates_pe(pe)
            keys_pe(pe, "a0")
            values_pe(pe, "a0")
            product(pe, "w_out", parts(0, 8), low_ready("gated"), then=sum_behind(pe, "l0o"))
            norm_sum(pe, "l0o", DT - 1)

        def lru_dve(dve):
            norm_parts_dve(dve, "l0n", xt, gain(0, 0))
            for j in range(8):
                dve.wait_ge(*at("products_read_by_act", ("w_in", 8 + j)))
                u, c = tile(8 + j), tile(16 + j)
                link(dve, nc.vector.tensor_scalar(c, u, pc("conv_w", 24 + j), pc("conv_b", j),
                                                  ALU.mult, ALU.add))
                for s in (1, 2, 3):
                    ins = nc.vector.scalar_tensor_tensor(
                        out=c[:, s:T], in0=u[:, 0:T - s], scalar=pc("conv_w", (3 - s) * 8 + j),
                        in1=c[:, s:T], op0=ALU.mult, op1=ALU.add)
                    if s < 3:
                        link(dve, ins)
                    else:
                        ins.then_inc(*mark("conv_ready", j))
            memory_norm(dve, "a0")
            for j in range(8):
                dve.wait_ge(*at("decay_ready", j))
                dve.wait_ge(*at("conv_ready", j))
                th, rec = tile(40 + j), TMP[:, j % 2, :]
                link(dve, nc.vector.tensor_scalar(rec, th, -1.0, 1.0, ALU.mult, ALU.add))
                link(dve, nc.vector.reciprocal(rec, rec))
                nc.vector.scalar_tensor_tensor(out=th, in0=th, scalar=-2.0, in1=rec,
                                               op0=ALU.mult, op1=ALU.mult).then_inc(
                    *mark("gain_squared_ready", j))
            for j in range(8):
                th = tile(40 + j)
                dve.wait_ge(*at("gain_ready", j))
                link(dve, nc.vector.tensor_tensor(th, th, tile(32 + j), ALU.mult))
                link(dve, nc.vector.tensor_tensor(th, th, tile(16 + j), ALU.mult))
                link(dve, nc.vector.tensor_tensor_scan(tile(8 + j), tile(24 + j), th, 0.0,
                                                       ALU.mult, ALU.add))
                nc.vector.tensor_tensor(tile(40 + j), tile(8 + j), tile(j), ALU.mult).then_inc(
                    *mark("gated_ready", j))
                if j:
                    low_part(dve, ("gated", j - 1), high(7 + j), tile(39 + j), high(j - 1))
            low_part(dve, ("gated", 7), high(15), tile(47), high(7))
            norm_add(dve, "l0o", arena(24), gain(0, 1))

        half = A.rearrange("p n (h t) -> p (n h) t", h=2)

        def memory(tag, k):
            return {"a0": H[:, k, 4:4 + M], "a1_": half[:, 64 + k, :], "c": half[:, 88 + k, :]}[tag]

        def key_tile(tag, j):
            return half[:, (108 if tag == "c" else 96) + j, :]

        def value_rows(tag, m, c0, n):
            first = 12 if tag == "c" else 52
            v = A[:, first:first + 4, :].rearrange("p (m a) t -> p m (a t)", m=2)
            return v[:, m, c0:c0 + n]

        def memory_squares(act, tag):
            norm_squares(act, tag + "m", lambda t: memory(tag, t), lambda t: [("loaded_" + tag, 0)],
                         width=M)

        def memory_norm(dve, tag):
            norm_apply(dve, tag + "m", lambda t: memory(tag, t), lambda t: memory(tag, t),
                       lambda t: pc("g_mem" if tag == "c" else "mem_norm", t), width=M)

        def keys_pe(pe, tag):
            product(pe, tag + "k", lambda k: memory(tag, k),
                    lambda k: [("normed_ready", (tag + "m", k))], width=M)

        def values_pe(pe, tag):
            product_rows(pe, tag + "v", lambda k, m: memory(tag, k)[:, m * P:(m + 1) * P],
                         lambda k: [])

        def take_key(act, tag, j):
            ps = take_product(act, tag + "k", j)
            nc.scalar.activation(key_tile(tag, j), ps[:, 0:M], ACT.Copy).then_inc(
                *mark("products_read_by_act", (tag + "k", j)))

        def take_value(act, tag, j):
            ps = take_product(act, tag + "v", j)
            nc.scalar.activation(value_rows(tag, j % 2, (j // 2) * 256, 256), ps[:, 0:256],
                                 ACT.Copy).then_inc(*mark("products_read_by_act", (tag + "v", j)))

        def attend_act(act, i, tag, prev, scale, heads, dt, g_in, g_out, own_mem):
            norm_squares(act, tag + "n", xt, x_ready(prev))
            first_highs(act, tag + "q")
            norm_parts_act(act, tag + "n")
            for j in range(8):
                ps = take_product(act, tag + "q", j)
                nc.scalar.activation(tile(16 + j), ps[:, :], ACT.Copy).then_inc(
                    *mark("products_read_by_act", (tag + "q", j)))
                if j == 4:
                    softmax_act(act, tag, 0, scale)
            softmax_act(act, tag, 1, scale)
            for h in range(heads):
                turned_act(act, tag, h, dt)
                if h + 2 < heads:
                    softmax_act(act, tag, h + 2, scale)
            for j in range(8):
                ps = take_product(act, tag + "o", j)
                nc.scalar.activation(tile(40 + j), ps[:, :], ACT.Copy).then_inc(
                    *mark("products_read_by_act", (tag + "o", j)))
                norm_square(act, tag + "x", j, tile(40 + j),
                            [("products_read_by_act", (tag + "o", j))])
            norm_root(act, tag + "x")

        def probs(h):
            return A[:, 32 + 2 * (h % 2):34 + 2 * (h % 2), :].rearrange("p a (b m) -> p (a b) m", b=2)

        def turned(h, m):
            return A[:, 36 + 2 * (h % 2) + m, :]

        scores = S2.rearrange("p a (b m) -> p (a b) m", b=2)

        def softmax_act(act, tag, h, scale):
            act.wait_ge(*at("row_max_ready", (tag, h)))
            if h >= 2:
                act.wait_ge(*at("probs_turned", (tag, h - 2, 1)))
            for q in range(TT):
                nc.scalar.activation(probs(h)[:, q, :], scores[:, q, :], ACT.Exp,
                                     bias=small[:, 32 + 4 * (h % 2) + q:33 + 4 * (h % 2) + q],
                                     scale=scale,
                                     accum_out=small[:, 40 + 4 * (h % 2) + q:41 + 4 * (h % 2) + q]).then_inc(
                    *mark("probs_ready", (tag, h, q)))

        def turned_act(act, tag, h, dt):
            for m in range(MT):
                act.wait_ge(*at("probs_turned", (tag, h, m)))
                if h >= 2 and m == 0:
                    act.wait_ge(*at("products_done", (tag + "ov", (h - 1) * dt - 1)))
                nc.scalar.activation(turned(h, m), (B6 if m == 0 else B7)[:, :], ACT.Copy).then_inc(
                    *mark("turned_ready", (tag, h, m)))
            for d in range(dt):
                j = h * dt + d
                if dt == 2:
                    high_part(act, (tag + "ov", j), high(24 + j), psum_of(tag + "ov", j)[:, :],
                              [("products_done", (tag + "ov", j))])
                    continue
                act.wait_ge(*at("products_done", (tag + "ov", j)))
                nc.scalar.activation(tile(24 + j), psum_of(tag + "ov", j)[:, :], ACT.Copy).then_inc(
                    *mark("products_read_by_act", (tag + "ov", j)))

        def attend_pe(pe, tag, heads, dt):
            norm_sum(pe, tag + "n")
            def early_scores(t):
                if t in (2, 5):
                    scores_pe(pe, tag, t // 3, dt)

            product(pe, tag + "q", hn_parts_attn, low_ready(tag + "n"), then=early_scores)
            for h in range(heads):
                mix_pe(pe, tag, h, dt)
                if h + 2 < heads:
                    scores_pe(pe, tag, h + 2, dt)
            product(pe, tag + "o", parts(24, 0),
                    lambda k: [("products_read_by_dve", (tag + "ov", k))],
                    then=sum_behind(pe, tag + "x"))
            norm_sum(pe, tag + "x", DT - 1)

        def scores_pe(pe, tag, h, dt):
            if h:
                pe.wait_ge(*at("probs_ready", (tag, h - 1, TT - 1)))
            own = tag == "c"
            pe.wait_ge(
                *at(*(("head_normed", 3) if own else ("products_read_by_act", (tag + "k", 7)))))
            for q in range(TT):
                for d in range(dt):
                    pe.wait_ge(
                        *at(*(("head_normed", 4 + h) if own else ("products_read_by_act", (tag + "q", h * dt + d)))))
                    mm = pe.matmul(scores[:, q, :], tile(16 + h * dt + d)[:, q * P:(q + 1) * P],
                                   key_tile(tag, h * dt + d), start=(d == 0), stop=(d == dt - 1))
            mm.then_inc(*mark("scores_ready", (tag, h)))

        def mix_pe(pe, tag, h, dt):
            pe.wait_ge(*at("probs_normed", (tag, h)))
            pe.wait_ge(*at("products_read_by_act", (tag + "v", by_name[tag + "v"].tiles - 1)))
            for m in range(MT):
                if h:
                    pe.wait_ge(*at("turned_ready", (tag, h - 1, m)))
                for q in range(TT):
                    mm = pe.transpose((B6 if m == 0 else B7)[:, q * P:(q + 1) * P],
                                      probs(h)[:, q, m * P:(m + 1) * P], ident)
                mm.then_inc(*mark("probs_turned", (tag, h, m)))
            for d in range(dt):
                j = h * dt + d
                bank = bank_for(pe, tag + "ov", j)
                for m in range(MT):
                    pe.wait_ge(*at("turned_ready", (tag, h, m)))
                    mm = pe.matmul(bank[:, :], value_rows(tag, m, j * P, P), turned(h, m),
                                   start=(m == 0), stop=(m == MT - 1))
                mm.then_inc(*mark("products_done", (tag + "ov", j)))

        def softmax_dve(dve, tag, h, scale):
            m0, d0 = 32 + 4 * (h % 2), 40 + 4 * (h % 2)
            dve.wait_ge(*at("scores_ready", (tag, h)))
            link(dve, nc.vector.tensor_reduce(small[:, m0:m0 + 4], scores, AX_X, ALU.max))
            nc.vector.tensor_scalar(small[:, m0:m0 + 4], small[:, m0:m0 + 4], -scale, None,
                                    ALU.mult).then_inc(*mark("row_max_ready", (tag, h)))
            dve.wait_ge(*at("probs_ready", (tag, h, TT - 1)))
            link(dve, nc.vector.reciprocal(small[:, d0:d0 + 4], small[:, d0:d0 + 4]))
            for q in range(TT):
                ins = nc.vector.tensor_scalar(probs(h)[:, q, :], probs(h)[:, q, :],
                                              small[:, d0 + q:d0 + q + 1], None, ALU.mult)
            ins.then_inc(*mark("probs_normed", (tag, h)))

        def attend_dve(dve, i, tag):
            norm_parts_dve(dve, tag + "n", xt, gain(i, 2), low0=40)
            for h in range(6):
                if h < 4:
                    softmax_dve(dve, tag, h, 1.0 / 16)
                for j in range(2 * h - 4, 2 * h - 2) if h >= 2 else ():
                    dve.wait_ge(*at("high_part_ready", (tag + "ov", j)))
                    nc.vector.tensor_tensor(high(j), psum_of(tag + "ov", j)[:, :], high(24 + j),
                                            ALU.subtract).then_inc(
                        *mark("products_read_by_dve", (tag + "ov", j)))
            norm_add(dve, tag + "x", arena(40), gain(i, 3))

        ROPE_C1, ROPE_C2 = 6.28125, 0.0019350051879882812
        ROPE_C3 = 2 * np.pi - ROPE_C1 - ROPE_C2
        MAGIC = 12582912.0
        HNORM = [(half[:, 108 + j, :], M, "ones", P, pc("knm")) for j in range(4)] + \
                [(tile(16 + j), T, "ones", P, pc("qnm")) for j in range(4)] + \
                [(tile(j), T, "blk", HD, pc("qn")) for j in range(6)] + \
                [(tile(6 + j), T, "blk", HD, pc("kn")) for j in range(6)]
        HREADY = [("ck", j) for j in range(4)] + [("cq", j) for j in range(4)] + \
                 [("qa", j) for j in range(6)] + [("ka", j) for j in range(6)]

        def hnorm_act(act, lo, hi, between):
            def square(i):
                src, w = HNORM[i][0], HNORM[i][1]
                act.wait_ge(*at("products_read_by_act", HREADY[i]))
                if i >= lo + 2:
                    act.wait_ge(*at("head_summed", i - 2))
                elif lo == 0:
                    act.wait_ge(*at("squares_summed", ("cn", 7)))
                nc.scalar.activation(SQ[:, i % 2, 0:w], src, ACT.Square).then_inc(
                    *mark("head_square", i))
            square(lo)
            for i in range(lo, hi):
                if i + 1 < hi:
                    square(i + 1)
                between(i - lo)
                act.wait_ge(*at("head_summed", i))
                w = HNORM[i][1]
                if i >= lo + 2:
                    act.wait_ge(*at("head_normed", i - 2))
                elif lo == 0:
                    act.wait_ge(*at("residual_free", 0))
                nc.scalar.activation(TMP[:, i % 2, 0:w], (B6, B7)[i % 2][:, 0:w], ACT.Sqrt,
                                     scale=1.0 / HNORM[i][3], bias=eps_col(EPS)).then_inc(
                    *mark("head_root", i))

        def hnorm_pe(pe, lo, first, last):
            for i in range(lo + first, lo + last + 1):
                pe.wait_ge(*at("head_square", i))
                if i >= lo + 2:
                    pe.wait_ge(*at("head_root", i - 2))
                elif lo == 0:
                    pe.wait_ge(*at("root_ready", "cn"))
                else:
                    pe.wait_ge(*at("turned_ready", ("c", 3, MT - 1)))
                w = HNORM[i][1]
                pe.matmul((B6, B7)[i % 2][:, 0:w], cc(HNORM[i][2]), SQ[:, i % 2, 0:w],
                          start=True, stop=True).then_inc(*mark("head_summed", i))

        def hnorm_dve(dve, lo, hi):
            for i in range(lo, hi):
                src, w, _, _, g = HNORM[i]
                dve.wait_ge(*at("head_root", i))
                s = TMP[:, i % 2, 0:w]
                link(dve, nc.vector.reciprocal(s, s))
                nc.vector.scalar_tensor_tensor(out=src, in0=src, scalar=g, in1=s, op0=ALU.mult,
                                               op1=ALU.mult).then_inc(*mark("head_normed", i))

        def angles_dve(dve):
            dve.wait_ge(*at("loaded_conC", 0))
            dve.wait_ge(*at("loaded_positions", 0))
            dve.wait_ge(*at("head_normed", 7))
            ang, k = TMP[:, 0, :], TMP[:, 1, :]
            link(dve, nc.vector.tensor_copy(ang, tile(20).bitcast(I32)))
            link(dve, nc.vector.tensor_scalar(ang, ang, cc("inv"), None, ALU.mult))
            link(dve, nc.vector.tensor_scalar(k, ang, 1.0 / (2 * np.pi), MAGIC, ALU.mult, ALU.add))
            link(dve, nc.vector.tensor_scalar(k, k, -MAGIC, None, ALU.add))
            for c in (ROPE_C1, ROPE_C2, ROPE_C3):
                link(dve, nc.vector.scalar_tensor_tensor(out=ang, in0=k, scalar=-c, in1=ang,
                                                         op0=ALU.mult, op1=ALU.add))
            nc.vector.tensor_scalar(tile(19), ang, 3.1415925, -3.1415925, ALU.min, ALU.max).then_inc(
                *mark("angle_ready", 0))
            dve.wait_ge(*at("half_sine_ready", 0))
            link(dve, nc.vector.tensor_tensor(tile(18), tile(18), tile(18), ALU.mult))
            link(dve, nc.vector.tensor_scalar(tile(18), tile(18), -2.0, 1.0, ALU.mult, ALU.add))

        def angles_act(act):
            act.wait_ge(*at("angle_ready", 0))
            nc.scalar.activation(tile(18), tile(19), ACT.Sin, scale=0.5).then_inc(
                *mark("half_sine_ready", 0))
            nc.scalar.activation(tile(19), tile(19), ACT.Sin).then_inc(*mark("sine_ready", 0))

        def rope_pe(pe):
            for i in range(12):
                pe.wait_ge(*at("head_normed", 8 + i))
                pe.wait_ge(*at("head_root", 19))
                if i >= 2:
                    pe.wait_ge(*at("rotated_read", i - 2))
                pe.matmul((B6, B7)[i % 2][:, :], cc("rot"), tile(i), start=True, stop=True).then_inc(
                    *mark("rotated", i))

        def rope_dve(dve):
            dve.wait_ge(*at("sine_ready", 0))
            dve.wait_ge(*at("head_normed", 19))
            for i in range(12):
                dve.wait_ge(*at("rotated", i))
                nc.vector.tensor_tensor(TMP[:, i % 2, :], (B6, B7)[i % 2][:, :], tile(19),
                                        ALU.mult).then_inc(*mark("rotated_read", i))
                link(dve, nc.vector.tensor_tensor(tile(i), tile(i), tile(18), ALU.mult))
                nc.vector.tensor_tensor(tile(i), tile(i), TMP[:, i % 2, :], ALU.add).then_inc(
                    *mark("roped", i))

        UNITS = [(s, n) for s in range(4) for n in range(TT)]
        VA = A[:, 12:18, :].rearrange("p a t -> p (a t)").rearrange("p (m c) -> p m c", m=TT)

        def near(n):
            return max(0, n - 1), min(TT - 1, n + 1)

        def score_set(i):
            return [BK[:, 0, :], BK[:, 1, :], BK[:, 2, :]] if i % 2 == 0 else \
                [BK[:, 3, :], S2[:, 0, :], S2[:, 1, :]]

        def key_blocks(n):
            lo, hi = near(n)
            return [(0, m) for m in range(lo, hi + 1)] + [(g, m) for g in (1, 2) for m in range(TT)]

        def unit_scores(i, n):
            w = P * len(key_blocks(n))
            v = A[:, 34 + 3 * (i % 2):37 + 3 * (i % 2), :].rearrange("p a t -> p (a t)")
            return v[:, 0:w]

        def unit_turned(i):
            return A[:, 40 + 3 * (i % 2):43 + 3 * (i % 2), :].rearrange("p a t -> p (a t)")

        def fills(n):
            b = key_blocks(n)
            return [b[k:k + 4] for k in range(0, len(b), 4)]

        def dil_scores_pe(pe, i):
            s, n = UNITS[i]
            pe.wait_ge(*at("roped", 11))
            if i >= 2:
                pe.wait_ge(*at("slot_out_read", i - 2))
                pe.wait_ge(*at("masked", (i - 2, 2)))
            else:
                pe.wait_ge(*at("products_read_by_act", ("va", 11)))
                pe.wait_ge(*at("probs_ready", ("c", 3, TT - 1)))
            lo, hi = near(n)
            r = slice(64 * (s % 2), 64 * (s % 2) + 64)
            for g in range(3):
                k0, k1 = (lo * P, (hi + 1) * P) if g == 0 else (0, T)
                t = 2 * g + s // 2
                mm = pe.matmul(score_set(i)[g][:, 0:k1 - k0], tile(t)[r, n * P:(n + 1) * P],
                               tile(6 + t)[r, k0:k1], start=True, stop=True)
            mm.then_inc(*mark("dil_scores_done", i))

        def dil_mix_pe(pe, i):
            s, n = UNITS[i]
            pe.wait_ge(*at("dil_normed", i))
            for f, blocks in enumerate(fills(n)):
                g = 3 * i + f
                if g >= 2:
                    pe.wait_ge(*at("dil_turned_read", divmod(g - 2, 3)))
                else:
                    pe.wait_ge(*at("rotated_read", 11))
                bank = (B6, B7)[g % 2]
                for k in range(len(blocks)):
                    c = (4 * f + k) * P
                    mm = pe.transpose(bank[:, k * P:(k + 1) * P], unit_scores(i, n)[:, c:c + P],
                                      ident)
                mm.then_inc(*mark("dil_turned", (i, f)))
            out_ = score_set(i)[0][64 * (s % 2):64 * (s % 2) + 64, 0:P]
            blocks = key_blocks(n)
            for k, (g, m) in enumerate(blocks):
                pe.wait_ge(*at("dil_turned_read", (i, k // 4)))
                h = 4 * g + s
                mm = pe.matmul(out_, VA[:, m, h * HD:(h + 1) * HD],
                               unit_turned(i)[:, k * P:(k + 1) * P],
                               start=(k == 0), stop=(k == len(blocks) - 1))
            mm.then_inc(*mark("slot_out", i))

        def dil_mask_dve(dve, i):
            s, n = UNITS[i]
            dve.wait_ge(*at("dil_scores_done", i))
            if i >= 2:
                dve.wait_ge(*at("dil_turned", (i - 2, 2)))
            lo, hi = near(n)
            sc_ = unit_scores(i, n)
            w0 = (hi + 1 - lo) * P
            c0 = 64 + 8 * (i % 2)
            for g in range(3):
                a0, w = (0, w0) if g == 0 else (w0 + (g - 1) * T, T)
                mask = (cc("m1", (lo - n + 1) * P, w0), cc("m2", (3 - n) * P, T), cc("m3"))[g]
                ins = nc.vector.tensor_tensor_reduce(out=sc_[:, a0:a0 + w], in0=score_set(i)[g][:, 0:w],
                                               in1=mask, scale=1.0, scalar=-3e38, op0=ALU.add,
                                               op1=ALU.max, accum_out=small[:, c0 + g:c0 + g + 1])
                ins.then_inc(*mark("masked", (i, g)))
            dve.wait_ge(*at("masked", (i, 2)))
            link(dve, nc.vector.tensor_reduce(small[:, c0 + 3:c0 + 4], small[:, c0:c0 + 3], AX_X,
                                              ALU.max))
            nc.vector.tensor_scalar(small[:, c0 + 4:c0 + 5], small[:, c0 + 3:c0 + 4], -0.125,
                                    None, ALU.mult).then_inc(*mark("dil_max_ready", i))

        def dil_norm_dve(dve, i):
            s, n = UNITS[i]
            c0 = 64 + 8 * (i % 2)
            dve.wait_ge(*at("dil_exp_ready", i))
            link(dve, nc.vector.reciprocal(small[:, c0 + 5:c0 + 6], small[:, c0 + 5:c0 + 6]))
            nc.vector.tensor_scalar(unit_scores(i, n), unit_scores(i, n),
                                    small[:, c0 + 5:c0 + 6], None, ALU.mult).then_inc(
                *mark("dil_normed", i))

        def dil_out_dve(dve, i):
            s, n = UNITS[i]
            r = slice(64 * (s % 2), 64 * (s % 2) + 64)
            dve.wait_ge(*at("slot_out", i))
            nc.vector.tensor_copy(tile(32 + s // 2)[r, n * P:(n + 1) * P],
                                  score_set(i)[0][r, 0:P]).then_inc(*mark("slot_out_read", i))

        def dil_exp_act(act, i):
            s, n = UNITS[i]
            c0 = 64 + 8 * (i % 2)
            act.wait_ge(*at("dil_max_ready", i))
            nc.scalar.activation(unit_scores(i, n), unit_scores(i, n), ACT.Exp,
                                 bias=small[:, c0 + 4:c0 + 5], scale=0.125,
                                 accum_out=small[:, c0 + 5:c0 + 6]).then_inc(
                *mark("dil_exp_ready", i))

        def dil_turn_act(act, i):
            s, n = UNITS[i]
            for f, blocks in enumerate(fills(n)):
                g = 3 * i + f
                act.wait_ge(*at("dil_turned", (i, f)))
                if i >= 2:
                    act.wait_ge(*at("slot_out", i - 2))
                w = P * len(blocks)
                nc.scalar.activation(unit_turned(i)[:, 4 * f * P:4 * f * P + w],
                                     (B6, B7)[g % 2][:, 0:w], ACT.Copy).then_inc(
                    *mark("dil_turned_read", (i, f)))

        NU = len(UNITS)
        LOW2 = [high(n) for n in (28, 29, 30, 31, 50, 51, 52, 53)]

        def hn_parts2(k):
            return HP[:, k, 4:], LOW2[k]

        def second_act(act, prev):
            if "B" not in phases:
                memory_squares(act, "c")
            for j in range(4):
                take_key(act, "c", j)
            norm_squares(act, "cn", xt, x_ready(prev))
            for j in range(4):
                take_value(act, "c", j)
            take(act, "cq", arena(16), ACT.Copy, n=4)

            def take_qa(j):
                if j < 6:
                    ps = take_product(act, "qa", j)
                    nc.scalar.activation(tile(j), ps[:, :], ACT.Copy).then_inc(
                        *mark("products_read_by_act", ("qa", j)))

            hnorm_act(act, 0, 8, take_qa)
            take(act, "ka", arena(6), ACT.Copy, n=6)
            for h in range(4):
                softmax_act(act, "c", h, P ** -0.5)
                if h:
                    turned_act(act, "c", h - 1, 1)
            turned_act(act, "c", 3, 1)

            def take_va(j):
                ps = take_product(act, "va", j)
                nc.scalar.activation(VA[:, j % TT, (j // TT) * 256:(j // TT + 1) * 256],
                                     ps[:, 0:256], ACT.Copy).then_inc(
                    *mark("products_read_by_act", ("va", j)))
            angles_act(act)
            hnorm_act(act, 8, 20, take_va)
            for i in range(NU + 1):
                if i:
                    dil_turn_act(act, i - 1)
                if i < NU:
                    dil_exp_act(act, i)
                if i < DT:
                    high_part(act, ("normed", i), SCP[:, i % 2, :], hn(i),
                              [("normed_in_parts", i - 2)] if i >= 2 else [])
                if 1 <= i <= DT:
                    act.wait_ge(*at("low_part_ready", ("normed", i - 1)))
                    nc.scalar.activation(HP[:, i - 1, 4:], SCP[:, (i - 1) % 2, :], ACT.Copy).then_inc(
                        *mark("normed_in_parts", i - 1))
            act.wait_ge(*at("slot_out", NU - 1))
            for n, first in (("cx", 0), ("cc", 6), ("cb", 12)):
                take(act, n, arena(first), ACT.Copy, n=6)
            for b in range(3):
                for j in range(8):
                    ps = take_product(act, f"gate{b}", j)
                    if b:
                        act.wait_ge(*at("products_read_by_dve", (f"proj{b - 1}", j)))
                    nc.scalar.activation(tile(34 + j), ps[:, :], ACT.Sigmoid).then_inc(
                        *mark("products_read_by_act", (f"gate{b}", j)))
            for j in range(8):
                high_part(act, ("merged", j), high(j), tile(42 + j), [("merged", j)])
            for j in range(8):
                take_product(act, "wout2", j)

        def second_pe(pe):
            if "B" not in phases:
                norm_sum(pe, "cm", width=M)
            keys_pe(pe, "c")
            norm_sum(pe, "cn")
            values_pe(pe, "c")
            product(pe, "cq", hn, lambda k: [("normed_ready", ("cn", k))])
            pe.wait_ge(*at("loaded_conC", 0))
            product(pe, "qa", hn, lambda k: [], then=lambda t: hnorm_pe(pe, 0, t, t))
            hnorm_pe(pe, 0, 6, 7)
            product(pe, "ka", hn, lambda k: [])
            for h in range(5):
                if h < 4:
                    scores_pe(pe, "c", h, 1)
                if h:
                    mix_pe(pe, "c", h - 1, 1)
            product_rows(pe, "va", lambda k, m: hn(k)[:, m * P:(m + 1) * P], lambda k: [],
                         then=lambda t: hnorm_pe(pe, 8, t, t))
            rope_pe(pe)
            for i in range(NU + 1):
                if i < NU:
                    dil_scores_pe(pe, i)
                if i:
                    dil_mix_pe(pe, i - 1)
            pe.wait_ge(*at("slot_out_read", NU - 1))
            for n in ("cx", "cc", "cb"):
                product(pe, n, hn_parts2, lambda k: [("normed_in_parts", k)])
            branch = (arena(32), arena(18), arena(24))
            ready = (lambda k: [("slot_out_read", NU - 1)], lambda k: [("conv2_ready", k)],
                     lambda k: [("products_read_by_act", ("cov", k))])
            for b in range(3):
                product(pe, f"gate{b}", hn_parts2, lambda k: [])
                product(pe, f"proj{b}", branch[b], ready[b])
            product(pe, "wout2", parts(0, 8), low_ready("merged"))

        def second_dve(dve):
            if "B" not in phases:
                memory_norm(dve, "c")
            norm_apply(dve, "cn", xt, hn, lambda t: pc("g_mix", t))
            nc.vector.memset(small[:, 254:255], 0.0).then_inc(*mark("residual_free", 0))
            hnorm_dve(dve, 0, 8)
            for h in range(4):
                softmax_dve(dve, "c", h, P ** -0.5)
            angles_dve(dve)
            hnorm_dve(dve, 8, 20)
            rope_dve(dve)
            for i in range(NU + 1):
                if i:
                    dil_norm_dve(dve, i - 1)
                if i < NU:
                    dil_mask_dve(dve, i)
                if i:
                    dil_out_dve(dve, i - 1)
                if i < DT:
                    low_part(dve, ("normed", i), LOW2[i], hn(i), SCP[:, i % 2, :])
            for j in range(6):
                u, y = tile(j), tile(18 + j)
                for n in ("cx", "cc", "cb"):
                    dve.wait_ge(*at("products_read_by_act", (n, j)))
                link(dve, nc.vector.tensor_tensor(u, u, tile(6 + j), ALU.mult))
                link(dve, nc.vector.tensor_scalar(y, u, pc("conv2", 6 + j), None, ALU.mult))
                link(dve, nc.vector.scalar_tensor_tensor(
                    out=y[:, 1:T], in0=u[:, 0:T - 1], scalar=pc("conv2", j), in1=y[:, 1:T],
                    op0=ALU.mult, op1=ALU.add))
                link(dve, nc.vector.scalar_tensor_tensor(
                    out=y[:, 0:T - 1], in0=u[:, 1:T], scalar=pc("conv2", 12 + j), in1=y[:, 0:T - 1],
                    op0=ALU.mult, op1=ALU.add))
                nc.vector.tensor_tensor(y, y, tile(12 + j), ALU.mult).then_inc(
                    *mark("conv2_ready", j))
            for b in range(3):
                for j in range(8):
                    dve.wait_ge(*at("products_read_by_act", (f"gate{b}", j)))
                    ps = await_product(dve, f"proj{b}", j)
                    dst = tile(42 + j) if b == 0 else TMP[:, j % 2, :]
                    nc.vector.tensor_tensor(dst, ps[:, :], tile(34 + j), ALU.mult).then_inc(
                        *mark("products_read_by_dve", (f"proj{b}", j)))
                    if b:
                        dve.wait_ge(*at("products_read_by_dve", (f"proj{b}", j)))
                        ins = nc.vector.tensor_tensor(tile(42 + j), tile(42 + j), dst, ALU.add)
                        if b == 1:
                            link(dve, ins)
                        else:
                            ins.then_inc(*mark("merged", j))
                            if j:
                                low_part(dve, ("merged", j - 1), high(7 + j), tile(41 + j),
                                         high(j - 1))
            low_part(dve, ("merged", 7), high(15), tile(49), high(7))
            for j in range(8):
                ps = await_product(dve, "wout2", j)
                nc.vector.tensor_tensor(X[:, j, :], ps[:, :], X[:, j, :], ALU.add).then_inc(
                    *mark("products_read_by_dve", ("wout2", j)))

        RT = A[:, 32, 0:288].rearrange("p (k n) -> p k n", k=8)
        BR = A[:, 33, 0:36]
        r4 = lambda t, c, n: A[:, t, c:c + 4 * n].rearrange("p (m n) -> p m n", m=4)
        LG = r4(34, 0, 36)
        SHG, EXG, OG = r4(34, 144, 4), r4(34, 160, 4), r4(34, 176, 4)
        MXG, SMG = A[:, 34, 192:196], A[:, 34, 196:200]
        SEL, SEL2, O1, O2 = (r4(34, 200 + 32 * i, 8) for i in range(4))
        M1, M2, DM, EX = (A[:, 34, 328 + 4 * i:332 + 4 * i] for i in range(4))
        TIEV = r4(34, 352, 8)
        TIEM = A[:, 34, 384:388]
        PROD = A[:, 35, 0:128].rearrange("p (m g e) -> p m g e", m=4, g=4)
        OE = [A[:, 35, 128 + 128 * i:256 + 128 * i].rearrange("p (m g e) -> p m g e", m=4, g=4)
              for i in range(2)]
        OM = A[:, 35, 384:512].rearrange("p (m n) -> p m n", m=4)
        CNT, NB, BEND, BST = (A[:, 36, 32 * i:32 * i + 32] for i in range(4))
        TMPB = A[:, 36, 128:256].rearrange("p (c n) -> p c n", c=4)
        DEST = A[:, 36, 256:384].rearrange("p (m n) -> p m n", m=4)
        DSUM = A[:, 36, 384:388]
        BF_ = A[0:1, 36, 392:392 + NBLK]
        CMP = A[0:1, 37:40, :].rearrange("p a t -> p (a t)")[:, 0:NBLK * NE]\
            .rearrange("p (b e) -> p b e", b=NBLK)
        XR = A[:, 48:56, :].rearrange("p (m a) t -> p m (a t)", m=TT)
        HR = A[:, 40:48, :].rearrange("p (m a) t -> p m (a t)", m=TT)
        WG = [A[:, 24 * s:24 * s + 8, :] for s in range(2)]
        WU = [A[:, 24 * s + 8:24 * s + 16, :] for s in range(2)]
        WD = [A[:, 24 * s + 16:24 * s + 24, :].rearrange("p (k a) t -> p k (a t)", k=4)
              for s in range(2)]
        XT = [flat[:, 1024 * s:1024 * s + 1024] for s in range(2)]
        XS = [flat[:, 2048 + 1024 * s:3072 + 1024 * s] for s in range(2)]
        HROW = [flat[:, 4096 + 512 * s:4608 + 512 * s] for s in range(2)]
        HT = [flat[:, 5120 + 512 * s:5632 + 512 * s] for s in range(2)]
        YR = [flat[:, 6144 + 1024 * s:7168 + 1024 * s] for s in range(2)]

        def onehot_dve(dve, shifted, n, dst):
            v = TIEV[:, :, 0:n]
            link(dve, nc.vector.tensor_scalar(v, shifted, 0.0, None, ALU.is_equal))
            link(dve, nc.vector.tensor_tensor(
                v, v, cc("tie", 0, n)[:, None, :].broadcast_to([P, 4, n]), ALU.mult))
            link(dve, nc.vector.tensor_reduce(TIEM, v, AX_X, ALU.max))
            link(dve, nc.vector.tensor_tensor(dst, v, TIEM[:, :, None].broadcast_to([P, 4, n]),
                                              ALU.is_equal))

        def wide(v, n):
            return v[:, :, None].broadcast_to([P, 4, n])

        def route_dve(dve):
            norm_apply(dve, "h2", xt, hn, lambda t: pc("g_ffn", t))
            dve.wait_ge(*at("loaded_conD", 0))
            dve.wait_ge(*at("loaded_router_bias", 0))
            dve.wait_ge(*at("loaded_router_bias2", 0))
            dve.wait_ge(*at("router_done", 0))
            link(dve, nc.vector.tensor_tensor(
                LG, BK[:, 0, 0:144].rearrange("p (m n) -> p m n", m=4),
                BR[:, None, :].broadcast_to([P, 4, 36]), ALU.add))
            link(dve, nc.vector.tensor_reduce(MXG, LG[:, :, 0:4], AX_X, ALU.max))
            nc.vector.tensor_tensor(SHG, LG[:, :, 0:4], wide(MXG, 4), ALU.subtract).then_inc(
                *mark("group_shifted", 0))
            dve.wait_ge(*at("group_shifted", 0))
            onehot_dve(dve, SHG, 4, OG)
            link(dve, nc.vector.tensor_tensor(
                PROD, LG[:, :, 4:36].rearrange("p m (g e) -> p m g e", g=4),
                OG[:, :, :, None].broadcast_to([P, 4, 4, 8]), ALU.mult))
            link(dve, nc.vector.tensor_reduce(SEL, PROD.rearrange("p m g e -> p m e g"), AX_X,
                                              ALU.add))
            link(dve, nc.vector.tensor_reduce(M1, SEL, AX_X, ALU.max))
            link(dve, nc.vector.tensor_tensor(SEL2, SEL, wide(M1, 8), ALU.subtract))
            onehot_dve(dve, SEL2, 8, O1)
            link(dve, nc.vector.scalar_tensor_tensor(out=SEL2, in0=O1, scalar=-BIG, in1=SEL,
                                                     op0=ALU.mult, op1=ALU.add))
            link(dve, nc.vector.tensor_reduce(M2, SEL2, AX_X, ALU.max))
            nc.vector.tensor_tensor(DM, M2, M1, ALU.subtract).then_inc(*mark("margin_ready", 0))
            link(dve, nc.vector.tensor_tensor(SEL2, SEL2, wide(M2, 8), ALU.subtract))
            onehot_dve(dve, SEL2, 8, O2)
            for k, o in enumerate((O1, O2)):
                link(dve, nc.vector.tensor_tensor(
                    OE[k], OG[:, :, :, None].broadcast_to([P, 4, 4, 8]),
                    o[:, :, None, :].broadcast_to([P, 4, 4, 8]), ALU.mult))
            oe = [v.rearrange("p m g e -> p m (g e)") for v in OE]
            nc.vector.tensor_tensor(OM, oe[0], oe[1], ALU.add).then_inc(*mark("choices_ready", 0))
            dve.wait_ge(*at("margin_exp_ready", 0))
            link(dve, nc.vector.tensor_reduce(SMG, EXG, AX_X, ALU.add))
            link(dve, nc.vector.tensor_scalar(wts[:, 0:4], EX, 1.0, None, ALU.add))
            link(dve, nc.vector.tensor_tensor(wts[:, 0:4], wts[:, 0:4], SMG, ALU.mult))
            link(dve, nc.vector.reciprocal(wts[:, 0:4], wts[:, 0:4]))
            link(dve, nc.vector.tensor_tensor(wts[:, 4:8], wts[:, 0:4], EX, ALU.mult))
            dve.wait_ge(*at("ranks_done", 0))
            link(dve, nc.vector.tensor_copy(CNT, BK[:, 1, 128:160]))
            for c in range(4):
                ins = nc.vector.tensor_scalar(TMPB[:, c, :], CNT, float(P * c), None, ALU.is_gt)
            link(dve, ins)
            link(dve, nc.vector.tensor_reduce(NB, TMPB.rearrange("p c n -> p n c"), AX_X, ALU.add))
            link(dve, nc.vector.tensor_tensor_scan(BEND, ones[:, 0:32], NB, 0.0, ALU.mult, ALU.add))
            link(dve, nc.vector.tensor_tensor(BST, BEND, NB, ALU.subtract))
            link(dve, nc.vector.tensor_tensor(
                CMP, BEND[0:1, None, :].broadcast_to([1, NBLK, NE]),
                cc("blkid")[0:1, :, None].broadcast_to([1, NBLK, NE]), ALU.is_le))
            link(dve, nc.vector.tensor_reduce(BF_, CMP, AX_X, ALU.add))
            link(dve, nc.vector.tensor_scalar(BF_, BF_, float(NE - 1), None, ALU.min))
            nc.vector.tensor_copy(bexp[0:1, 0:NBLK], BF_).then_inc(
                *mark("block_experts_ready", 0))
            link(dve, nc.vector.scalar_tensor_tensor(
                out=DEST, in0=BST[:, None, :].broadcast_to([P, 4, 32]), scalar=float(P),
                in1=BK[:, 1, 0:128].rearrange("p (m n) -> p m n", m=4), op0=ALU.mult, op1=ALU.add))
            for k in range(2):
                link(dve, nc.vector.tensor_tensor(oe[k], oe[k], DEST, ALU.mult))
                link(dve, nc.vector.tensor_reduce(DSUM, oe[k], AX_X, ALU.add))
                link(dve, nc.vector.tensor_copy(rows_of[:, 4 * k:4 * k + 4], DSUM))
            nc.vector.memset(small[:, 253:254], 0.0).then_inc(*mark("rows_known", 0))

        def route_act(act, prev):
            norm_squares(act, "h2", xt, prev)
            act.wait_ge(*at("group_shifted", 0))
            nc.scalar.activation(EXG, SHG, ACT.Exp).then_inc(*mark("group_exp_ready", 0))
            act.wait_ge(*at("margin_ready", 0))
            nc.scalar.activation(EX, DM, ACT.Exp).then_inc(*mark("margin_exp_ready", 0))
            act.wait_ge(*at("scratch_cleared", PIECES - 1))
            for key, dst in (("h2", HR), ("xr", XR)):
                for m in range(TT):
                    for g in range(2):
                        act.wait_ge(*at("turned", (key, m, g)))
                        nc.scalar.activation(dst[:, m, g * 512:(g + 1) * 512],
                                             (B6, B7)[g][:, :], ACT.Copy).then_inc(
                            *mark("rows_ready", (key, m, g)))

        def turn_rows_pe(pe, src, key, ready):
            for m in range(TT):
                for g in range(2):
                    for r in ready(m, g):
                        pe.wait_ge(*at(*r))
                    for i in range(4):
                        mm = pe.transpose((B6, B7)[g][:, i * P:(i + 1) * P],
                                          src(4 * g + i)[:, m * P:(m + 1) * P], ident)
                    mm.then_inc(*mark("turned", (key, m, g)))

        def route_pe(pe):
            norm_sum(pe, "h2")
            pe.wait_ge(*at("loaded_router0", 0))
            pe.wait_ge(*at("loaded_router1", 0))
            for m in range(TT):
                for k in range(8):
                    pe.wait_ge(*at("normed_ready", ("h2", k)))
                    mm = pe.matmul(BK[:, 0, 36 * m:36 * m + 36], hn(k)[:, m * P:(m + 1) * P],
                                   RT[:, k, :], start=(k == 0), stop=(k == 7))
            mm.then_inc(*mark("router_done", 0))
            turn_rows_pe(pe, hn, "h2", lambda m, g: [("root_ready", "h2")] +
                         ([("rows_ready", ("h2", m - 1, g))] if m else []))
            turn_rows_pe(pe, xt, "xr", lambda m, g: [("rows_ready", ("xr", m - 1, g) if m else
                                                      ("h2", 3, g))])
            pe.wait_ge(*at("choices_ready", 0))
            for m in range(TT):
                for k in range(m + 1):
                    pe.matmul(BK[:, 1, 32 * m:32 * m + 32], ones if k < m else cc("tri"),
                              OM[:, k, :], start=(k == 0), stop=(k == m))
            for k in range(TT):
                mm = pe.matmul(BK[:, 1, 128:160], ones, OM[:, k, :], start=(k == 0), stop=(k == 3))
            mm.then_inc(*mark("ranks_done", 0))

        def scatter_pool(pool):
            pool.wait_ge(*at("rows_known", 0))
            pool.wait_ge(*at("rows_ready", ("h2", 3, 1)))
            pool.wait_ge(*at("scratch_cleared", PIECES - 1))
            for k in range(2):
                for m in range(TT):
                    j = 4 * k + m
                    pool.indirect_dma_start(
                    out=xs_dram, out_offset=bass.IndirectOffsetOnAxis(
                        ap=rows_of[:, j:j + 1].bitcast(U32), axis=0),
                    in_=HR[:, m, :], in_offset=None).then_inc(*mark(f"scattered{j}", 0, 16))

        if "D" in phases:
            s_x = [sem(f"block_rows_loaded{s}") for s in range(2)]
            s_g = [sem(f"block_gate_loaded{s}") for s in range(2)]
            s_u = [sem(f"block_up_loaded{s}") for s in range(2)]
            s_d = [sem(f"block_down_loaded{s}") for s in range(2)]
            s_y = [sem(f"block_stored{s}") for s in range(2)]
            s_xturned = sem("block_rows_turned")
            s_xt = sem("block_rows_ready")
            s_gate, s_up, s_down = (sem("block_" + n) for n in
                                    ("gate_done", "up_done", "down_done"))
            s_silu, s_h = sem("block_silu_ready"), sem("block_hidden_ready")
            s_hturned, s_ht = sem("block_hidden_turned"), sem("block_turned_ready")
            s_yr = sem("block_output_ready")

        def over(count):
            return count // 2 + 1

        def block_loads(sp, b, s, uses, first):
            e = sp.value_load(bexp[0:1, b:b + 1] if isinstance(b, int)
                              else bexp[0:1, bass.ds(b, 1)], min_val=0, max_val=NE - 1)
            if not first:
                sp.wait_ge(s_xturned, b - 1)
            sp.dma_start(XS[s], xs_dram[bass.ds(b * P, P), :]).then_inc(s_x[s], 16)
            if not first:
                sp.wait_ge(s_gate, b - 1)
            sp.dma_start(WG[s], a.w_gate_2[0][bass.ds(e, 1)].rearrange(
                "o (p k) n -> p (o k) n", p=P)).then_inc(s_g[s], 16)
            if not first:
                sp.wait_ge(s_up, b - 1)
            sp.dma_start(WU[s], a.w_up_2[0][bass.ds(e, 1)].rearrange(
                "o (p k) n -> p (o k) n", p=P)).then_inc(s_u[s], 16)
            if not first:
                sp.wait_ge(s_down, b - 1)
            sp.dma_start(WD[s], a.w_down_2[0][bass.ds(e, 1)].rearrange(
                "o (p k) n -> p (o k) n", p=P)).then_inc(s_d[s], 16)

        def block_turn_pe(pe, b, s, uses, first):
            pe.wait_ge(s_x[s], 16 * uses)
            if not first:
                pe.wait_ge(s_xt, 2 * b)
            for g in range(2):
                for i in range(4):
                    mm = pe.transpose((B6, B7)[g][:, i * P:(i + 1) * P],
                                      XS[s][:, 4 * g + i:D:DT], ident)
            mm.then_inc(s_xturned, 1)

        def block_up_pe(pe, b, s, uses, first):
            pe.wait_ge(s_xt, 2 * b + 2)
            pe.wait_ge(s_g[s], 16 * uses)
            if not first:
                pe.wait_ge(s_silu, b)
            for k in range(8):
                mm = pe.matmul(BK[:, 0, :], XT[s][:, k * P:(k + 1) * P], WG[s][:, k, :],
                               start=(k == 0), stop=(k == 7))
            mm.then_inc(s_gate, 1)
            pe.wait_ge(s_u[s], 16 * uses)
            if not first:
                pe.wait_ge(s_h, b)
            for k in range(8):
                mm = pe.matmul(BK[:, 1, :], XT[s][:, k * P:(k + 1) * P], WU[s][:, k, :],
                               start=(k == 0), stop=(k == 7))
            mm.then_inc(s_up, 1)

        def block_down_pe(pe, b, s, uses, first):
            pe.wait_ge(s_h, b + 1)
            if not first:
                pe.wait_ge(s_ht, b)
            for k in range(4):
                mm = pe.transpose(S2[:, 0, k * P:(k + 1) * P], HROW[s][:, k:EF:EF // P], ident)
            mm.then_inc(s_hturned, 1)
            pe.wait_ge(s_ht, b + 1)
            pe.wait_ge(s_d[s], 16 * uses)
            if not first:
                pe.wait_ge(s_yr, 2 * b)
            for n in range(2):
                for k in range(4):
                    mm = pe.matmul(BK[:, 2 + n, :], HT[s][:, k * P:(k + 1) * P],
                                   WD[s][:, k, n * T:(n + 1) * T], start=(k == 0), stop=(k == 3))
            mm.then_inc(s_down, 1)

        def block_rows_act(act, b, s):
            act.wait_ge(s_xturned, b + 1)
            for g in range(2):
                nc.scalar.activation(XT[s][:, g * T:(g + 1) * T], (B6, B7)[g][:, :], ACT.Copy)\
                    .then_inc(s_xt, 1)

        def block_silu_act(act, b, s, first):
            act.wait_ge(s_gate, b + 1)
            if not first:
                act.wait_ge(s_hturned, b - 1)
            nc.scalar.activation(HROW[s], BK[:, 0, :], ACT.Silu).then_inc(s_silu, 1)

        def block_out_act(act, b, s, uses, first):
            act.wait_ge(s_hturned, b + 1)
            nc.scalar.activation(HT[s], S2[:, 0, :], ACT.Copy).then_inc(s_ht, 1)
            act.wait_ge(s_down, b + 1)
            if not first:
                act.wait_ge(s_y[s], 16 * (uses - 1))
            for n in range(2):
                nc.scalar.activation(YR[s][:, n * T:(n + 1) * T], BK[:, 2 + n, :], ACT.Copy)\
                    .then_inc(s_yr, 1)
            act.wait_ge(s_yr, 2 * b + 2)
            act.dma_start(ys_dram[bass.ds(b * P, P), :], YR[s]).then_inc(s_y[s], 16)

        def block_hidden_dve(dve, b, s):
            dve.wait_ge(s_silu, b + 1)
            dve.wait_ge(s_up, b + 1)
            nc.vector.tensor_tensor(HROW[s], BK[:, 1, :], HROW[s], ALU.mult).then_inc(s_h, 1)

        LOOPED = (NBLK - 3) // 2

        def experts_sp(sp):
            sp.wait_ge(*at("block_experts_ready", 0))
            for j in range(8):
                sp.wait_ge(*at(f"scattered{j}", 0))
            sp.wait_ge(*at("rows_ready", ("h2", 3, 1)))
            block_loads(sp, 0, 0, 1, True)
            block_loads(sp, 1, 1, 1, True)
            with sp.Fori(0, LOOPED) as i:
                block_loads(sp, 2 * i + 2, 0, i + 2, False)
                block_loads(sp, 2 * i + 3, 1, i + 2, False)
            block_loads(sp, NBLK - 1, 0, NBLK // 2 + 1, False)

        def experts_pe(pe):
            pe.wait_ge(*at("rows_ready", ("xr", 3, 1)))
            pe.wait_ge(*at("block_experts_ready", 0))
            pe.wait_ge(*at("rows_known", 0))
            block_turn_pe(pe, 0, 0, 1, True)
            block_up_pe(pe, 0, 0, 1, True)
            block_turn_pe(pe, 1, 1, 1, False)

            def step(b, s, uses, before, first=False, last=False):
                block_up_pe(pe, b, s, uses, False)
                if not last:
                    block_turn_pe(pe, b + 1, 1 - s, before + 1, False)
                block_down_pe(pe, b - 1, 1 - s, before, first)
            step(1, 1, 1, 1, first=True)
            step(2, 0, 2, 1)
            with pe.Fori(1, LOOPED) as i:
                step(2 * i + 1, 1, i + 1, i + 1)
                step(2 * i + 2, 0, i + 2, i + 1)
            step(NBLK - 2, 1, NBLK // 2, NBLK // 2)
            step(NBLK - 1, 0, NBLK // 2 + 1, NBLK // 2, last=True)
            block_down_pe(pe, NBLK - 1, 0, NBLK // 2 + 1, False)

        def experts_act(act):
            block_rows_act(act, 0, 0)
            block_silu_act(act, 0, 0, True)
            block_rows_act(act, 1, 1)

            def step(b, s, uses, first=False, last=False):
                block_silu_act(act, b, s, first)
                if not last:
                    block_rows_act(act, b + 1, 1 - s)
                block_out_act(act, b - 1, 1 - s, uses, first)
            step(1, 1, 1, first=True)
            block_silu_act(act, 2, 0, False)
            block_rows_act(act, 3, 1)
            block_out_act(act, 1, 1, 1, True)
            with act.Fori(1, LOOPED) as i:
                step(2 * i + 1, 1, i + 1)
                step(2 * i + 2, 0, i + 1)
            step(NBLK - 2, 1, NBLK // 2)
            step(NBLK - 1, 0, NBLK // 2, last=True)
            block_out_act(act, NBLK - 1, 0, NBLK // 2 + 1, False)

        def experts_dve(dve):
            block_hidden_dve(dve, 0, 0)
            with dve.Fori(0, NBLK // 2) as i:
                block_hidden_dve(dve, 2 * i + 1, 1)
                block_hidden_dve(dve, 2 * i + 2, 0)

        def got(k, m):
            return A[:, 8 * k:8 * k + 8, :].rearrange("p (m a) t -> p m (a t)", m=TT)[:, m, :]

        def gather_pool(pool):
            pool.wait_ge(s_y[0], 16 * (NBLK // 2 + 1))
            pool.wait_ge(s_y[1], 16 * (NBLK // 2))
            for m in range(TT):
                for k in range(2):
                    j = 4 * k + m
                    pool.indirect_dma_start(
                    out=got(k, m), out_offset=None, in_=ys_dram,
                    in_offset=bass.IndirectOffsetOnAxis(ap=rows_of[:, j:j + 1].bitcast(U32),
                                                        axis=0)).then_inc(
                        *mark(f"gathered{j}", 0, 16))

        def combine_dve(dve):
            for m in range(TT):
                for k in range(2):
                    dve.wait_ge(*at(f"gathered{4 * k + m}", 0))
                    dve.wait_ge(*at("rows_ready", ("xr", 3, 1)))
                    ins = nc.vector.scalar_tensor_tensor(
                        out=XR[:, m, :], in0=got(k, m), scalar=wts[:, 4 * k + m:4 * k + m + 1],
                        in1=XR[:, m, :], op0=ALU.mult, op1=ALU.add)
                    if k == 0:
                        link(dve, ins)
                    else:
                        ins.then_inc(*mark("token_done", m))

        def store_sp(sp):
            for m in range(TT):
                sp.wait_ge(*at("token_done", m))
                sp.dma_start(out[m * P:(m + 1) * P, :], XR[:, m, :]).then_inc(
                    *mark(f"output_stored{m}", 0, 16))
            for m in range(TT):
                sp.wait_ge(*at(f"output_stored{m}", 0))

        def memory_ahead(tag):
            return tag == "m1" and "C" in phases

        def mlp_act(act, tag, prev):
            norm_squares(act, tag + "n", xt, x_ready(prev))
            norm_parts_act(act, tag + "n")
            for h in range(2):
                up = f"{tag}up{h}"
                for j in range(16):
                    z = tile(40 + j % 4)
                    ps = take_product(act, up, j)
                    if j >= 4:
                        act.wait_ge(*at("low_part_ready", (up, j - 4)))
                    nc.scalar.activation(z, ps[:, :], ACT.Relu).then_inc(
                        *mark("products_read_by_act", (up, j)))
                    act.wait_ge(*at("products_read_by_act", (up, j)))
                    alink(act, nc.scalar.activation(z, z, ACT.Square))
                    high_part(act, (up, j), high(j), z, [])
                    if tag == "m0" and "D" in phases and j % 2 and 8 * h + j // 2 < PIECES:
                        clear_scratch(act, 8 * h + j // 2)
                    if h and j >= 8 and memory_ahead(tag):
                        norm_square(act, "cm", j - 8, memory("c", j - 8), [("loaded_c", 0)], M)
                if h and memory_ahead(tag):
                    norm_root(act, "cm", width=M)
                if h == 0:
                    for j in range(8):
                        ps = take_product(act, tag + "down0", j)
                        nc.scalar.activation(tile(32 + j), ps[:, :], ACT.Copy).then_inc(
                            *mark("products_read_by_act", (tag + "down0", j)))
                else:
                    for j in range(8):
                        take_product(act, tag + "down1", j)
                        norm_square(act, tag + "x", j, tile(32 + j),
                                    [("products_read_by_dve", (tag + "down1", j))])
            norm_root(act, tag + "x")

        def mlp_pe(pe, tag):
            norm_sum(pe, tag + "n")
            for h in range(2):
                ahead = h and memory_ahead(tag)
                product(pe, f"{tag}up{h}", hn_parts, low_ready(tag + "n"),
                        then=sum_behind(pe, "cm", 9, width=M) if ahead else lambda t: None)
                if ahead:
                    norm_sum(pe, "cm", DT - 1, width=M)
                product(pe, f"{tag}down{h}", parts(0, 16), low_ready(f"{tag}up{h}"),
                        then=sum_behind(pe, tag + "x") if h else lambda t: None)
            norm_sum(pe, tag + "x", DT - 1)

        def mlp_dve(dve, i, tag):
            norm_parts_dve(dve, tag + "n", xt, gain(i, 4))
            for h in range(2):
                up, down = f"{tag}up{h}", f"{tag}down{h}"
                for j in range(16):
                    low_part(dve, (up, j), high(16 + j), tile(40 + j % 4), high(j))
                if h and memory_ahead(tag):
                    memory_norm(dve, "c")
            for j in range(8):
                ps = await_product(dve, tag + "down1", j)
                dve.wait_ge(*at("products_read_by_act", (tag + "down0", j)))
                nc.vector.tensor_tensor(tile(32 + j), ps[:, :], tile(32 + j), ALU.add).then_inc(
                    *mark("products_read_by_dve", (tag + "down1", j)))
            dve.wait_ge(*at("products_read_by_dve", (tag + "down1", 7)))
            norm_add(dve, tag + "x", arena(32), gain(i, 5))

        MIX = [(0, "r"), (1, "w"), (2, "k"), (4, "a"), (5, "g"), (3, "v")]
        LASTMM = {"r": ("r", 7), "w": ("w1", 0), "k": ("k_", 7), "a": ("a1", 0), "v": ("v_", 7),
                  "g": ("g1", 0)}
        RB = flat[:, 0:2048].rearrange("p (h t) -> p h t", h=NH)
        W1T = flat[:, 2048:3072].rearrange("p (q t) -> p q t", q=8)
        W2 = flat[:, 3072:4096].rearrange("p (u q i) -> p u q i", u=2, q=8)
        ST = flat[:, 4096:6656].rearrange("p (s q i) -> p s q i", s=5, q=8)
        scf = SC.rearrange("p a t -> p (a t)")
        NXA = [v.rearrange("p (pp u c) -> p pp u c", pp=2, u=2)
               for v in (flat[:, 6656:8192], scf[:, 1536:3072])]
        GM = [scf[:, 768 * i:768 * (i + 1)].rearrange("p (u c) -> p u c", u=2) for i in range(2)]
        AV = [LB[:, 0, 128 * i:128 * (i + 1)].rearrange("p (u c) -> p u c", u=2) for i in range(2)]
        VR = A[:, 40:48, :].rearrange("p (m a) t -> p m (a t)", m=TT)
        ROW = A[:, 16:24, :].rearrange("p (m a) t -> p m (a t)", m=4)
        U = ROW[:, 3, :].rearrange("p (u q i) -> p u q i", u=2, q=8)
        Y0 = 24
        KT_, RT_, BT_, AT_ = 8, 0, 32, 48

        def mixbuf(m, t):
            return tile((48 if m % 2 == 0 else 40) + t)

        MIX_PARTS = {0: parts(16, 48), 2: parts(16, 48),
                     5: lambda k: (HP[:, k, 4:], high(40 + k))}

        def mix_parts_act(act, m):
            for t in range(8):
                high_part(act, (("mix", m), t), MIX_PARTS[m](t)[0], mixbuf(m, t),
                          [("mix_ready", (m, t))])

        def mix_act(act, m):
            i, name = MIX[m]
            for t in range(8):
                act.wait_ge(*at("normed_ready", ("l1n", t)))
                act.wait_ge(*at("complements_ready", 0))
                if m >= 2:
                    act.wait_ge(*at("products_done", LASTMM[MIX[m - 2][1]]))
                nc.scalar.activation(mixbuf(m, t), hn(t), ACT.Copy,
                                     scale=comp[:, i * 8 + t:i * 8 + t + 1]).then_inc(
                    *mark("mix_started", (m, t)))
            if m in MIX_PARTS:
                mix_parts_act(act, m)

        PIECES = 13

        def clear_scratch(act, piece):
            n = NBLK // PIECES
            act.wait_ge(*at("zeros_set", 0))
            act.dma_start(xs_dram[piece * n * P:(piece + 1) * n * P, :]
                          .rearrange("(b p) n -> p b n", p=P),
                          LB.rearrange("p a t -> p (a t)")[:, None, :]
                          .broadcast_to([P, n, D])).then_inc(
                *mark("scratch_cleared", piece, 16))

        def take(act, name, dst, func, bias=None, n=8, rows=P):
            for j in range(n):
                ps = take_product(act, name, j)
                kw = {} if bias is None else {"bias": pc(bias, j)}
                nc.scalar.activation(dst(j), ps[0:rows, :], func, **kw).then_inc(
                    *mark("products_read_by_act", (name, j)))

        def rwkv_act(act, prev):
            norm_squares(act, "l1n", xt, x_ready(prev))
            first_highs(act, "r")
            if "D" in phases:
                act.wait_ge(*at("scratch_cleared", PIECES - 1))
            mix_act(act, 0)
            mix_act(act, 1)
            take(act, "r", arena(0), ACT.Copy)
            mix_act(act, 2)
            take(act, "w1", lambda j: LW[0:64, :], ACT.Tanh, n=1, rows=64)
            mix_act(act, 3)
            take(act, "w2", arena(24), ACT.Sigmoid, "w0")
            first_highs(act, "k_")
            take(act, "k_", arena(8), ACT.Copy)
            mix_act(act, 4)
            take(act, "a1", lambda j: LB[0:64, 0, :], ACT.Copy, n=1, rows=64)
            mix_act(act, 5)
            take(act, "a2", arena(32), ACT.Sigmoid, "a0")
            take(act, "g1", lambda j: LB[:, 1, :], ACT.Sigmoid, n=1)
            first_highs(act, "v_")
            def square(j):
                act.wait_ge(*at("kk_raw", j))
                if j >= 2:
                    act.wait_ge(*at("kk_summed", j - 2))
                nc.scalar.activation(SQ[:, j % 2, :], tile(48 + j), ACT.Square).then_inc(
                    *mark("kk_square", j))
            square(0)
            for j in range(8):
                if j < 7:
                    square(j + 1)
                ps = take_product(act, "v_", j)
                nc.scalar.activation(tile(16 + j), ps[:, :], ACT.Copy).then_inc(
                    *mark("products_read_by_act", ("v_", j)))
                act.wait_ge(*at("kk_summed", j))
                if j >= 2:
                    act.wait_ge(*at("kk_ready", j - 2))
                nc.scalar.activation(TMP[:, j % 2, :], (B6, B7)[j % 2][:, :], ACT.Sqrt).then_inc(
                    *mark("kk_root", j))
            for j in range(8):
                act.wait_ge(*at("log_decay_ready", j))
                act.wait_ge(*at("kk_ready", 7))
                if j >= 2:
                    act.wait_ge(*at("tilde_ready", j - 2))
                nc.scalar.activation(tile(24 + j), tile(24 + j), ACT.Exp, scale=-DECAY).then_inc(
                    *mark("decays_ready", (j, 0)))
                nc.scalar.activation(TMP[:, j % 2, :], tile(40 + j), ACT.Exp, scale=DECAY).then_inc(
                    *mark("decays_ready", (j, 1)))
                nc.scalar.activation(tile(40 + j), tile(40 + j), ACT.Exp, scale=-DECAY).then_inc(
                    *mark("decays_ready", (j, 2)))
                act.wait_ge(*at("decays_ready", (j, 2)))
                nc.scalar.activation(Pc[:, j, :], tile(40 + j)[:, CH - 1:T:CH], ACT.Copy).then_inc(
                    *mark("chunk_decay_ready", j))
            for m in range(TT):
                for g in range(2):
                    act.wait_ge(*at("turned", ("v", m, g)))
                    if m == 0 and g == 0:
                        act.wait_ge(*at("tilde_ready", 7))
                    nc.scalar.activation(VR[:, m, g * 512:(g + 1) * 512],
                                         (B6, B7)[g][:, :], ACT.Copy).then_inc(
                        *mark("rows_ready", ("v", m, g)))
            for tl in range(TT):
                rows_act(act, tl)
                for q0 in range(0, 8, 2):
                    for step in range(len(PAIR_ACT)):
                        for q in (q0, q0 + 1):
                            PAIR_ACT[step](act, tl, q)
            act.wait_ge(*at("w1_ready", (TT - 1, 7)))
            act.wait_ge(*at("w2_ready", (TT - 1, 7)))
            memory_squares(act, "a1_")
            gn_act(act)
            for j in range(8):
                take_value(act, "a1_", j)
            first_highs(act, "w_o")
            for j in range(8):
                high_part(act, ("y", j), high(j), tile(Y0 + j), [("products_read_by_dve", ("g2", j))])
            for j in range(8):
                ps = take_product(act, "w_o", j)
                nc.scalar.activation(tile(40 + j), ps[:, :], ACT.Copy).then_inc(
                    *mark("products_read_by_act", ("w_o", j)))
                norm_square(act, "l1o", j, tile(40 + j), [("products_read_by_act", ("w_o", j))])
            norm_root(act, "l1o")

        def rows_act(act, tl):
            for n in range(3):
                for g in range(2):
                    act.wait_ge(*at("turned", (tl, n, g)))
                    nc.scalar.activation(ROW[:, n, g * 512:(g + 1) * 512],
                                         (B6, B7)[g][:, :], ACT.Copy).then_inc(
                        *mark("rows_ready", (tl, n, g)))

        def pair_banks(q):
            return BK[:, 2 * (q % 2):2 * (q % 2) + 2, :]

        def pa_keep(act, tl, q):
            act.wait_ge(*at("grams_masked", (tl, q, 1)))
            nc.scalar.activation(RB[:, 2 * q:2 * q + 2, :], GM[q % 2][:, :, 0:128], ACT.Copy).then_inc(
                *mark("rb_kept", (tl, q)))

        def pa_level(level):
            def f(act, tl, q):
                act.wait_ge(*at("level_done", (tl, q, level)))
                dst = NXA[q % 2][:, level % 2, :, :]
                src = pair_banks(q)[:, 0, :].rearrange("p (x u c) -> p u x c", x=2, u=2)
                v = dst.rearrange("p u (x c) -> p u x c", x=3)
                if level < 4:
                    for u in range(2):
                        ins = nc.scalar.activation(v[:, u, 0:3:2, :], src[:, u, :, :], ACT.Copy)
                    ins.then_inc(*mark("powers_ready", (tl, q, level)))
                else:
                    nc.scalar.activation(v[:, :, 2, :], src[:, :, 1, :], ACT.Copy).then_inc(
                        *mark("powers_ready", (tl, q, level)))
            return f

        def pa_w1(act, tl, q):
            act.wait_ge(*at("pair_done", (tl, q)))
            nc.scalar.activation(W1T[:, q, :], pair_banks(q)[:, 0, 128:256], ACT.Copy).then_inc(
                *mark("w1_ready", (tl, q)))

        PAIR_ACT = [pa_keep, pa_level(1), pa_level(2), pa_level(3), pa_level(4), pa_w1]

        def head(n, q, u, tl):
            return tile(n + q)[64 * u:64 * u + 64, tl * P:(tl + 1) * P]

        def pp_gram(pe, tl, q):
            if q >= 2:
                pe.wait_ge(*at("w2_ready", (tl, q - 2)))
                pe.wait_ge(*at("w1_ready", (tl, q - 2)))
            elif tl:
                pe.wait_ge(*at("wkv_added", (tl - 1, 1)))
            for u in range(2):
                bank = pair_banks(q)[:, u, :]
                for j, n in enumerate((BT_, KT_)):
                    for i, r in enumerate((AT_, RT_)):
                        mm = pe.matmul(bank[:, (2 * j + i) * P:(2 * j + i + 1) * P],
                                       head(n, q, u, tl), head(r, q, u, tl),
                                       start=True, stop=True)
            mm.then_inc(*mark("grams_done", (tl, q)))

        def pp_low(pe, tl, q):
            pe.wait_ge(*at("grams_masked", (tl, q, 1)))
            for u in range(2):
                mm = pe.matmul(pair_banks(q)[:, u, 384:512], head(AT_, q, u, tl),
                               head(BT_, q, u, tl), start=True, stop=True)
            mm.then_inc(*mark("low_done", (tl, q)))

        def pp_level(level):
            def f(pe, tl, q):
                b = NXA[q % 2][:, (level - 1) % 2, :, :]
                if level == 1:
                    pe.wait_ge(*at("start_ready", (tl, q)))
                else:
                    pe.wait_ge(*at("powers_ready", (tl, q, level - 1)))
                    if level > 2:
                        pe.wait_ge(*at("inverse_ready", (tl, q, level - 1)))
                    else:
                        pe.wait_ge(*at("av_ready", (tl, q)))
                bank = pair_banks(q)
                for u in range(2):
                    N, X_, A_ = b[:, u, 0:128], b[:, u, 128:256], b[:, u, 256:384]
                    if level < 4:
                        pe.matmul(bank[:, 0, u * P:(u + 1) * P], A_, N, start=True, stop=True)
                    if level > 1:
                        pe.matmul(bank[:, 1, u * P:(u + 1) * P], A_, X_, start=True, stop=True)
                    else:
                        h = 2 * q + u
                        v = VR[:, tl, h * 64:(h + 1) * 64]
                        pe.matmul(bank[:, 1, 256 + 64 * u:320 + 64 * u], GM[q % 2][:, u, 128:256], v,
                                  start=True, stop=True)
                        pe.matmul(bank[64 * u:64 * u + 64, 1, 384:512], v,
                                  GM[q % 2][:, u, 256:384], start=True, stop=True)
                    mm = pe.matmul(bank[:, 0, 256 + u * P:256 + (u + 1) * P], N, A_,
                                   start=True, stop=True)
                mm.then_inc(*mark("level_done", (tl, q, level)))
            return f

        def pp_last(pe, tl, q):
            pe.wait_ge(*at("powers_ready", (tl, q, 4)))
            pe.wait_ge(*at("inverse_ready", (tl, q, 4)))
            b = NXA[q % 2][:, 0, :, :]
            for u in range(2):
                mm = pe.matmul(pair_banks(q)[:, 1, u * P:(u + 1) * P], b[:, u, 256:384],
                               b[:, u, 128:256],
                               start=True, stop=True)
            mm.then_inc(*mark("level_done", (tl, q, 5)))

        def pp_end(pe, tl, q):
            pe.wait_ge(*at("inverse_ready", (tl, q, 5)))
            for u in range(2):
                h = 2 * q + u
                X_ = NXA[q % 2][:, 1, u, 128:256]
                pe.matmul(pair_banks(q)[:, 1, u * 64:(u + 1) * 64], X_, AV[q % 2][:, u, :], start=True, stop=True)
                mm = pe.matmul(pair_banks(q)[64 * u:64 * u + 64, 0, 128:256],
                               ROW[:, 0, h * 64:(h + 1) * 64], X_, start=True, stop=True)
            mm.then_inc(*mark("pair_done", (tl, q)))

        PAIR_PE = [pp_gram, pp_low, pp_level(1), pp_level(2), pp_level(3), pp_level(4), pp_last,
                   pp_end]

        def pd_mask(dve, tl, q):
            dve.wait_ge(*at("grams_done", (tl, q)))
            src = pair_banks(q)
            for u in range(2):
                nc.vector.tensor_tensor(NXA[q % 2][:, 0, u, 0:128], src[:, u, 0:128],
                                        cc("gmask", 0, 128), ALU.mult).then_inc(
                    *mark("strict_ready", (tl, q, u)))
                if u == 0 and tl + q >= 2 or tl:
                    who = (tl, q - 2) if q >= 2 else (tl - 1, q + 6)
                    if who[0] >= 0:
                        dve.wait_ge(*at("rb_kept", who))
                nc.vector.tensor_tensor(GM[q % 2][:, u, :], src[:, u, 128:512],
                                        cc("gmask", 128, 384), ALU.mult).then_inc(
                    *mark("grams_masked", (tl, q, u)))

        def pd_low(dve, tl, q):
            dve.wait_ge(*at("low_done", (tl, q)))
            dve.wait_ge(*at("strict_ready", (tl, q, 1)))
            for u in range(2):
                nc.vector.tensor_tensor(NXA[q % 2][:, 1, u, 128:256], NXA[q % 2][:, 0, u, 0:128],
                                        ident, ALU.add)
                ins = nc.vector.tensor_tensor(NXA[q % 2][:, 0, u, 256:384],
                                              pair_banks(q)[:, u, 384:512], cc("lmask"), ALU.mult)
            ins.then_inc(*mark("start_ready", (tl, q)))

        def pd_av(dve, tl, q):
            dve.wait_ge(*at("level_done", (tl, q, 1)))
            nc.vector.tensor_copy(tile(Y0 + q)[:, tl * P:(tl + 1) * P],
                                  pair_banks(q)[:, 1, 384:512])
            nc.vector.tensor_copy(AV[q % 2].rearrange("p u c -> p (u c)"),
                                  pair_banks(q)[:, 1, 256:384]).then_inc(
                *mark("av_ready", (tl, q)))

        def pd_level(level):
            def f(dve, tl, q):
                dve.wait_ge(*at("level_done", (tl, q, level)))
                if level > 2:
                    dve.wait_ge(*at("inverse_ready", (tl, q, level - 1)))
                else:
                    dve.wait_ge(*at("start_ready", (tl, q)))
                old, new = NXA[q % 2][:, (level - 1) % 2], NXA[q % 2][:, level % 2]
                nc.vector.tensor_tensor(new[:, :, 128:256], 
                                        pair_banks(q)[:, 1, 0:256].rearrange(
                                            "p (u c) -> p u c", u=2),
                                        old[:, :, 128:256], ALU.add).then_inc(
                    *mark("inverse_ready", (tl, q, level)))
            return f

        def pd_w2(dve, tl, q):
            dve.wait_ge(*at("pair_done", (tl, q)))
            nc.vector.tensor_copy(W2[:, :, q, :], pair_banks(q)[:, 1, 0:128].rearrange(
            "p (u c) -> p u c", u=2)).then_inc(*mark("w2_ready", (tl, q)))

        PAIR_DVE = [pd_mask, pd_low, pd_av, pd_level(2), pd_level(3), pd_level(4), pd_level(5),
                    pd_w2]

        def chunk_pe(pe, tl, c):
            n = tl * 4 + c
            r0 = CH * c
            rows = slice(r0, r0 + CH)
            pe.wait_ge(*at("w1_ready", (tl, 7)))
            pe.wait_ge(*at("state_ready", n))
            if c:
                pe.wait_ge(*at("u_ready", n - 1))
            for q in range(8):
                for u in range(2):
                    mm = pe.matmul(S2[rows, u, q * 64:(q + 1) * 64],
                                   W1T[64 * u:64 * u + 64, q, rows], ST[64 * u:64 * u + 64, n % 5, q, :],
                                   start=True, stop=True)
            mm.then_inc(*mark("u_part_done", n))
            for q in range(8):
                for u in range(2):
                    h = 2 * q + u
                    pe.matmul(B6[64 * u:64 * u + 64, q * 64:(q + 1) * 64],
                              ROW[rows, 2, h * 64:(h + 1) * 64], VR[rows, tl, h * 64:(h + 1) * 64],
                              start=(q == 0), stop=False, skip_group_check=True,
                              tile_position=(r0, 64 * u))
            pe.wait_ge(*at("u_ready", n))
            for q in range(8):
                for u in range(2):
                    h = 2 * q + u
                    mm = pe.matmul(B6[64 * u:64 * u + 64, q * 64:(q + 1) * 64],
                                   ROW[rows, 1, h * 64:(h + 1) * 64], U[rows, u, q, :],
                                   start=False, stop=True, skip_group_check=True,
                                   tile_position=(r0, 64 * u))
            mm.then_inc(*mark("state_part_done", n))

        def y_pe(pe, tl):
            pe.wait_ge(*at("rb_kept", (tl, 7)))
            pe.wait_ge(*at("w2_ready", (tl, 7)))
            for u in range(2):
                for q in range(8):
                    out_ = BK[64 * u:64 * u + 64, 2 * u + q // 4, (q % 4) * P:(q % 4 + 1) * P]
                    pe.matmul(out_, U[:, u, q, :], RB[:, 2 * q + u, :], start=True, stop=False)
                    for c in range(4):
                        mm = pe.matmul(out_[:, c * CH:(c + 1) * CH],
                                       ST[64 * u:64 * u + 64, (tl * 4 + c) % 5, q, :],
                                       head(RT_, q, u, tl)[:, c * CH:(c + 1) * CH],
                                       start=False, stop=(c == 3))
                mm.then_inc(*mark("wkv_done", (tl, u)))

        def chunk_dve(dve, tl, c):
            n = tl * 4 + c
            rows = slice(CH * c, CH * c + CH)
            dve.wait_ge(*at("u_part_done", n))
            dve.wait_ge(*at("w2_ready", (tl, 7)))
            if tl:
                dve.wait_ge(*at("wkv_done", (tl - 1, 1)))
            nc.vector.tensor_tensor(U[rows, :, :, :].rearrange("p u q i -> p u (q i)"),
                                    S2[rows, :, :],
                                    W2[rows, :, :, :].rearrange("p u q i -> p u (q i)"), ALU.add).then_inc(
                *mark("u_ready", n))
            dve.wait_ge(*at("state_part_done", n))
            dve.wait_ge(*at("state_ready", n))
            new = ST[:, (n + 1) % 5, :, :]
            nc.vector.tensor_tensor(new, B6.rearrange("p (q i) -> p q i", q=8),
                                    ST[:, n % 5, :, :], ALU.add).then_inc(
                *mark("state_summed", n))
            dve.wait_ge(*at("state_summed", n))
            nc.vector.tensor_tensor(new, new, Pc[:, :, n:n + 1].broadcast_to([P, 8, HD]),
                                    ALU.mult).then_inc(*mark("state_ready", n + 1))

        def y_dve(dve, tl):
            dve.wait_ge(*at("av_ready", (tl, 7)))
            for u in range(2):
                dve.wait_ge(*at("wkv_done", (tl, u)))
                y = A[64 * u:64 * u + 64, Y0:Y0 + 8, tl * P:(tl + 1) * P]
                for g in range(2):
                    ins = nc.vector.tensor_tensor(
                        y[:, 4 * g:4 * g + 4, :],
                        BK[64 * u:64 * u + 64, 2 * u + g, :].rearrange("p (q t) -> p q t", q=4),
                        y[:, 4 * g:4 * g + 4, :], ALU.add)
                ins.then_inc(*mark("wkv_added", (tl, u)))

        def rwkv_pe(pe):
            def kk_sum(j):
                pe.wait_ge(*at("kk_square", j))
                if j >= 2:
                    pe.wait_ge(*at("kk_root", j - 2))
                pe.matmul((B6, B7)[j % 2][:, :], cc("blk"), SQ[:, j % 2, :], start=True,
                          stop=True).then_inc(*mark("kk_summed", j))

            norm_sum(pe, "l1n")
            for m, (i, name) in enumerate(MIX):
                ready = (lambda m: lambda k: [("mix_ready", (m, k))])(m)
                rhs = (lambda m: lambda k: mixbuf(m, k))(m)
                if m in MIX_PARTS:
                    ready, rhs = low_ready(("mix", m)), MIX_PARTS[m]
                first = {"r": "r", "w": "w1", "k": "k_", "a": "a1", "v": "v_", "g": "g1"}[name]
                product(pe, first, rhs, ready, then=kk_sum if name == "v" else lambda t: None)
                if name == "w":
                    product(pe, "w2", lambda k: LW[0:64, :],
                            lambda k: [("products_read_by_act", ("w1", 0))])
                if name == "a":
                    product(pe, "a2", lambda k: LB[0:64, 0, :],
                            lambda k: [("products_read_by_act", ("a1", 0))])
            for j in range(8):
                pe.wait_ge(*at("bonus_raw", j))
                pe.wait_ge(*at("kk_root", 7))
                if j >= 2:
                    pe.wait_ge(*at("bonus_ready", j - 2))
                pe.matmul((B6, B7)[j % 2][:, :], cc("blk"), SQ[:, j % 2, :], start=True,
                          stop=True).then_inc(*mark("bonus_summed", j))
            turn_pe(pe, 16, lambda g: [("bonus_ready", 7)], None, "v")
            for tl in range(TT):
                for n, src in enumerate((AT_, BT_, KT_)):
                    for g in range(2):
                        pe.wait_ge(*at("tilde_ready", 7))
                        if tl:
                            pe.wait_ge(*at("state_ready", 4 * tl))
                        if n:
                            pe.wait_ge(*at("rows_ready", (tl, n - 1, g)))
                        elif tl == 0:
                            pe.wait_ge(*at("rows_ready", ("v", TT - 1, g)))
                        for i in range(4):
                            mm = pe.transpose((B6, B7)[g][:, i * P:(i + 1) * P],
                                              tile(src + 4 * g + i)[:, tl * P:(tl + 1) * P], ident)
                        mm.then_inc(*mark("turned", (tl, n, g)))
                pe.wait_ge(*at("rows_ready", (tl, 2, 1)))
                pe.wait_ge(*at("rows_ready", ("v", TT - 1, 1)))
                for q0 in range(0, 8, 2):
                    for f in PAIR_PE:
                        for q in (q0, q0 + 1):
                            f(pe, tl, q)
                for c in range(4):
                    chunk_pe(pe, tl, c)
                    if tl == TT - 1:
                        norm_sum(pe, "a1_m", 2 * c, 2 * c + 1, width=M)
                y_pe(pe, tl)
            gn_pe(pe)
            product(pe, "w_o", parts(0, 8), low_ready("y"), then=sum_behind(pe, "l1o"))
            norm_sum(pe, "l1o", DT - 1)

        def turn_pe(pe, src, ready, _, key):
            for m in range(TT):
                for g in range(2):
                    for r in ready(g):
                        pe.wait_ge(*at(*r))
                    if m:
                        pe.wait_ge(*at("rows_ready", (key, m - 1, g)))
                    for i in range(4):
                        mm = pe.transpose((B6, B7)[g][:, i * P:(i + 1) * P],
                                          tile(src + 4 * g + i)[:, m * P:(m + 1) * P], ident)
                    mm.then_inc(*mark("turned", (key, m, g)))

        def rwkv_dve(dve):
            nc.vector.tensor_scalar(comp[:, 0:48], pc("mu", 0, 48), -1.0, 1.0, ALU.mult, ALU.add)
            nc.vector.memset(H[:, :, 3:4], 0.0)
            link(dve, nc.vector.tensor_scalar(comp[:, 48:56], pc("k_a", 0, 8), -1.0, 1.0, ALU.mult,
                                              ALU.add))
            nc.vector.memset(small[:, 255:256], 0.0).then_inc(*mark("complements_ready", 0))
            norm_apply(dve, "l1n", xt, hn, gain(1, 0))
            for m, (i, name) in enumerate(MIX):
                for t in range(8):
                    dve.wait_ge(*at("normed_ready", ("l1n", t)))
                    dve.wait_ge(*at("mix_started", (m, t)))
                    nc.vector.scalar_tensor_tensor(out=mixbuf(m, t), in0=H[:, t, 3:3 + T],
                                                   scalar=pc("mu", i * 8 + t), in1=mixbuf(m, t),
                                                   op0=ALU.mult, op1=ALU.add).then_inc(
                        *mark("mix_ready", (m, t)))
                for t in range(8) if m in MIX_PARTS else ():
                    hi, lo = MIX_PARTS[m](t)
                    low_part(dve, (("mix", m), t), lo, mixbuf(m, t), hi)
            dve.wait_ge(*at("products_done", ("g1", 0)))
            dve.wait_ge(*at("loaded_conB", 0))
            for j in range(8):
                dve.wait_ge(*at("products_read_by_act", ("k_", j)))
                nc.vector.tensor_scalar(tile(48 + j), tile(8 + j), pc("k_k", j), None,
                                        ALU.mult).then_inc(*mark("kk_raw", j))
            dve.wait_ge(*at("products_read_by_act", ("g1", 0)))
            for j in range(8):
                link(dve, nc.vector.tensor_scalar(RS[:, :], tile(32 + j), pc("k_a", j),
                                                  comp[:, 48 + j:49 + j], ALU.mult, ALU.add))
                nc.vector.tensor_tensor(tile(8 + j), tile(8 + j), RS[:, :], ALU.mult).then_inc(
                    *mark("k_ready", j))
                dve.wait_ge(*at("kk_root", j))
                s = TMP[:, j % 2, :]
                link(dve, nc.vector.tensor_scalar(s, s, 1e-12, None, ALU.max))
                link(dve, nc.vector.reciprocal(s, s))
                nc.vector.tensor_tensor(tile(48 + j), tile(48 + j), s, ALU.mult).then_inc(
                    *mark("kk_ready", j))
                dve.wait_ge(*at("kk_ready", j))
                nc.vector.tensor_tensor(tile(32 + j), tile(32 + j), tile(48 + j), ALU.mult).then_inc(
                    *mark("b_ready", j))
            dve.wait_ge(*at("products_read_by_act", ("v_", 7)))
            for j in range(8):
                link(dve, nc.vector.tensor_tensor_scan(tile(40 + j), cc("reset"), tile(24 + j), 0.0,
                                                       ALU.mult, ALU.add))
                nc.vector.tensor_tensor(tile(24 + j), tile(40 + j), tile(24 + j),
                                        ALU.subtract).then_inc(*mark("log_decay_ready", j))
            def bonus(j):
                dve.wait_ge(*at("bonus_summed", j))
                nc.vector.tensor_tensor(hn(j), (B6, B7)[j % 2][:, :], tile(16 + j), ALU.mult).then_inc(
                    *mark("bonus_ready", j))
            for j in range(8):
                if j >= 2:
                    dve.wait_ge(*at("bonus_summed", j - 2))
                dve.wait_ge(*at("kk_summed", 7))
                dve.wait_ge(*at("k_ready", j))
                nc.vector.scalar_tensor_tensor(out=SQ[:, j % 2, :], in0=tile(j),
                                               scalar=pc("r_k", j), in1=tile(8 + j),
                                               op0=ALU.mult, op1=ALU.mult).then_inc(
                    *mark("bonus_raw", j))
                if j:
                    bonus(j - 1)
            bonus(7)
            for j in range(8):
                dve.wait_ge(*at("b_ready", j))
                dve.wait_ge(*at("decays_ready", (j, 0)))
                nc.vector.scalar_tensor_tensor(out=tile(48 + j), in0=tile(48 + j), scalar=-1.0,
                                               in1=tile(24 + j), op0=ALU.mult, op1=ALU.mult).then_inc(
                    *mark("a_tilde", j))
                dve.wait_ge(*at("decays_ready", (j, 1)))
                nc.vector.tensor_tensor(tile(32 + j), tile(32 + j), TMP[:, j % 2, :], ALU.mult)
                nc.vector.tensor_tensor(tile(8 + j), tile(8 + j), TMP[:, j % 2, :], ALU.mult)
                dve.wait_ge(*at("chunk_decay_ready", j))
                nc.vector.tensor_tensor(tile(j), tile(j), tile(40 + j), ALU.mult).then_inc(
                    *mark("tilde_ready", j))
            dve.wait_ge(*at("turned", ("v", TT - 1, 1)))
            nc.vector.memset(ST[:, 0, :, :], 0.0).then_inc(*mark("state_ready", 0))
            for tl in range(TT):
                for q0 in range(0, 8, 2):
                    for f in PAIR_DVE:
                        for q in (q0, q0 + 1):
                            f(dve, tl, q)
                for c in range(4):
                    chunk_dve(dve, tl, c)
                if tl == TT - 1:
                    memory_norm(dve, "a1_")
                y_dve(dve, tl)
            gn_dve(dve)
            norm_add(dve, "l1o", arena(40), gain(1, 1))

        def gn_pe(pe):
            for j in range(8):
                pe.wait_ge(*at("wkv_added", (TT - 1, 1)))
                if j >= 2:
                    pe.wait_ge(*at("y_centred", j - 2))
                pe.matmul((B6, B7)[j % 2][:, :], cc("blk"), tile(Y0 + j), start=True,
                          stop=True).then_inc(*mark("y_summed", j))
            keys_pe(pe, "a1_")
            for j in range(8):
                pe.wait_ge(*at("y_square", j))
                pe.wait_ge(*at("y_centred", 7))
                if j >= 2:
                    pe.wait_ge(*at("y_root", j - 2))
                pe.matmul((B6, B7)[j % 2][:, :], cc("blk"), SQ[:, j % 2, :], start=True,
                          stop=True).then_inc(*mark("y_square_summed", j))
            values_pe(pe, "a1_")
            product(pe, "g2", lambda k: LB[:, 1, :], lambda k: [])

        def gn_act(act):
            def square(j):
                act.wait_ge(*at("y_centred", j))
                if j >= 2:
                    act.wait_ge(*at("y_square_summed", j - 2))
                else:
                    act.wait_ge(*at("wkv_added", (TT - 1, 1)))
                nc.scalar.activation(SQ[:, j % 2, :], tile(Y0 + j), ACT.Square).then_inc(
                    *mark("y_square", j))
            square(0)
            square(1)
            for j in range(8):
                take_key(act, "a1_", j)
            for j in range(8):
                if 1 <= j < 7:
                    square(j + 1)
                act.wait_ge(*at("y_square_summed", j))
                if j >= 2:
                    act.wait_ge(*at("y_normed", j - 2))
                nc.scalar.activation(TMP[:, j % 2, :], (B6, B7)[j % 2][:, :], ACT.Sqrt,
                                     scale=1.0 / HD, bias=eps_col(GN_EPS)).then_inc(
                    *mark("y_root", j))

        def gn_dve(dve):
            for j in range(8):
                dve.wait_ge(*at("y_summed", j))
                dve.wait_ge(*at("wkv_added", (TT - 1, 1)))
                nc.vector.scalar_tensor_tensor(out=tile(Y0 + j), in0=(B6, B7)[j % 2][:, :],
                                               scalar=-1.0 / HD, in1=tile(Y0 + j),
                                               op0=ALU.mult, op1=ALU.add).then_inc(
                    *mark("y_centred", j))
            for j in range(8):
                dve.wait_ge(*at("y_root", j))
                s, y = TMP[:, j % 2, :], tile(Y0 + j)
                link(dve, nc.vector.reciprocal(s, s))
                nc.vector.scalar_tensor_tensor(out=y, in0=y, scalar=pc("gn_g", j), in1=s,
                                               op0=ALU.mult, op1=ALU.mult).then_inc(
                    *mark("y_normed", j))
                dve.wait_ge(*at("y_normed", j))
                link(dve, nc.vector.scalar_tensor_tensor(out=y, in0=y, scalar=pc("gn_b", j),
                                                         in1=hn(j), op0=ALU.add, op1=ALU.add))
            for j in range(8):
                ps = await_product(dve, "g2", j)
                nc.vector.tensor_tensor(tile(Y0 + j), ps[:, :], tile(Y0 + j), ALU.mult).then_inc(
                    *mark("products_read_by_dve", ("g2", j)))
                if j:
                    low_part(dve, ("y", j - 1), high(7 + j), tile(Y0 + j - 1), high(j - 1))
            low_part(dve, ("y", 7), high(15), tile(Y0 + 7), high(7))

        if "A" in phases:
            for n in ("l0n", "a0m", "l0o", "a0n", "a0x", "m0n", "m0x"):
                order.append((n, DT - 1))

        if "B" in phases:
            for n in ("l1n", "a1_m", "l1o", "a1_n", "a1_x", "m1n", "m1x"):
                order.append((n, DT - 1))
        if "C" in phases:
            order.insert(-1 if "B" in phases else 0, ("cm", DT - 1))
            order.append(("cn", DT - 1))
        if "D" in phases:
            order.append(("h2", DT - 1))

        block = ctx.enter_context(nc.Block())

        @block.sync
        def _(sp):
            for i in range(4):
                sp.dma_start(X[:, 2 * i:2 * i + 2, :], a.xT[:, 2 * i:2 * i + 2, :]).then_inc(
                    *mark(f"loaded_x{i}", 0, 16))
            load_weights(sp)
            if "D" in phases:
                experts_sp(sp)
                store_sp(sp)

        @block.gpsimd
        def _(pool):
            pool.dma_start(par[:, :], a.par).then_inc(*mark("loaded_par", 0, 16))
            pool.dma_start(con["all"][:, :], a.conall).then_inc(*mark("loaded_conall", 0, 16))
            if "A" in phases:
                split_weights(pool, ("w_in",))
                pool.wait_ge(*at("products_done", ("w_in", 15)))
                pool.dma_start(H[:, :, 4:4 + M], a.memT).then_inc(*mark("loaded_a0", 0, 16))
                split_weights(pool, ("w_out",))
                split_weights(pool, ("a0q", "a0o", "m0up0", "m0down0", "m0up1", "m0down1"))

            if "B" in phases:
                pool.dma_start(shared[:, 0:CWIDTH["B"]], a.conB).then_inc(
                    *mark("loaded_conB", 0, 16))
                split_weights(pool, ("r", "k_", "v_"))
                pool.wait_ge(*at("pair_done", (TT - 1, 7)))
                pool.dma_start(half[:, 64:72, :], a.memT).then_inc(*mark("loaded_a1_", 0, 16))
                split_weights(pool, ("w_o", "a1_q", "a1_o", "m1up0"))
                if "C" in phases:
                    pool.wait_ge(*at("residual_ready", ("a1_x", 7)))
                    pool.dma_start(half[:, 88:96, :], a.mem2T).then_inc(*mark("loaded_c", 0, 16))
                split_weights(pool, ("m1down0", "m1up1", "m1down1"))

            if "C" in phases:
                if "B" in phases:
                    pool.wait_ge(*at("products_done", ("m1down1", 7)))
                pool.dma_start(shared[:, 0:CWIDTH["C"]], a.conC).then_inc(
                    *mark("loaded_conC", 0, 16))
                if "B" not in phases:
                    pool.dma_start(half[:, 88:96, :], a.mem2T).then_inc(*mark("loaded_c", 0, 16))
                pos = a.positions_2.broadcast_to([P, T])
                pool.dma_start(tile(20).bitcast(I32), pos).then_inc(
                    *mark("loaded_positions", 0, 16))
                split_weights(pool, ("cx", "cc", "cb", "gate0", "gate1", "gate2", "wout2"))

            if "D" in phases:
                if "C" in phases:
                    pool.wait_ge(*at("products_read_by_dve", ("wout2", 7)))
                pool.dma_start(shared[:, 0:CWIDTH["D"]], a.conD).then_inc(
                    *mark("loaded_conD", 0, 16))
                for n, (w, c, k) in enumerate(((a.w_router_group_2, 0, 4),
                                               (a.w_router_expert_2, 4, 32))):
                    pool.dma_start(RT[:, :, c:c + k], w[0].rearrange("(k p) n -> p k n", p=P)).then_inc(
                        *mark(f"loaded_router{n}", 0, 16))
                pool.dma_start(BR[:, 0:4], a.b_router_group_2.broadcast_to([P, 4])).then_inc(
                    *mark("loaded_router_bias", 0, 16))
                pool.dma_start(BR[:, 4:36], a.b_router_expert_2.broadcast_to([P, 32])).then_inc(
                    *mark("loaded_router_bias2", 0, 16))
                scatter_pool(pool)
                gather_pool(pool)

        @block.scalar
        def _(act):
            if "D" in phases and "A" not in phases:
                for piece in range(PIECES):
                    clear_scratch(act, piece)
            act.wait_ge(*at("constants_set", 0))
            act.wait_ge(*at("loaded_par", 0))
            if "A" in phases:
                lru_act(act)
                attend_act(act, 0, "a0", "l0o", 1.0 / 16, 4, 2, None, None, None)
                mlp_act(act, "m0", "a0x")
            if "B" in phases:
                rwkv_act(act, "m0x" if "A" in phases else None)
                attend_act(act, 1, "a1_", "l1o", 1.0 / 16, 4, 2, None, None, None)
                mlp_act(act, "m1", "a1_x")
            if "C" in phases:
                second_act(act, "m1x" if "B" in phases else None)
            if "D" in phases:
                route_act(act, (lambda t: [("products_read_by_dve", ("wout2", t))])
                          if "C" in phases else x_ready(None))
                experts_act(act)
            if phases[-1] == "C":
                act.wait_ge(*at("products_read_by_dve", ("wout2", 7)))
                act.dma_start(out, X[:, :, :]).then_inc(*mark("output_stored", 0, 16))
                act.wait_ge(*at("output_stored", 0))
            elif phases[-1] != "D":
                act.wait_ge(*at("residual_ready", ({"A": "m0x", "B": "m1x"}[phases[-1]], 7)))
                act.dma_start(out, X[:, :, :]).then_inc(*mark("output_stored", 0, 16))
                act.wait_ge(*at("output_stored", 0))

        @block.tensor
        def _(pe):
            pe.wait_ge(*at("loaded_conall", 0))
            if "A" in phases:
                lru_pe(pe)
                attend_pe(pe, "a0", 4, 2)
                mlp_pe(pe, "m0")
            if "B" in phases:
                rwkv_pe(pe)
                attend_pe(pe, "a1_", 4, 2)
                mlp_pe(pe, "m1")
            if "C" in phases:
                second_pe(pe)
            if "D" in phases:
                route_pe(pe)
                experts_pe(pe)

        @block.vector
        def _(dve):
            if "D" in phases:
                nc.vector.memset(LB[:, :, :], 0.0).then_inc(*mark("zeros_set", 0))
            for v, j in EPSC.items():
                ins = nc.vector.memset(eps_sb[:, j:j + 1], v)
            ins.then_inc(*mark("constants_set", 0))
            dve.wait_ge(*at("loaded_par", 0))
            dve.wait_ge(*at("loaded_conall", 0))
            for i in range(4):
                dve.wait_ge(*at(f"loaded_x{i}", 0))
            if "A" in phases:
                lru_dve(dve)
                attend_dve(dve, 0, "a0")
                mlp_dve(dve, 0, "m0")
            if "B" in phases:
                rwkv_dve(dve)
                attend_dve(dve, 1, "a1_")
                mlp_dve(dve, 1, "m1")
            if "C" in phases:
                second_dve(dve)
            if "D" in phases:
                route_dve(dve)
                experts_dve(dve)
                combine_dve(dve)

    return marked


def host_layout(inp):
    f = {n: np.asarray(v) for n, v in inp.items()}

    def cols(v):
        return np.ascontiguousarray(v).reshape(-1, P).T

    par = np.concatenate([
        cols(f["ln_gains"]), cols(f["mem_norm"]), cols(f["a_conv_w"]), cols(f["a_conv_b"]),
        cols(f["a_b_in"]), cols(f["a_gate_b"]), cols(f["a_lambda"]), cols(f["a_b_out"]),
        cols(f["b_mu"]), cols(f["b_w0"]), cols(f["b_a0"]), cols(f["b_k_k"]), cols(f["b_k_a"]),
        cols(f["b_r_k"]), cols(f["b_gn_g"]), cols(f["b_gn_b"]), cols(f["g_mix_2"]),
        cols(f["g_mem_2"]), cols(f["g_ffn_2"]), cols(np.tile(f["g_qn_attn_2"][0], 2)),
        cols(np.tile(f["g_kn_attn_2"][0], 2)), cols(f["g_qn_mem_2"]), cols(f["g_kn_mem_2"]),
        cols(f["w_conv_2"]),
    ], 1)

    def channels_first(v):
        return np.ascontiguousarray(v.reshape(-1, DT, P).transpose(2, 1, 0))

    arrays = {"par": par, **{"con" + r: v for r, v in constants().items()}, "xT": channels_first(f["x"][0]),
              "memT": channels_first(f["mem"][0]), "mem2T": channels_first(f["mem_2"][0])}
    for n in WEIGHTS:
        arrays[n] = f[n]
    return arrays


WEIGHTS = ["a_w_in", "a_gate_w", "a_w_out", "b_w_rkv", "b_w1", "b_w2", "b_a1", "b_a2", "b_g1",
           "b_g2", "b_w_o", "c_w_q", "c_w_kv", "c_w_o", "m_w_up", "m_w_down", "positions_2",
           "w_in_2", "w_mem_kv_2", "w_proj_attn_2", "w_proj_conv_2", "w_proj_mem_2", "w_out_2",
           "w_router_group_2", "b_router_group_2", "w_router_expert_2", "b_router_expert_2",
           "w_gate_2", "w_up_2", "w_down_2"]
PHASES = "ABCD"


def kernel(**inputs):
    from types import SimpleNamespace

    import concourse.bacc as bacc
    from concourse.bass_utils import run_bass_kernel_spmd

    arrays = {n: np.ascontiguousarray(v) for n, v in host_layout(inputs).items()}

    def build(known):
        nc = bacc.Bacc("TRN2", target_bir_lowering=False, num_devices=1)
        a = SimpleNamespace(**{n: nc.dram_tensor(f"in_{n}", v.shape, mybir.dt.from_np(v.dtype),
                                                 kind="ExternalInput").ap()
                               for n, v in arrays.items()})
        shape = (T, D) if PHASES[-1] == "D" else (P, DT, T)
        out = nc.dram_tensor("out_dram", shape, F32, kind="ExternalOutput").ap()
        return nc, program(nc, a, out, PHASES, known)

    _, counts = build(None)
    nc, _ = build(counts)
    r = run_bass_kernel_spmd(nc, [{f"in_{n}": v for n, v in arrays.items()}], core_ids=[0])
    got = r.results[0]["out_dram"]
    if PHASES[-1] == "D":
        return got.reshape(1, T, D)
    return got.transpose(2, 1, 0).reshape(1, T, D)
```
